# Optimizing a Trainium2 kernel written in Bass

```python
import jax
import jax.numpy as jnp
from jax import lax
import numpy as np

D_MODEL = 1024
BATCH = 1
SEQ = 512
DEPTH = 1
DEC_BATCH = 8
DEC_SEQ = 1
PAST_LEN = 2048
PAGE_SIZE = 128

N_BRANCH = 4
BRANCH_DIM = D_MODEL // 2
SC_DIM = BRANCH_DIM
SC_WIDTH = 3
GDN_HEADS = 4
GDN_DK = BRANCH_DIM // GDN_HEADS
GDN_DV = BRANCH_DIM // GDN_HEADS
GDN_QKV = GDN_HEADS * (2 * GDN_DK + GDN_DV)
GDN_CONV_WIDTH = 4
GDN_CHUNK = 64
CONF_DIM = BRANCH_DIM
CONF_WIDTH = 31
FOX_HEADS = 8
FOX_DH = BRANCH_DIM // FOX_HEADS
Q_BLOCK = 128
MEM_LEN = 256
X_HEADS = 4
X_DH = 128
D_FF = 2816
FFN_CONV_WIDTH = 3
IN_WIDTHS = (SC_DIM, SC_DIM, SC_DIM,
             GDN_HEADS * GDN_DK, GDN_HEADS * GDN_DK, GDN_HEADS * GDN_DV, GDN_HEADS * GDN_DV, GDN_HEADS, GDN_HEADS,
             CONF_DIM, CONF_DIM,
             FOX_HEADS * FOX_DH, FOX_HEADS * FOX_DH, FOX_HEADS * FOX_DH, FOX_HEADS,
             N_BRANCH * D_MODEL)
N_IN = sum(IN_WIDTHS)
NEG_INF = -1e30
F32 = jnp.float32

kernel_name = 'hybrid_gated_branch_decoder_step'

def rmsnorm(x, g, eps=1e-6):
    xf = x.astype(F32)
    y = xf * lax.rsqrt(jnp.mean(xf * xf, axis=-1, keepdims=True) + eps)
    return y.astype(x.dtype) * g

def layernorm(x, g, b, eps=1e-5):
    xf = x.astype(F32)
    mu = jnp.mean(xf, axis=-1, keepdims=True)
    var = jnp.mean(jnp.square(xf - mu), axis=-1, keepdims=True)
    return ((xf - mu) * lax.rsqrt(var + eps)).astype(x.dtype) * g + b

def l2norm(x, eps=1e-6):
    xf = x.astype(F32)
    return xf * lax.rsqrt(jnp.sum(xf * xf, axis=-1, keepdims=True) + eps)

def split_cols(z, widths):
    parts, start = [], 0
    for w in widths:
        parts.append(z[..., start:start + w])
        start += w
    return parts

def causal_dwconv(x, hist, w):
    width = w.shape[0]
    xc = jnp.concatenate([hist.astype(x.dtype), x], axis=1)
    y = lax.conv_general_dilated(xc, w[:, None, :].astype(x.dtype), window_strides=(1,), padding='VALID',
                                 dimension_numbers=('NWC', 'WIO', 'NWC'), feature_group_count=x.shape[-1])
    return y, xc[:, xc.shape[1] - (width - 1):]

def gated_delta_chunked(q, k, v, g, beta, s0):
    B_, T, H, DK = q.shape
    DV = v.shape[-1]
    C = min(GDN_CHUNK, T)
    n = -(-T // C)
    pad = n * C - T

    def chunks(a):
        a = jnp.pad(a, [(0, 0), (0, pad)] + [(0, 0)] * (a.ndim - 2))
        return jnp.moveaxis(a.reshape((B_, n, C) + a.shape[2:]), 3, 1)

    q = chunks(q) * (DK ** -0.5)
    k, v, g, beta = chunks(k), chunks(v), chunks(g), chunks(beta)
    d = jnp.cumsum(g, axis=-1)
    tril = jnp.tril(jnp.ones((C, C), dtype=bool))
    strict = jnp.tril(jnp.ones((C, C), dtype=bool), -1)
    diff = d[..., :, None] - d[..., None, :]
    L = jnp.where(tril, jnp.exp(jnp.where(tril, diff, 0.0)), 0.0)
    kb = k * beta[..., None]
    A = jnp.where(strict, jnp.einsum('bhnik,bhnjk->bhnij', kb, k) * L, 0.0) + jnp.eye(C, dtype=F32)
    rhs = jnp.concatenate([v * beta[..., None], kb * jnp.exp(d)[..., None]], axis=-1)
    sol = lax.linalg.triangular_solve(A, rhs, left_side=True, lower=True, unit_diagonal=True)
    u, w = sol[..., :DV], sol[..., DV:]
    qk = jnp.where(tril, jnp.einsum('bhnik,bhnjk->bhnij', q, k) * L, 0.0)
    q_dec = q * jnp.exp(d)[..., None]
    k_dec = k * jnp.exp(d[..., -1:] - d)[..., None]
    d_last = jnp.exp(d[..., -1])

    def step(S, xs):
        u_i, w_i, qk_i, qd_i, kd_i, dl_i = xs
        v_new = u_i - jnp.einsum('bhck,bhkv->bhcv', w_i, S)
        o = jnp.einsum('bhck,bhkv->bhcv', qd_i, S) + jnp.einsum('bhcs,bhsv->bhcv', qk_i, v_new)
        S = S * dl_i[..., None, None] + jnp.einsum('bhck,bhcv->bhkv', kd_i, v_new)
        return S, o

    xs = tuple(jnp.moveaxis(a, 2, 0) for a in (u, w, qk, q_dec, k_dec, d_last))
    S, o = lax.scan(step, s0, xs)
    o = o.transpose(1, 0, 3, 2, 4).reshape(B_, n * C, H, DV)[:, :T]
    return o, S

def forgetting_attention(q, k, v, c_q, c_k, q_pos, k_pos):
    B_, Tq, H, d = q.shape
    blk = Q_BLOCK if Tq % Q_BLOCK == 0 else Tq
    nb = Tq // blk
    ck = jnp.swapaxes(c_k, 1, 2)[:, :, None, :]
    qb = jnp.swapaxes(q.reshape(B_, nb, blk, H, d), 0, 1)
    cqb = jnp.swapaxes(c_q.reshape(B_, nb, blk, H), 0, 1)
    pb = q_pos.reshape(nb, blk)

    def block(args):
        qi, ci, pi = args
        s = jnp.einsum('bqhd,bkhd->bhqk', qi, k, preferred_element_type=F32) * (d ** -0.5)
        s = s + jnp.swapaxes(ci, 1, 2)[..., None] - ck
        s = jnp.where(k_pos[None, None, None, :] <= pi[None, None, :, None], s, NEG_INF)
        p = jax.nn.softmax(s, axis=-1)
        return jnp.einsum('bhqk,bkhd->bqhd', p.astype(v.dtype), v)

    o = lax.map(block, (qb, cqb, pb))
    return jnp.swapaxes(o, 0, 1).reshape(B_, Tq, H, d)

def token_mixer(xn, p, hist, past):
    B_, T, _ = xn.shape
    z = xn @ p['w_in']
    (a_h, a_b, a_c, g_q, g_k, g_v, g_z, g_a, g_b, c_v, c_g, f_q, f_k, f_v, f_f, gate) = split_cols(z, IN_WIDTHS)

    ya, sc_hist = causal_dwconv(a_c * a_h, hist['sconv'], p['sconv_w'])
    o_a = a_b * ya

    qkv, gdn_conv_hist = causal_dwconv(jnp.concatenate([g_q, g_k, g_v], axis=-1), hist['gdn_conv'], p['gdn_conv_w'])
    q, k, v = split_cols(jax.nn.silu(qkv), (GDN_HEADS * GDN_DK, GDN_HEADS * GDN_DK, GDN_HEADS * GDN_DV))
    q = l2norm(q.reshape(B_, T, GDN_HEADS, GDN_DK))
    k = l2norm(k.reshape(B_, T, GDN_HEADS, GDN_DK))
    v = v.reshape(B_, T, GDN_HEADS, GDN_DV).astype(F32)
    beta = jax.nn.sigmoid(g_b.astype(F32))
    g_log = -jnp.exp(p['gdn_a_log'].astype(F32)) * jax.nn.softplus(g_a.astype(F32) + p['gdn_dt_bias'].astype(F32))
    o, S = gated_delta_chunked(q, k, v, g_log, beta, hist['gdn'].astype(F32))
    o = rmsnorm(o, p['gdn_norm']) * jax.nn.silu(g_z.reshape(B_, T, GDN_HEADS, GDN_DV).astype(F32))
    o_b = o.astype(xn.dtype).reshape(B_, T, GDN_HEADS * GDN_DV)

    glu = c_v * jax.nn.sigmoid(c_g)
    yc, conf_hist = causal_dwconv(glu, hist['conf'], p['conf_dw_w'])
    o_c = jax.nn.silu(layernorm(yc + p['conf_dw_b'], p['conf_ln_g'], p['conf_ln_b']))

    fq = f_q.reshape(B_, T, FOX_HEADS, FOX_DH)
    fk = f_k.reshape(B_, T, FOX_HEADS, FOX_DH)
    fv = f_v.reshape(B_, T, FOX_HEADS, FOX_DH)
    flog = jax.nn.log_sigmoid((f_f + p['fox_fbias']).astype(F32))
    if past is None:
        kk, vv, ll = fk, fv, flog
        q_pos = jnp.arange(T, dtype=jnp.int32)
        k_pos = q_pos
    else:
        kp, vp, lp = past
        P = kp.shape[1]
        kk = jnp.concatenate([kp.astype(fk.dtype), fk], axis=1)
        vv = jnp.concatenate([vp.astype(fv.dtype), fv], axis=1)
        ll = jnp.concatenate([lp.astype(F32), flog], axis=1)
        q_pos = P + jnp.arange(T, dtype=jnp.int32)
        k_pos = jnp.arange(P + T, dtype=jnp.int32)
    c = jnp.cumsum(ll, axis=1)
    o_d = forgetting_attention(fq, kk, vv, c[:, -T:], c, q_pos, k_pos).reshape(B_, T, FOX_HEADS * FOX_DH)

    gates = jax.nn.sigmoid(gate).reshape(B_, T, N_BRANCH, D_MODEL)
    merged = 0.0
    for i, o_i in enumerate((o_a, o_b, o_c, o_d)):
        merged = merged + gates[:, :, i] * (o_i @ p['w_branch'][i])
    out = merged @ p['w_out']
    state = dict(sconv=sc_hist, gdn_conv=gdn_conv_hist, gdn=S, conf=conf_hist, fox_k=fk, fox_v=fv, fox_logf=flog)
    return out, state

def cross_attention(xn, mk, mv, w_cq, w_co):
    B_, T, _ = xn.shape
    q = (xn @ w_cq).reshape(B_, T, X_HEADS, X_DH)
    s = jnp.einsum('bqhd,bkhd->bhqk', q, mk, preferred_element_type=F32) * (X_DH ** -0.5)
    pr = jax.nn.softmax(s, axis=-1).astype(mv.dtype)
    o = jnp.einsum('bhqk,bkhd->bqhd', pr, mv)
    return o.reshape(B_, T, X_HEADS * X_DH) @ w_co

def conv_ffn(xn, p, hist):
    gu = xn @ p['w_ffn_in']
    g, u = gu[..., :D_FF], gu[..., D_FF:]
    gc, new_hist = causal_dwconv(g, hist, p['ffn_conv_w'])
    return (jax.nn.silu(gc) * u) @ p['w_ffn_out'], new_hist

def trunk(x, params, hists, mems, pasts, norm_final):
    states = []
    for l in range(DEPTH):
        p = params[l]
        mix, st = token_mixer(rmsnorm(x, p['norm_mix']), p, hists[l], pasts[l])
        x = x + mix
        x = x + cross_attention(rmsnorm(x, p['norm_cross']), mems[l][0], mems[l][1], p['w_cq'], p['w_co'])
        ff, st['ffn'] = conv_ffn(rmsnorm(x, p['norm_ffn']), p, hists[l]['ffn'])
        x = x + ff
        states.append(st)
    return rmsnorm(x, norm_final), states

def stack_state(states, name, axis):
    return jnp.stack([s[name] for s in states], axis=axis)

def setup_inputs(seed: int = 0) -> dict:
    key = jax.random.key(seed)
    ks = iter(jax.random.split(key, 64))

    def nrm(shape, scale=1.0):
        return jax.random.normal(next(ks), shape, F32) * scale

    def gain(shape):
        return 1.0 + nrm(shape, 0.02)

    n_pages = PAST_LEN // PAGE_SIZE
    n_used = DEC_BATCH * n_pages
    n_pool = n_used + n_used // 4
    inp = {}
    inp['x_prompt'] = nrm((BATCH, SEQ, D_MODEL))
    inp['x_sample'] = nrm((DEC_BATCH, DEC_SEQ, D_MODEL))
    inp['cache_fox_k'] = nrm((n_pool, PAGE_SIZE, DEPTH, FOX_HEADS, FOX_DH))
    inp['cache_fox_v'] = nrm((n_pool, PAGE_SIZE, DEPTH, FOX_HEADS, FOX_DH))
    inp['cache_fox_logf'] = jax.nn.log_sigmoid(nrm((n_pool, PAGE_SIZE, DEPTH, FOX_HEADS)) + 3.5)
    inp['cache_mem_k'] = nrm((DEC_BATCH, DEPTH, MEM_LEN, X_HEADS, X_DH))
    inp['cache_mem_v'] = nrm((DEC_BATCH, DEPTH, MEM_LEN, X_HEADS, X_DH))
    inp['state_sconv'] = nrm((DEC_BATCH, DEPTH, SC_WIDTH - 1, SC_DIM))
    inp['state_gdn_conv'] = nrm((DEC_BATCH, DEPTH, GDN_CONV_WIDTH - 1, GDN_QKV))
    inp['state_gdn'] = nrm((DEC_BATCH, DEPTH, GDN_HEADS, GDN_DK, GDN_DV), 0.1)
    inp['state_conf_conv'] = nrm((DEC_BATCH, DEPTH, CONF_WIDTH - 1, CONF_DIM))
    inp['state_ffn_conv'] = nrm((DEC_BATCH, DEPTH, FFN_CONV_WIDTH - 1, D_FF))
    inp['page_table'] = jax.random.permutation(next(ks), n_pool)[:n_used].reshape(DEC_BATCH, n_pages).astype(jnp.int32)
    inp['mem_prompt'] = nrm((BATCH, MEM_LEN, D_MODEL))
    inp['norm_mix'] = gain((DEPTH, D_MODEL))
    inp['w_in'] = nrm((DEPTH, D_MODEL, N_IN), D_MODEL ** -0.5)
    inp['w_branch'] = nrm((DEPTH, N_BRANCH, BRANCH_DIM, D_MODEL), BRANCH_DIM ** -0.5)
    inp['w_out'] = nrm((DEPTH, D_MODEL, D_MODEL), D_MODEL ** -0.5)
    inp['sconv_w'] = nrm((DEPTH, SC_WIDTH, SC_DIM), SC_WIDTH ** -0.5)
    inp['gdn_conv_w'] = nrm((DEPTH, GDN_CONV_WIDTH, GDN_QKV), GDN_CONV_WIDTH ** -0.5)
    inp['gdn_a_log'] = jnp.log(jax.random.uniform(next(ks), (DEPTH, GDN_HEADS), F32, minval=1.0, maxval=16.0))
    dt = jnp.exp(jax.random.uniform(next(ks), (DEPTH, GDN_HEADS), F32, minval=-6.9, maxval=-2.3))
    inp['gdn_dt_bias'] = dt + jnp.log(-jnp.expm1(-dt))
    inp['gdn_norm'] = gain((DEPTH, GDN_DV))
    inp['conf_dw_w'] = nrm((DEPTH, CONF_WIDTH, CONF_DIM), CONF_WIDTH ** -0.5)
    inp['conf_dw_b'] = nrm((DEPTH, CONF_DIM), 0.02)
    inp['conf_ln_g'] = gain((DEPTH, CONF_DIM))
    inp['conf_ln_b'] = nrm((DEPTH, CONF_DIM), 0.02)
    inp['fox_fbias'] = jax.random.uniform(next(ks), (DEPTH, FOX_HEADS), F32, minval=1.0, maxval=6.0)
    inp['norm_cross'] = gain((DEPTH, D_MODEL))
    inp['norm_mem'] = gain((DEPTH, D_MODEL))
    inp['w_cq'] = nrm((DEPTH, D_MODEL, X_HEADS * X_DH), D_MODEL ** -0.5)
    inp['w_ckv'] = nrm((DEPTH, D_MODEL, 2 * X_HEADS * X_DH), D_MODEL ** -0.5)
    inp['w_co'] = nrm((DEPTH, X_HEADS * X_DH, D_MODEL), (X_HEADS * X_DH) ** -0.5)
    inp['norm_ffn'] = gain((DEPTH, D_MODEL))
    inp['w_ffn_in'] = nrm((DEPTH, D_MODEL, 2 * D_FF), D_MODEL ** -0.5)
    inp['ffn_conv_w'] = nrm((DEPTH, FFN_CONV_WIDTH, D_FF), FFN_CONV_WIDTH ** -0.5)
    inp['w_ffn_out'] = nrm((DEPTH, D_FF, D_MODEL), D_FF ** -0.5)
    inp['norm_final'] = gain((D_MODEL,))
    return inp

def reference(x_prompt, x_sample, cache_fox_k, cache_fox_v, cache_fox_logf, cache_mem_k, cache_mem_v,
              state_sconv, state_gdn_conv, state_gdn, state_conf_conv, state_ffn_conv, page_table, mem_prompt,
              norm_mix, w_in, w_branch, w_out, sconv_w, gdn_conv_w, gdn_a_log, gdn_dt_bias, gdn_norm,
              conf_dw_w, conf_dw_b, conf_ln_g, conf_ln_b, fox_fbias, norm_cross, norm_mem, w_cq, w_ckv, w_co,
              norm_ffn, w_ffn_in, ffn_conv_w, w_ffn_out, norm_final):
    params = [dict(norm_mix=norm_mix[l], w_in=w_in[l], w_branch=w_branch[l], w_out=w_out[l], sconv_w=sconv_w[l],
                   gdn_conv_w=gdn_conv_w[l], gdn_a_log=gdn_a_log[l], gdn_dt_bias=gdn_dt_bias[l], gdn_norm=gdn_norm[l],
                   conf_dw_w=conf_dw_w[l], conf_dw_b=conf_dw_b[l], conf_ln_g=conf_ln_g[l], conf_ln_b=conf_ln_b[l],
                   fox_fbias=fox_fbias[l], norm_cross=norm_cross[l], w_cq=w_cq[l], w_co=w_co[l],
                   norm_ffn=norm_ffn[l], w_ffn_in=w_ffn_in[l], ffn_conv_w=ffn_conv_w[l], w_ffn_out=w_ffn_out[l])
              for l in range(DEPTH)]

    b_p = x_prompt.shape[0]
    dt = x_prompt.dtype
    xw = X_HEADS * X_DH
    mems_p = []
    for l in range(DEPTH):
        kv = rmsnorm(mem_prompt, norm_mem[l]) @ w_ckv[l]
        mems_p.append((kv[..., :xw].reshape(b_p, MEM_LEN, X_HEADS, X_DH),
                       kv[..., xw:].reshape(b_p, MEM_LEN, X_HEADS, X_DH)))
    zero_hist = dict(sconv=jnp.zeros((b_p, SC_WIDTH - 1, SC_DIM), dt),
                     gdn_conv=jnp.zeros((b_p, GDN_CONV_WIDTH - 1, GDN_QKV), dt),
                     gdn=jnp.zeros((b_p, GDN_HEADS, GDN_DK, GDN_DV), F32),
                     conf=jnp.zeros((b_p, CONF_WIDTH - 1, CONF_DIM), dt),
                     ffn=jnp.zeros((b_p, FFN_CONV_WIDTH - 1, D_FF), dt))
    y_prompt, st_p = trunk(x_prompt, params, [zero_hist] * DEPTH, mems_p, [None] * DEPTH, norm_final)

    b_s = x_sample.shape[0]
    hists_s = [dict(sconv=state_sconv[:, l], gdn_conv=state_gdn_conv[:, l], gdn=state_gdn[:, l],
                    conf=state_conf_conv[:, l], ffn=state_ffn_conv[:, l]) for l in range(DEPTH)]
    mems_s = [(cache_mem_k[:, l], cache_mem_v[:, l]) for l in range(DEPTH)]
    pasts_s = [(cache_fox_k[page_table, :, l].reshape(b_s, -1, FOX_HEADS, FOX_DH),
                cache_fox_v[page_table, :, l].reshape(b_s, -1, FOX_HEADS, FOX_DH),
                cache_fox_logf[page_table, :, l].reshape(b_s, -1, FOX_HEADS)) for l in range(DEPTH)]
    y_sample, st_s = trunk(x_sample, params, hists_s, mems_s, pasts_s, norm_final)

    return (y_prompt, y_sample,
            stack_state(st_p, 'fox_k', 2), stack_state(st_p, 'fox_v', 2), stack_state(st_p, 'fox_logf', 2),
            jnp.stack([m[0] for m in mems_p], axis=1), jnp.stack([m[1] for m in mems_p], axis=1),
            stack_state(st_p, 'sconv', 1), stack_state(st_p, 'gdn_conv', 1), stack_state(st_p, 'gdn', 1),
            stack_state(st_p, 'conf', 1), stack_state(st_p, 'ffn', 1),
            stack_state(st_s, 'fox_k', 2), stack_state(st_s, 'fox_v', 2), stack_state(st_s, 'fox_logf', 2),
            stack_state(st_s, 'sconv', 1), stack_state(st_s, 'gdn_conv', 1), stack_state(st_s, 'gdn', 1),
            stack_state(st_s, 'conf', 1), stack_state(st_s, 'ffn', 1))


_drawn_inputs = setup_inputs


def setup_inputs(seed=0):
    import zlib

    import numpy as np

    out = dict(_drawn_inputs(seed))
    spreads = {}
    factors = {'cache_fox_logf': 12.688,
     'gdn_norm': 8.0,
     'conf_dw_b': 4.99,
     'conf_ln_g': 8.0,
     'conf_ln_b': 8.0,
     'norm_cross': 8.0,
     'norm_mem': 2.935,
     'norm_ffn': 2.893,
     'norm_final': 7.412}
    for name, (base, spread) in spreads.items():
        noise = np.random.default_rng([zlib.crc32(name.encode()), seed]).standard_normal(out[name].shape)
        drawn = base * np.exp(spread * noise) if base else spread * noise
        out[name] = jnp.asarray(drawn.astype(out[name].dtype))
    for name, factor in factors.items():
        out[name] = (out[name] * factor).astype(out[name].dtype)
    return out
```

```python
from contextlib import ExitStack

import numpy as np

import concourse.bass as bass
from concourse import mybir

F32 = mybir.dt.float32
F32R = mybir.dt.float32r
I32 = mybir.dt.int32
ALU = mybir.AluOpType
ACT = mybir.ActivationFunctionType
AX = mybir.AxisListType.X
MUL, ADD, SUB, MAX, MIN = ALU.mult, ALU.add, ALU.subtract, ALU.max, ALU.min

P = 128
D = 1024
KD = D // P
SEQ, NB = 512, 8
T = SEQ + NB
TH = T // 2
QT = SEQ // P
BD = 512
KB = BD // P
SCW, GCW, CFW, FCW = 3, 4, 31, 3
GH = 4
FH, FD = 8, 64
XH = 4
MEM = 256
FF = 2816
KF = FF // P
PAGES = 16
NEG = -1e30
LEVELS = 7

C_AH, C_AB, C_AC, C_GQ = 0, BD, 2 * BD, 3 * BD
C_GZ = 6 * BD
C_GA = 7 * BD
C_CV = C_GA + 2 * GH
C_CG = C_CV + BD
C_FQ = C_CG + BD
C_FF = C_FQ + 3 * BD
C_GATE = C_FF + FH
N_IN = C_GATE + 4 * D

(I_ID, I_ONE, I_UP, I_NEGLOW, I_CAUSAL, I_LO, I_HI, I_PAGE, I_LVL) = range(9)
N_CST = I_LVL + LEVELS

V_MIX, V_CROSS, V_FFN, V_FIN, V_MEM, V_CB, V_LG, V_LB, V_GN, V_SW, V_GW = 0, 8, 16, 24, 32, 40, 44, 48, 52, 53, 65
B_VEC, B_CW, B_FW, B_SS, B_GS, B_CS, B_FS = 0, 1, 2, 3, 4, 8, 16
N_BLK = 20


def constants():
    r, c = np.arange(P)[:, None], np.arange(P)[None, :]
    out = np.zeros((P, N_CST, P), np.float32)
    out[:, I_ID] = r == c
    out[:, I_ONE] = 1.0
    out[:, I_UP] = r <= c
    out[:, I_NEGLOW] = -(r > c).astype(np.float32)
    out[:, I_CAUSAL] = np.where(c > r, np.float32(NEG), np.float32(0))
    out[:, I_LO] = r < FD
    out[:, I_HI] = r >= FD
    out[:, I_PAGE] = (r // PAGES == c // PAGES) & (r < c)
    for n in range(LEVELS):
        s = 1 << n
        out[:, I_LVL + n] = (r // (2 * s) == c // (2 * s)) & ((r // s) % 2 == 1) & ((c // s) % 2 == 0)
    return out.reshape(P, N_CST * P)


def plan():
    units, pieces = [], []

    def unit(w, row, kt, col, kind, idx, first=True, last=True):
        units.append((w, row, kt, col))
        for h in range(2):
            pieces.append((len(units) - 1, h, kt, kind, idx + h, first, last))

    for n, kind in enumerate(("fq", "fk", "fv")):
        for h in range(2):
            unit("w_in", 0, KD, C_FQ + n * BD + h * 256, kind, 2 * h)
    for h in range(2):
        unit("w_in", 0, KD, C_CV + h * 256, "cv", 2 * h)
        unit("w_in", 0, KD, C_CG + h * 256, "cg", 2 * h)
    for h in range(2):
        unit("w_in", 0, KD, C_AC + h * 256, "ac", 2 * h)
        unit("w_in", 0, KD, C_AH + h * 256, "ah", 2 * h)
        unit("w_in", 0, KD, C_AB + h * 256, "ab", 2 * h)
    for n in range(6):
        unit("w_in", 0, KD, C_GQ + n * 256, "gx", 2 * n)
    for n, br in enumerate("ACBD"):
        if br == "B":
            for h in range(2):
                unit("w_in", 0, KD, C_GZ + h * 256, "gz", 2 * h)
        b = "ABCD".index(br)
        for h in range(4):
            unit("w_in", 0, KD, C_GATE + b * D + h * 256, "gate" + br, 2 * h)
            unit("w_branch", b * BD, KB, h * 256, "br" + br, 2 * h)
    for h in range(4):
        unit("w_out", 0, KD, h * 256, "wo", 2 * h)
    for h in range(4):
        unit("w_ckv", 0, KD, h * 256, "kv", 2 * h)
    for h in range(2):
        unit("w_cq", 0, KD, h * 256, "cq", 2 * h)
    for h in range(4):
        unit("w_co", 0, KB, h * 256, "co", 2 * h)
    for h in range(KF // 2):
        unit("w_ffn_in", 0, KD, h * 256, "fg", 2 * h)
        unit("w_ffn_in", 0, KD, FF + h * 256, "fu", 2 * h)
    for h in range(4):
        for k in range(0, KF, KD):
            unit("w_ffn_out", k * P, min(KD, KF - k), h * 256, "fo", 2 * h, k == 0, k + KD >= KF)
    return units, pieces


UNITS, PIECES = plan()
NP_ = len(PIECES)
PIECE_MT = []
MT_LAST = []
for _p, (_u, _h, _k, _kind, _idx, _first, _last) in enumerate(PIECES):
    if _first:
        PIECE_MT.append(len(MT_LAST))
        MT_LAST.append(_p)
    else:
        PIECE_MT.append(PIECE_MT[_p - 2])
        MT_LAST[PIECE_MT[_p]] = _p
BY_ACT = {"fq", "fk", "fv", "cv", "cg", "gx", "ac", "gateA", "gateB", "gateC", "gateD", "gz", "kv", "cq", "fg"}
MT_KIND = [PIECES[p][3] for p in MT_LAST]
MT_ACT = [k in BY_ACT for k in MT_KIND]


def first_piece(kind):
    return min(p for p, x in enumerate(PIECES) if x[3] == kind)


def last_piece(kind):
    return max(p for p, x in enumerate(PIECES) if x[3] == kind)


GROUPS = 32
FOX = 4 * FH
XU = 4 * XH
TAPS_TICK, K_TICK = 2, 3
V_FILLED, V_BARE = 1, 2
SIDE = ([("sm", n) for n in range(3)]
        + [("AFTER", "fv")]
        + [("fst", n) for n in range(4)] + [("KSTART",)]
        + [("fvt", n) for n in range(5)] + [("fkt", n) for n in range(5)]
        + [("fox", n) for n in range(FOX + 3)]
        + [("AFTER", "gx")]
        + [("l2", n) for n in range(9)]
        + [("gdn", n, 0) for n in range(-1, 18)]
        + [("TAPS",)]
        + [("cln", n) for n in range(6)] + [("BEFORE", "gateC")]
        + [("REDUCES",)]
        + [("dc", n) for n in range(3)] + [("ds", n) for n in range(4)] + [("VSTART",)]
        + [("gdn", n, c) for c in range(1, 4) for n in range(-1, 18)]
        + [("gs", n) for n in range(13)]
        + [("gp", n) for n in range(5)] + [("BEFORE", "gz")]
        + [("PAGES",), ("df", 0)] + [("BEFORE", "gateD")]
        + [("ex", n) for n in range(6)] + [("ml", n) for n in range(3)] + [("BEFORE", "wo")]
        + [("AFTER", "cq")]
        + [("xm", n) for n in range(3)] + [("x", n) for n in range(XU + 3)] + [("xd", n) for n in range(4)]
        + [("BEFORE", "co")]
        + [("AFTER", "fu")] + [("ef", n) for n in range(7)]
        + [("BEFORE", "END")] + [("y", n) for n in range(11)])


MARKS = ("AFTER", "BEFORE", "TAPS", "REDUCES", "KSTART", "VSTART", "PAGES")
N_TAP = KB * CFW
N_PAGE = PAGES * NB


def timeline():
    out, pos, step_n, bg = [], [0], [0], {"tap": None, "k": None, "v": None}
    size = {"tap": N_TAP, "k": N_PAGE, "v": N_PAGE}

    def background(kind, n):
        for _ in range(n):
            if bg[kind] is not None and bg[kind] < size[kind]:
                out.append((kind, bg[kind]))
                bg[kind] += 1

    def step(done, filled=True):
        while pos[0] < len(SIDE):
            s = SIDE[pos[0]]
            if s[0] == "AFTER":
                if done <= last_piece(s[1]) + 1:
                    return
            elif s[0] in ("TAPS", "REDUCES", "PAGES"):
                background({"TAPS": "tap", "REDUCES": "k", "PAGES": "v"}[s[0]], 10 ** 6)
                if s[0] == "REDUCES":
                    out.append(("kend",))
            elif s[0] == "KSTART":
                bg["k"] = 0
                out.append(("kstart",))
            elif s[0] == "VSTART":
                bg["v"] = 0
                out.append(("vstart",))
            elif s[0] != "BEFORE":
                background("v", V_FILLED if filled else V_BARE)
                out.append(("side", step_n[0], s))
                step_n[0] += 1
                pos[0] += 1
                return
            elif s[1] == "END":
                return
            pos[0] += 1

    def through(mark):
        at = SIDE.index(mark)
        if pos[0] <= at and any(s[0] == "AFTER" for s in SIDE[pos[0]:at]):
            out.append(("flush",))
        while pos[0] < at and any(s[0] not in ("AFTER", "BEFORE") for s in SIDE[pos[0]:at]):
            step(10 ** 6, False)

    out.append(("norm", "mix"))
    for p in range(NP_):
        kind = PIECES[p][3]
        if p == first_piece(kind) and ("BEFORE", kind) in SIDE:
            through(("BEFORE", kind))
        if kind in ("wo", "kv", "co", "fg", "fo") and p == first_piece(kind):
            out.append(("flush",))
        if p == first_piece("wo"):
            out.append(("split", "merged"))
        if p == first_piece("kv"):
            out.append(("norm", "mem"))
            out.append(("norm", "cross"))
        if p == first_piece("co"):
            out.append(("split", "brX"))
        if p == first_piece("fg"):
            out.append(("norm", "ffn"))
        if bg["tap"] is None and p > last_piece("cg") + 1:
            bg["tap"] = 0
        for h in range(2):
            out.append(("piece", p, h))
            if kind in ("gateC", "gateB", "gateD") and p == first_piece(kind) and h == 0:
                out.append(("split", "br" + kind[-1]))
            step(p)
            background("tap", TAPS_TICK)
            background("k", 1 + h if K_TICK == 3 else 1)
    out.append(("flush",))
    through(("BEFORE", "END"))
    pos[0] = SIDE.index(("BEFORE", "END")) + 1
    out.append(("norm", "fin"))
    for n in range(pos[0], len(SIDE)):
        step(10 ** 6)
    return out


TIMELINE = timeline()
ITEMS = [e[2] for e in TIMELINE if e[0] == "side"]
assert len(ITEMS) == len([s for s in SIDE if s[0] not in MARKS])
assert [e[1] for e in TIMELINE if e[0] == "k"] == list(range(N_PAGE))
assert [e[1] for e in TIMELINE if e[0] == "v"] == list(range(N_PAGE))
assert TIMELINE.index(("tap", N_TAP - 1)) < TIMELINE.index(("piece", first_piece("brA") + 6, 0))


def pe_works(s):
    kind, n = s[0], s[1]
    return n < {"sm": 2, "fst": 3, "fvt": 4, "fkt": 4, "fox": FOX + 2, "l2": 8, "gdn": 17, "cln": 5, "gp": 4, "dc": 2,
                "ds": 3, "df": 0, "ex": 5, "xm": 2, "x": XU + 2, "xd": 3, "ef": 6, "y": 10,
                "gs": 11, "ml": 2}[kind] and not (kind in ("gs", "ml") and n == 0)


def act_works(s):
    kind, n = s[0], s[1]
    if kind in ("sm", "fst", "fvt", "fkt", "ex", "ef", "y", "fox"):
        return n > 0
    if kind == "gdn":
        return n == 0 or n >= 3 and n % 2 == 1 or n == 16
    if kind == "ds":
        return n == 2
    if kind == "x":
        return n > 0 and n < XU + 2
    if kind == "xm":
        return n > 0
    if kind == "xd":
        return n == 2
    if kind == "cln":
        return n > 0
    return kind in ("l2", "gp")


def dve_works(s):
    kind, n = s[0], s[1]
    if kind == "gdn":
        return n in (0, 1, 17) or n <= 14 and n >= 2 and n % 2 == 0
    if kind in ("sm", "fox", "l2", "gp", "x"):
        return n > 0
    if kind == "gs":
        return n < 12 and n != 1
    if kind == "cln":
        return n in (0, 1, 5)
    if kind == "ml":
        return n == 2
    return kind in ("dc", "ds", "df", "xd")


def to_act(s):
    kind, n = s[0], s[1]
    if kind == "fox":
        return int(1 <= n <= FOX)
    if kind == "x":
        return int(1 <= n <= XU)
    return {("sm", 1): 1, ("sm", 2): 1, ("gdn", 0): 2, ("cln", 1): 1, ("cln", 5): 3, ("ds", 2): 1, ("xd", 2): 1}.get((kind, n), 0)


def to_dve(s):
    kind, n = s[0], s[1]
    if kind == "fox":
        return int(1 <= n <= FOX)
    if kind == "x":
        return int(1 <= n <= XU)
    if kind == "l2" or kind == "gp":
        return int(n > 0)
    return {("sm", 1): 1, ("sm", 2): 1, ("gdn", 0): 2, ("cln", 5): 5, ("ds", 2): 1, ("xd", 2): 1}.get((kind, n), 0)


def upto(what, k):
    return sum(int(what(s)) for s in ITEMS[:k])


class Stage:

    def __init__(self, sem):
        self.sem, self.n = sem, 0

    def by(self, ins):
        ins.then_inc(self.sem, 1)
        self.n += 1


def build(nc, a, out):
    ctx = ExitStack()
    with ctx:
        def sb(name, shape, dt=F32):
            return ctx.enter_context(nc.sbuf_tensor(name, shape, dt))

        def ps(name, shape):
            return ctx.enter_context(nc.psum_tensor(name, shape, F32))

        def sem(name):
            return ctx.enter_context(nc.semaphore(name))

        def stage(name):
            return Stage(sem(name))

        cst = sb("cst", [P, N_CST * P + NB])
        cols = sb("cols", [P, N_BLK, P])
        xT = sb("xT", [P, KD, T])
        xh, xl = sb("xh", [P, KD, T], F32R), sb("xl", [P, KD, T], F32R)
        oh, ol = sb("oh", [P, KB, T], F32R), sb("ol", [P, KB, T], F32R)
        raw = sb("raw", [P, 2, KD, 256])
        wh, wl = sb("wh", [P, 2, KD, P], F32R), sb("wl", [P, 2, KD, P], F32R)
        OD, OB, OC, QKV, G, DEC = 0, 2080, 4160, 6240, 12480, 18624
        DEC_N = 4 * 512 + 512 + PAGES * NB * FH
        SQ = DEC + DEC_N
        PR = SQ + 2 * T
        SM = PR + 4 * T + 2 * 524 + T
        ptr_, ptc = sb("ptr", [1, PAGES * NB], I32), sb("ptc", [P, 1], I32)
        base = -(-nc.sbuf_base // 32) * 32
        ar = sb("ar", [P, SM + 694])

        def v(at, *shape):
            n = int(np.prod(shape))
            x = ar[:, at:at + n]
            if len(shape) == 2:
                x = x.rearrange("p (a b) -> p a b", a=shape[0])
            if len(shape) == 3:
                x = x.rearrange("p (a b c) -> p a b c", a=shape[0], b=shape[1])
            return x

        oD, oB, oC = v(OD, KB, T), v(OB, KB, T), v(OC, KB, T)
        qkv = v(QKV, 12, T)
        fq, fk, fv = qkv[:, 0:4, :], qkv[:, 4:8, :], qkv[:, 8:12, :]

        def gx_tile(n):
            return qkv[:, (8 + n) % 12, :]

        kring = v(DEC, 4, 512)
        qb = v(DEC + 2048, 512)
        sc = v(DEC + 2560, PAGES * NB, FH)
        lsq, lrs = v(SQ, T), v(SQ + T, T)
        pairA, pairB = v(PR, 2, T), v(PR + 2 * T, 2, T)
        cb = v(PR + 4 * T, 2, 524)
        tmp = v(PR + 4 * T + 1048, T)
        sm_at = [SM]

        def small(n, *shape):
            at = sm_at[0]
            sm_at[0] += n
            assert sm_at[0] <= SM + 694
            return v(at, *(shape or (n,)))

        glu = xT[:, :, :].rearrange("p a b -> p (a b)")[:, KD * T - 4 * 550:].rearrange("p (a b) -> p a b", a=4)
        tail_gx, tail_cf = small(132, 12, 11), small(152, 4, 38)
        tail_sc = cols[:, B_SS, 64:104].rearrange("p (a b) -> p a b", a=KB)
        fs = small(96, 12, 8)
        gtok, btok = small(16, 4, 4), small(16, 4, 4)
        fltok = small(32, 4, 8)
        zsam = small(16)
        bsc = small(128, 8, 16)
        bias = small(20)
        eps6, eps5 = small(1), small(1)
        dcol, edc, edl, kdf, bed = (small(16) for _ in range(5))
        nmx, rsum = small(2), small(2)
        fl8 = cols[:, B_SS, 104:112]
        htmp = v(PR + 4 * T + 1048, NB, 30)

        ident, ones = cst[:, 0:P], cst[:, P:2 * P]

        def cs(n):
            return cst[:, n * P:(n + 1) * P]

        def col(n):
            return cols[:, B_VEC, n:n + 1]

        pb = ps("pb", [P, 2, 2, 512])
        sd = ps("sd", [P, 4, 512])
        s0, s1, s2, s3 = (sd[:, n, :] for n in range(4))

        xscr = nc.dram_tensor("x_scratch", (P, KD * T), F32, kind="Internal").ap()
        qscr = nc.dram_tensor("q_scratch", (NB, 512), F32, kind="Internal").ap()

        par_in, x_in, small_in, mem_in, lf_in, pt_in = (sem(n) for n in (
            "par_in", "x_in", "small_in", "mem_in", "lf_in", "pt_in"))
        raw_in = [sem(f"raw_in{n}") for n in range(2)]
        page_in = [sem(f"page_in{n}") for n in range(4)]
        qb_in, xs_out, xs_in, qs_out = sem("qb_in"), sem("xs_out"), sem("xs_in"), sem("qs_out")
        out_sem = sem("out_sem")
        stg_out = [sem(f"stg_out{n}") for n in range(2)]
        ss_in, ss_out, mv_in = sem("ss_in"), sem("ss_out"), [sem(f"mv_in{n}") for n in range(2)]
        pool_c, act_c, dve_c = stage("pool_chain"), stage("act_chain"), stage("dve_chain")
        pool_made = stage("pool_made")
        hi, lo = stage("hi_ready"), stage("lo_ready")
        piece_done, mt_act, mt_dve = stage("piece_done"), stage("mt_act"), stage("mt_dve")
        ev_y, ev_t, ev_all = stage("conv_ready"), stage("act_second"), stage("dve_tile_done")
        pe_s, act_s, dve_s = stage("pe_side"), stage("act_side"), stage("dve_side")
        v2a, a2v = stage("dve_to_act"), stage("act_to_dve")
        prod_done, page_free, v_used = stage("prod_done"), stage("page_free"), stage("v_used")
        n_sq, n_pe, n_rt, n_tmp, n_hi = (stage(n) for n in ("norm_sq", "norm_pe", "norm_root", "norm_tmp", "norm_hi"))
        n_lo, sp_hi, sp_lo = stage("norm_lo"), stage("split_hi"), stage("split_lo")
        pro_pe, pro_dve = stage("pro_pe"), stage("pro_dve")
        ss_st, vt_out, gs_out, mk_in = sem("row_stores"), sem("vt_out"), sem("gs_out"), sem("mk_in")
        side_at, out_total = [0], [16 * 8]
        mt_a = [sum(MT_ACT[:m + 1]) for m in range(len(MT_ACT))]
        mt_d = [m + 1 - mt_a[m] for m in range(len(MT_ACT))]
        dve_tile = [k in ("cg", "gx", "ac", "ah", "ab", "gz", "wo", "co", "fg", "fu", "fo") and k != "ac" or k.startswith("br")
                    for k in MT_KIND]
        conv_tile = [k in ("gx", "fg") for k in MT_KIND]
        second_tile = [k in ("gx", "fg", "ab", "fu") for k in MT_KIND]

        def count(flags, m):
            return sum(int(x) for x in flags[:m + 1])

        def mt_of(kind, idx=None):
            return max(m for m, k in enumerate(MT_KIND) if k == kind and (idx is None or PIECES[MT_LAST[m]][4] == idx))

        def n_of(flags, m):
            return sum(int(x) for x in flags[:m])

        pv = v(QKV, N_BLK, P)
        xrow = v(0, 5, D)
        wsm = v(G, KD, 16)
        vt = v(G, QT, 512)
        fP, fPT = v(G + 2048, 512), v(G + 2560, QT, P)
        stg = v(G + 4096, 2, 512)
        cneg, srow = v(G + 5120, 512), v(G + 3072, 2, 512)
        gR, gkd, gvb, gQK, gqd, gN, gX, gXT, gQ, gM, gW, gS = (v(G + 512 * n, GH, P) for n in range(12))
        ssam = v(G, NB * GH, P)
        g2 = G + 4096
        kc, qkp, vc, kqs, dl, oo = (v(g2, 32), v(g2 + 32, 32, 2), v(g2 + 96, 32), v(g2 + 128, 32), v(g2 + 160, 32), v(g2 + 192, 32))
        krow, drow_, blk = v(g2 + 256, P), v(g2 + 384, P), v(g2 + 512, 4, P)
        lf, cpg = v(DEC, P, FH), v(DEC + 1024, FH, P)
        g3 = DEC + 2048
        tot, totm, offs, cq = v(g3, 8), v(g3 + 8, NB, FH), v(g3 + 72, 8), v(g3 + 80, NB, FH)
        qk32, m1, pn, rd64 = v(g3 + 144, 4, NB), v(g3 + 176, 1), v(g3 + 192, NB, FH), v(g3 + 256, NB, FH)
        mx64, mb, rs64, dg64 = v(g3 + 320, NB, FH), v(g3 + 384, NB, FH), v(g3 + 448, NB, FH), v(SQ, 64)
        mkT, mvT, mv = v(0, XH, MEM), v(1024, XH, MEM), v(2048, 2, 512)
        qc, oX = v(3072, XH, T), v(5152, XH, T)
        xP, xPT = v(7232, MEM), v(7488, 2, P)
        memT, mrow = v(7744, KD, MEM), v(9792, 2, D)
        kvc = v(11840, NB, 2, 512)
        xstg, qrow = v(20032, 2, 512), v(21056, 512)
        xsc = v(21568, NB, 2, XH)
        x4 = 21632
        xmx, xm1, xdg, xrs, xrd = v(x4, NB, XH), v(x4 + 32, 1), v(x4 + 64, 32), v(x4 + 96, NB, XH), v(x4 + 128, NB, XH)
        mstg = v(PR + 4 * T, 2, 512)
        tail_ff = v(SM, KF, 10)
        hh = nc.alloc_sbuf_tensor_at("hh", [P, KF, T], F32R, offset=base)
        hl = nc.alloc_sbuf_tensor_at("hl", [P, KF, T], F32R, offset=base + 4 * T * KF)

        def sel(h):
            return ident[0:NB, h:h + 1].to_broadcast([NB, P])

        sqb = pairA
        memh = oh[:, :, :].rearrange("p a b -> p (a b)")[:, 0:KD * MEM].rearrange("p (a b) -> p a b", a=KD)
        meml = ol[:, :, :].rearrange("p a b -> p (a b)")[:, 0:KD * MEM].rearrange("p (a b) -> p a b", a=KD)
        zt, az, zl, zb, exs = v(SQ, 80), v(SQ + 80, 80), v(SQ + 160, 80), v(SQ + 240, 80), v(SQ + 320, NB, 16)
        exports = {
            "ex": [(tail_gx, 4 * j, 4, 11, 3, out["gc_p"][0, 0, :, 512 * j:512 * j + 512],
                    out["gc_s"][:, 0, GCW - 2, 512 * j:512 * j + 512]) for j in range(3)]
            + [(tail_sc, 0, 4, 10, 2, out["sc_p"][0, 0], out["sc_s"][:, 0, SCW - 2]),
               (tail_cf, 0, 4, 38, 30, out["cf_p"][0, 0], out["cf_s"][:, 0, CFW - 2])],
            "ef": [(tail_ff, 4 * j, min(4, KF - 4 * j), 10, 2, out["ff_p"][0, 0, :, 512 * j:min(512 * (j + 1), FF)],
                    out["ff_s"][:, 0, FCW - 2, 512 * j:min(512 * (j + 1), FF)]) for j in range(6)]}

        def both(x):
            return x.rearrange("p (a b) -> p a b", a=2)

        def bulk(m):
            return pb[:, m % 2, :, 0:TH]

        def spread(x, n, axis):
            return x[:, None, :].to_broadcast([x.shape[0], n, x.shape[1]]) if axis == 1 else \
                x[:, :, None].to_broadcast([x.shape[0], x.shape[1], n])

        def fox_stored(eng):
            eng.wait_ge(qs_out, 16)
            eng.wait_ge(ss_st, 32)
            eng.wait_ge(vt_out, 64)
            for b in range(2):
                eng.wait_ge(stg_out[b], 32)

        W = {"w_in": a["w_in"][0], "w_branch": a["w_branch"][0].rearrange("i r c -> (i r) c"), "w_out": a["w_out"][0],
             "w_ckv": a["w_ckv"][0], "w_cq": a["w_cq"][0], "w_co": a["w_co"][0], "w_ffn_in": a["w_ffn_in"][0],
             "w_ffn_out": a["w_ffn_out"][0]}

        block = ctx.enter_context(nc.Block())

        @block.sync
        def _(sp):
            for t in range(QT):
                sp.dma_start(xrow[:, t, :], a["x_prompt"][0, t * P:(t + 1) * P, :]).then_inc(x_in, 16)
            sp.dma_start(xrow[0:NB, QT, :], a["x_sample"].rearrange("b t d -> (b t) d")).then_inc(x_in, 16)
            sp.dma_start(cst[:, :], a["cst"]).then_inc(par_in, 16)
            sp.wait_ge(pool_made.sem, 1)
            rows = [(V_MIX, "norm_mix"), (V_CROSS, "norm_cross"), (V_FFN, "norm_ffn"), (V_MEM, "norm_mem"),
                    (V_CB, "conf_dw_b"), (V_LG, "conf_ln_g"), (V_LB, "conf_ln_b"), (V_GN, "gdn_norm")]
            for at, name in rows:
                src = a[name].rearrange("l (r c) -> (l r) c", c=P)
                sp.dma_start(pv[at:at + src.shape[0], B_VEC, :], src).then_inc(par_in, 16)
            sp.dma_start(pv[V_FIN:V_FIN + 8, B_VEC, :], a["norm_final"].rearrange("(r c) -> r c", c=P)).then_inc(par_in, 16)
            for at, b, name in ((V_SW, B_VEC, "sconv_w"), (V_GW, B_VEC, "gdn_conv_w"), (0, B_CW, "conf_dw_w"),
                                (0, B_FW, "ffn_conv_w")):
                src = a[name].rearrange("l w (r c) -> (l w r) c", c=P)
                sp.dma_start(pv[at:at + src.shape[0], b, :], src).then_inc(par_in, 16)
            for b, n, name in ((B_SS, 1, "state_sconv"), (B_GS, 4, "state_gdn_conv"), (B_CS, 8, "state_conf_conv"),
                               (B_FS, 4, "state_ffn_conv")):
                src = a[name].rearrange("b l w (r c) -> (b l w r) c", c=P)
                m = src.shape[0] // n
                sp.dma_start(pv[0:m, b:b + n, :], src.rearrange("(n m) c -> m n c", n=n)).then_inc(par_in, 16)
            with nc.allow_non_contiguous_dma(reason="16 columns of w_in, and vectors read by all partitions"):
                sp.wait_ge(pool_made.sem, 2)
                sp.dma_start(wsm[:, :, 0:8], W["w_in"][:, C_GA:C_GA + 8].rearrange("(k p) n -> p k n", p=P)).then_inc(small_in, 16)
                sp.dma_start(wsm[:, :, 8:16], W["w_in"][:, C_FF:C_FF + 8].rearrange("(k p) n -> p k n", p=P)).then_inc(small_in, 16)
                sp.dma_start(bias[:, 0:4], a["gdn_dt_bias"].to_broadcast([P, 4])).then_inc(small_in, 16)
                sp.dma_start(bias[:, 8:16], a["fox_fbias"].to_broadcast([P, 8])).then_inc(small_in, 16)
                sp.dma_start(bias[:, 16:20], a["gdn_a_log"].to_broadcast([P, 4])).then_inc(small_in, 16)
            for u, (w, row, kt, c) in enumerate(UNITS):
                if u >= 2:
                    sp.wait_ge(lo.sem, 2 * u - 2)
                sp.dma_start(raw[:, u % 2, 0:kt, :], W[w][row:row + kt * P, c:c + 256].rearrange("(k p) n -> p k n", p=P))\
                    .then_inc(raw_in[u % 2], 16)
            sp.dma_start(out["sc_s"][:, 0, 0:SCW - 2], a["state_sconv"][:, 0, 1:]).then_inc(out_sem, 16)
            sp.dma_start(out["gc_s"][:, 0, 0:GCW - 2], a["state_gdn_conv"][:, 0, 1:]).then_inc(out_sem, 16)
            sp.dma_start(out["cf_s"][:, 0, 0:CFW - 2], a["state_conf_conv"][:, 0, 1:]).then_inc(out_sem, 16)
            sp.dma_start(out["ff_s"][:, 0, 0:FCW - 2], a["state_ffn_conv"][:, 0, 1:]).then_inc(out_sem, 16)

        @block.gpsimd
        def _(pool):
            def own(ins, st=pool_c):
                st.by(ins)
                pool.wait_ge(st.sem, st.n)

            own(pool.memset(pv[:, :, :], 0.0), pool_made)
            own(pool.memset(bias[:, :], 0.0), pool_made)
            own(pool.memset(cb[:, :, 0:3], 0.0), pool_made)
            own(pool.memset(eps6[:, :], 1e-6), pool_made)
            own(pool.memset(eps5[:, :], 1e-5), pool_made)
            own(pool.memset(fl8, 0.0), pool_made)
            pages = PAGES * NB
            pool.dma_start(ptr_[:, :], a["page_table"].rearrange("(o b) j -> o (b j)", o=1)).then_inc(pt_in, 16)
            pool.dma_start(ptc[:, :], a["page_table"].rearrange("b (j o) -> (b j) o", o=1)).then_inc(pt_in, 16)
            pool.wait_ge(pt_in, 32)

            def load(cache, i):
                page = pool.value_load(ptr_[0:1, i:i + 1], min_val=0, max_val=a[cache].shape[0] - 1)
                pool.dma_start(kring[:, i % 4, :], a[cache][bass.ds(page, 1)].rearrange("a p l h d -> (a p) (l h d)"))\
                    .then_inc(page_in[i % 4], 16)

            def split(p):
                u, half, kt = PIECES[p][:3]
                pool.wait_ge(hi.sem, p + 1)
                lo.by(pool.tensor_tensor(wl[:, p % 2, 0:kt, :], raw[:, u % 2, 0:kt, half * P:(half + 1) * P],
                                         wh[:, p % 2, 0:kt, :].bitcast(F32), SUB))

            def product(i):
                if i + 2 < N_PAGE:
                    if i >= 2:
                        pool.wait_ge(page_free.sem, i - 1)
                    load("cache_fox_k", i + 2)
                if i % PAGES == 0:
                    if i == 0:
                        pool.wait_ge(qs_out, 16)
                    pool.dma_start(qb[:, :], qscr[i // PAGES:i // PAGES + 1, :].to_broadcast([P, 512])).then_inc(qb_in, 16)
                    pool.wait_ge(qb_in, 16 * (i // PAGES + 1))
                pool.wait_ge(page_in[i % 4], 16 * (i // 4 + 1))
                own(pool.tensor_tensor(kring[:, i % 4, :], kring[:, i % 4, :], qb[:, :], MUL), prod_done)

            for i in range(2):
                load("cache_fox_k", i)
            split(0)
            for e in TIMELINE:
                if e[0] == "piece" and e[2] == 0 and e[1] + 1 < NP_:
                    split(e[1] + 1)
                elif e[0] == "k":
                    product(e[1])
                elif e[0] == "kend":
                    pool.wait_ge(page_free.sem, N_PAGE)
                    pool.indirect_dma_start(lf[:, :, :].rearrange("p a b -> p (a b)"), None,
                                            a["cache_fox_logf"].rearrange("n p l h -> n (p l h)"),
                                            bass.IndirectOffsetOnAxis(ap=ptc[:, 0:1], axis=0)).then_inc(lf_in, 16)
                elif e[0] == "vstart":
                    pool.wait_ge(pe_s.sem, upto(pe_works, ITEMS.index(("dc", 1)) + 1))
                    for i in range(3):
                        load("cache_fox_v", i)
                elif e[0] == "v" and e[1] + 3 < N_PAGE:
                    if e[1] >= 1:
                        pool.wait_ge(v_used.sem, e[1])
                    load("cache_fox_v", e[1] + 3)

        @block.tensor
        def _(pe):
            def mm(o, l, r, start=True, stop=True):
                return pe.matmul(o, l, r, start=start, stop=stop, skip_group_check=True)

            def tr(o, i):
                n = i.shape[0]
                return pe.transpose(o, i, ident[0:n, 0:n])

            pe.wait_ge(par_in, 16 * 18)
            for j in range(5):
                if j == 4:
                    pe.wait_ge(pro_dve.sem, 1)
                for b in range(4 * j, min(4 * j + 4, N_BLK)):
                    last = tr(sd[:, j % 4, (b % 4) * P:(b % 4 + 1) * P], pv[:, b, :])
                pro_pe.by(last)
            pe.wait_ge(x_in, 16 * 5)
            for j in range(9):
                pe.wait_ge(pro_dve.sem, 5 + j - 3)
                o = sd[:, (5 + j) % 4, :]
                if j < KD:
                    for t in range(QT):
                        last = tr(o[:, t * P:(t + 1) * P], xrow[:, t, j * P:(j + 1) * P])
                else:
                    for k in range(KD):
                        last = tr(o[:, k * NB:(k + 1) * NB], xrow[0:NB, QT, k * P:(k + 1) * P])
                pro_pe.by(last)

            def norm(i, width):
                if i > 0:
                    m = mt_of({1: "wo", 2: "wo", 3: "co", 4: "fo"}[i])
                    for st, c in ((mt_act, mt_a), (mt_dve, mt_d)):
                        pe.wait_ge(st.sem, c[m])
                if i > 0:
                    pe.wait_ge(n_rt.sem, i)
                for k in range(KD):
                    pe.wait_ge(n_sq.sem, KD * i + k + 1)
                    for h in range(1 if width == MEM else 2):
                        w = MEM if width == MEM else TH
                        last = mm(pb[:, 0, h, 0:w], ones, sqb[:, k % 2, h * w:(h + 1) * w], k == 0, k == KD - 1)
                    n_pe.by(last)

            ready = {}

            def rhs_ready(p):
                kind = PIECES[p][3]
                if kind == "fq":
                    pe.wait_ge(n_lo.sem, KD)
                elif kind == "brA":
                    pe.wait_ge(ev_all.sem, count(dve_tile, mt_of("ab")))
                elif kind in ("brC", "brB", "brD", "co"):
                    pe.wait_ge(sp_lo.sem, {"brC": 4, "brB": 8, "brD": 12, "co": 12 + KD + 4}[kind])
                elif kind == "wo":
                    pe.wait_ge(sp_lo.sem, 12 + KD)
                elif kind == "kv":
                    pe.wait_ge(n_lo.sem, 2 * KD)
                    pe.wait_ge(n_rt.sem, 3)
                elif kind == "cq":
                    pe.wait_ge(n_lo.sem, 3 * KD)
                elif kind == "fg":
                    pe.wait_ge(n_lo.sem, 4 * KD)
                elif kind == "fo":
                    pe.wait_ge(ev_all.sem, count(dve_tile, mt_of("fu")))
                else:
                    return

            def piece(p, h):
                u, half, kt, kind, idx, first, last_ = PIECES[p]
                m = PIECE_MT[p]
                if h == 0:
                    pe.wait_ge(hi.sem, p + 1)
                    pe.wait_ge(lo.sem, p + 1)
                    if kind not in ready:
                        ready[kind] = True
                        rhs_ready(p)
                    if first and m >= 2:
                        if MT_ACT[m - 2]:
                            pe.wait_ge(mt_act.sem, mt_a[m - 2])
                        else:
                            pe.wait_ge(mt_dve.sem, mt_d[m - 2])
                    if p == 0:
                        pe.wait_ge(n_rt.sem, 1)
                if kind == "kv" and h == 1:
                    return
                w = MEM if kind == "kv" else TH
                c = slice(0, MEM) if kind == "kv" else slice(h * TH, (h + 1) * TH)
                k0 = UNITS[u][1] // P if kind == "fo" else 0
                for k in range(kt):
                    if kind == "kv":
                        xa, xb = memh[:, k, :], meml[:, k, :]
                    elif kind.startswith("br") or kind == "co":
                        xa, xb = oh[:, k, c], ol[:, k, c]
                    elif kind == "fo":
                        xa, xb = hh[:, k0 + k, c], hl[:, k0 + k, c]
                    else:
                        xa, xb = xh[:, k, c], xl[:, k, c]
                    o = pb[:, m % 2, h, 0:w]
                    mm(o, wh[:, p % 2, k, :], xa, first and k == 0, False)
                    mm(o, wh[:, p % 2, k, :], xb, False, False)
                    last = mm(o, wl[:, p % 2, k, :], xa, False, last_ and k == kt - 1)
                if h == 1 or kind == "kv":
                    piece_done.by(last)

            def side(K, s):
                kind, n = s[0], s[1]
                if not pe_works(s):
                    return
                if upto(act_works, K + 1):
                    pe.wait_ge(act_s.sem, upto(act_works, K + 1))
                if upto(dve_works, K + 1):
                    pe.wait_ge(dve_s.sem, upto(dve_works, K + 1))
                last = None
                if kind == "sm" and n == 0:
                    pe.wait_ge(small_in, 16 * 5)
                    for t in range(5):
                        w = P if t < QT else NB
                        for k in range(KD):
                            mm(s3[0:w, t * 16:t * 16 + 16], xh[:, k, t * P:t * P + w].bitcast(F32), wsm[:, k, :], k == 0, False)
                            last = mm(s3[0:w, t * 16:t * 16 + 16], xl[:, k, t * P:t * P + w].bitcast(F32), wsm[:, k, :], False, k == KD - 1)
                elif kind == "sm" and n == 1:
                    for t in range(QT):
                        tr(s0[0:FH, t * P:(t + 1) * P], fltok[:, t, :])
                    mm(s1[:, 0:P], ones[0:NB, :], exs[0:NB, :])
                    mm(s2[:, 0:16], cs(I_UP), gtok[:, :, :].rearrange("p a b -> p (a b)"))
                    last = mm(s2[:, 16:32], ones, gtok[:, :, :].rearrange("p a b -> p (a b)"))
                elif kind == "fst" and n < 3:
                    if n == 0:
                        pe.wait_ge(mt_act.sem, mt_a[mt_of("fv")])
                    for c in range(4):
                        last = tr(s0[0:NB, c * P:(c + 1) * P], fs[:, 4 * n + c, :])
                elif kind in ("fvt", "fkt") and n < QT:
                    src = fv if kind == "fvt" else fk
                    for c in range(4):
                        last = tr(s0[:, c * P:(c + 1) * P], src[:, c, n * P:(n + 1) * P])
                elif kind == "fox":
                    if n < FOX:
                        h, q = divmod(n, QT)
                        r = slice(FD * (h % 2), FD * (h % 2) + FD)
                        w = (q + 1) * P
                        mm(s0[:, 0:w], fq[r, h // 2, q * P:(q + 1) * P], fk[r, h // 2, 0:w], True, False)
                        mm(s0[:, 0:w], sel(h), cneg[0:FH, 0:w], False, False)
                        last = mm(s0[:, q * P:w], ident, cs(I_CAUSAL), False, True)
                    if 1 <= n <= FOX:
                        for b in range((n - 1) % QT + 1):
                            last = tr(s1[:, b * P:(b + 1) * P], fP[:, b * P:(b + 1) * P])
                    if 2 <= n <= FOX + 1:
                        h, q = divmod(n - 2, QT)
                        for b in range(q + 1):
                            last = mm(s2[FD * (h % 2):FD * (h % 2) + FD, 0:P], vt[:, b, h * FD:(h + 1) * FD], fPT[:, b, :], b == 0, b == q)
                elif kind in ("l2", "gp"):
                    if n < (8 if kind == "l2" else 4):
                        for h in range(2):
                            last = mm(sd[:, h, 0:TH], ones, lsq[:, h * TH:(h + 1) * TH])
                elif kind == "gdn":
                    c = s[2]
                    cc = slice(c * P, (c + 1) * P)
                    for h in range(GH):
                        o = slice(h * P, (h + 1) * P)
                        q_, k_, v_ = (gx_tile(4 * j + h)[:, cc] for j in range(3))
                        if n == -1:
                            tr(s0[:, o], k_)
                            tr(s1[:, o], v_)
                            last = mm(s2[:, o], gtok[:, c, h:h + 1].to_broadcast([P, P]), cs(I_UP))
                        elif n == 0:
                            last = mm(s0[:, o], k_, k_)
                        elif n == 1:
                            mm(s0[:, o], k_, q_)
                            last = tr(s1[:, o], gM[:, h, :])
                        elif 2 <= n <= 12 and n % 2 == 0:
                            last = mm(s0[:, o], gM[:, h, :], gXT[:, h, :])
                        elif 3 <= n <= 13:
                            last = mm(s1[:, o], gX[:, h, :], gQ[:, h, :])
                            if n < 13:
                                last = mm(s2[:, o], gQ[:, h, :], gX[:, h, :])
                        elif n == 14:
                            mm(s0[:, o], gXT[:, h, :], gvb[:, h, :], h == 0, False)
                            last = mm(s1[:, o], gR[:, h, :], gXT[:, h, :])
                        elif n == 15:
                            last = mm(s0[:, o], gW[:, h, :], gS[:, h, :], False, h == GH - 1)
                        elif n == 16:
                            mm(s2[:, o], gS[:, h, :], gqd[:, h, :], True, False)
                            mm(s2[:, o], gM[:, h, :], gQK[:, h, :], False, True)
                            last = mm(s1[:, o], gkd[:, h, :], gM[:, h, :])
                elif kind == "cln":
                    for c in (range(KB) if n == 0 else [n - 1] if n < 5 else []):
                        src = oC[:, c, :] if n == 0 else lsq
                        for h in range(2):
                            last = mm(sd[:, (0 if n == 0 else 2) + h, 0:TH], ones, src[:, h * TH:(h + 1) * TH], c == 0, c == KB - 1)
                elif kind == "gs":
                    if n == 1:
                        pe.wait_ge(ss_in, 16)
                        for u in range(32):
                            mm(s0[:, 2 * u:2 * u + 2], ssam[:, u, :], qkp[:, u, :])
                        last = mm(s1[:, 0:32], ones, kqs)
                    elif n == 2:
                        tr(s2[0:32, 0:P], dl)
                        last = tr(s2[0:32, P:2 * P], kc)
                    elif 3 <= n <= 10:
                        last = mm(s0[:, :], krow[0:32, :], blk[0:32, :, :].rearrange("p a b -> p (a b)"))
                elif kind == "dc" and n == 0:
                    mm(s0[:, 0:FH], cs(I_PAGE), tot)
                    last = mm(s1[:, 0:64], ones, totm[:, :, :].rearrange("p a b -> p (a b)"))
                elif kind == "dc" and n == 1:
                    for h in range(FH):
                        last = tr(sd[:, 2 + h // 4, (h % 4) * P:(h % 4 + 1) * P], cpg[:, h, :])
                elif kind == "ds" and n == 0:
                    tr(s0[0:64, 0:P], mx64[:, :, :].rearrange("p a b -> p (a b)"))
                    f = qk32[:, :, :].rearrange("p a b -> p (a b)")
                    mm(s1[:, 0:32], cs(I_LO), f)
                    last = mm(s1[:, 32:64], cs(I_HI), f)
                elif kind == "ds" and n == 1:
                    last = mm(s2[:, 0:64], ones[0:64, :], dg64[0:64, :])
                elif kind == "ds" and n == 2:
                    last = mm(s3[:, 0:64], ones, rs64[:, :, :].rearrange("p a b -> p (a b)"))
                elif kind in ("ex", "ef") and pe_works(s):
                    src, c0, nc_, w = exports[kind][n][:4]
                    for c in range(nc_):
                        last = tr(s0[0:w, c * P:(c + 1) * P], src[:, c0 + c, :])
                elif kind == "ml" and n == 1:
                    pe.wait_ge(mem_in, 16)
                    for k in range(KD):
                        for t in range(2):
                            last = tr(sd[:, k // 2, ((k % 2) * 2 + t) * P:((k % 2) * 2 + t + 1) * P], mrow[:, t, k * P:(k + 1) * P])
                elif kind == "xm" and n == 0:
                    pe.wait_ge(mt_act.sem, mt_a[mt_of("cq")])
                    for t in range(2):
                        for h in range(XH):
                            tr(sd[:, t, h * P:(h + 1) * P], mvT[:, h, t * P:(t + 1) * P])
                            last = tr(sd[:, 2 + t, h * P:(h + 1) * P], mkT[:, h, t * P:(t + 1) * P])
                elif kind == "xm" and n == 1:
                    for h in range(XH):
                        last = tr(s0[0:NB, h * P:(h + 1) * P], qc[:, h, SEQ:T])
                elif kind == "x":
                    if n < XU:
                        h, q = divmod(n, QT)
                        last = mm(s0[:, 0:MEM], qc[:, h, q * P:(q + 1) * P], mkT[:, h, :])
                    if 1 <= n <= XU:
                        for t in range(2):
                            last = tr(s1[:, t * P:(t + 1) * P], xP[:, t * P:(t + 1) * P])
                    if 2 <= n <= XU + 1:
                        h, q = divmod(n - 2, QT)
                        for t in range(2):
                            last = mm(s2[:, 0:P], mv[:, t, h * P:(h + 1) * P], xPT[:, t, :], t == 0, t == 1)
                    if 1 <= n <= NB:
                        last = mm(s3[:, :], sel(n - 1), qrow[0:NB, :])
                elif kind == "xd" and n == 0:
                    last = tr(s0[0:32, 0:P], xmx[:, :, :].rearrange("p a b -> p (a b)"))
                elif kind == "xd" and n == 1:
                    last = mm(s1[:, 0:32], ones[0:32, :], xdg[0:32, :])
                elif kind == "xd" and n == 2:
                    mm(s2[:, 0:32], ones, xrs[:, :, :].rearrange("p a b -> p (a b)"))
                    for b in range(NB):
                        if b < 2:
                            pe.wait_ge(mv_in[b], 16 * NB // 2)
                        for h in range(XH):
                            for t in range(2):
                                last = mm(s3[:, b * 4 + h:b * 4 + h + 1], kvc[:, b, t, h * P:(h + 1) * P], xsc[:, b, t, h:h + 1], t == 0, t == 1)
                elif kind == "y" and n < 10:
                    if n == 0:
                        pe.wait_ge(n_tmp.sem, 5 * KD)
                    for c in range(4):
                        k = (n % 2) * 4 + c
                        t = n // 2
                        w = P if t < QT else NB
                        last = tr(s0[0:w, c * P:(c + 1) * P], xT[:, k, t * P:t * P + w])
                pe_s.by(last)

            def page(i):
                if i == 0:
                    pe.wait_ge(dve_s.sem, upto(dve_works, ITEMS.index(("ds", 3)) + 1))
                pe.wait_ge(page_in[i % 4], 16 * (N_PAGE // 4 + i // 4 + 1))
                for c in range(4):
                    at = (i // PAGES * 4 + c) * 2
                    last = mm(s3[:, at:at + 2], kring[:, i % 4, c * P:(c + 1) * P], sc[:, i, 2 * c:2 * c + 2],
                              i == 0 and c == 0, i == N_PAGE - 1 and c == 3)
                v_used.by(last)

            for e in TIMELINE:
                if e[0] == "norm":
                    norm(["mix", "mem", "cross", "ffn", "fin"].index(e[1]), MEM if e[1] == "mem" else T)
                elif e[0] == "piece":
                    piece(e[1], e[2])
                elif e[0] == "side":
                    side(e[1], e[2])
                elif e[0] == "v":
                    page(e[1])

        @block.scalar
        def _(act):
            def own(ins, st=act_c):
                st.by(ins)
                act.wait_ge(st.sem, st.n)

            def fn(o, i, f, st=act_c, **kw):
                own(act.activation(o, i, f, **kw), st)

            def split(p):
                u, half, kt = PIECES[p][:3]
                if half == 0:
                    act.wait_ge(raw_in[u % 2], 16 * (u // 2 + 1))
                if p >= 2:
                    act.wait_ge(piece_done.sem, p - 1)
                    act.wait_ge(lo.sem, p - 1)
                fn(wh[:, p % 2, 0:kt, :], raw[:, u % 2, 0:kt, half * P:(half + 1) * P], ACT.Copy, hi)

            def evac(m):
                p = MT_LAST[m]
                kind, idx = PIECES[p][3:5]
                s = idx % 2
                if MT_ACT[m] or second_tile[m]:
                    if m >= 2:
                        act.wait_ge(ev_all.sem, count(dve_tile, m - 2))
                if MT_ACT[m]:
                    act.wait_ge(piece_done.sem, p + 1)
                x = bulk(m)
                if kind in ("fq", "fk", "fv"):
                    j = 4 * ("fq", "fk", "fv").index(kind) + idx
                    fn(both(qkv[:, j, :]), x, ACT.Copy)
                    fn(fs[:, j, :], pb[:, m % 2, 1, TH - NB:TH], ACT.Copy, mt_act)
                elif kind == "cv":
                    fn(both(pairA[:, s, :]), x, ACT.Copy, mt_act, scale=0.5)
                elif kind == "cg" or kind.startswith("gate"):
                    fn(both(pairB[:, s, :]), x, ACT.Tanh, mt_act, scale=0.5)
                elif kind in ("gx", "fg"):
                    fn(both(cb[:, s, 3:3 + T]), x, ACT.Copy, mt_act)
                    y = gx_tile(idx) if kind == "gx" else pairA[:, s, :]
                    act.wait_ge(ev_y.sem, count(conv_tile, m))
                    fn(pairB[:, s, :], y, ACT.Tanh, ev_t)
                elif kind == "ac":
                    fn(both(pairA[:, s, :]), x, ACT.Copy, mt_act)
                elif kind == "gz":
                    fn(both(pairA[:, s, :]), x, ACT.Copy, scale=0.5)
                    fn(both(pairB[:, s, :]), x, ACT.Tanh, mt_act, scale=0.5)
                elif kind == "kv":
                    o = mkT[:, idx, :] if idx < XH else mvT[:, idx - XH, :]
                    fn(o, pb[:, m % 2, 0, 0:MEM], ACT.Copy, mt_act)
                elif kind == "cq":
                    fn(both(qc[:, idx, :]), x, ACT.Copy, mt_act)
                elif kind in ("ab", "fu"):
                    act.wait_ge(mt_dve.sem, mt_d[m])
                    fn(oh[:, idx, :] if kind == "ab" else hh[:, idx, :], tmp, ACT.Copy, ev_t)

            def norm(i, src, width, gain):
                scale = 1.0 / D
                for k in range(KD):
                    if k >= 2:
                        act.wait_ge(n_pe.sem, KD * i + k - 1)
                    if k == 0:
                        if i == 0:
                            act.wait_ge(pro_dve.sem, 14)
                            act.wait_ge(pool_made.sem, 6)
                        elif i == 1:
                            act.wait_ge(dve_s.sem, upto(dve_works, ITEMS.index(("ml", 2)) + 1))
                            act.wait_ge(ev_all.sem, count(dve_tile, mt_of("wo")))
                        elif i > 1:
                            act.wait_ge(ev_all.sem, count(dve_tile, mt_of({2: "wo", 3: "co", 4: "fo"}[i])))
                            act.wait_ge(n_lo.sem, KD * i)
                    fn(sqb[:, k % 2, 0:width], src[:, k, :], ACT.Square, n_sq)
                act.wait_ge(n_pe.sem, KD * (i + 1))
                if width == MEM:
                    fn(lrs[:, 0:MEM], pb[:, 0, 0, 0:MEM], ACT.Sqrt, n_rt, scale=scale, bias=eps6[:, 0:1])
                else:
                    fn(both(lrs), pb[:, 0, :, 0:TH], ACT.Sqrt, n_rt, scale=scale, bias=eps6[:, 0:1])
                if i == 4:
                    return
                for k in range(KD):
                    act.wait_ge(n_tmp.sem, KD * i + k + 1)
                    o = memh[:, k, :] if width == MEM else xh[:, k, :]
                    fn(o, sqb[:, k % 2, 0:width], ACT.Copy, n_hi)

            def store(dst, src, st=out_sem):
                act.dma_start(dst, src).then_inc(st, 16)

            used = [0, 0]

            def staged(n, copy):
                if used[n % 2]:
                    act.wait_ge(stg_out[n % 2], 16 * used[n % 2])
                copy()

            def sent(n, dst, src):
                used[n % 2] += 1
                store(dst, src, stg_out[n % 2])

            def side(K, s):
                kind, n = s[0], s[1]
                works = act_works(s) or s in (("gs", 0), ("gs", 12), ("ml", 0)) or (kind == "x" and n > 0)
                if not works:
                    return
                if upto(pe_works, K):
                    act.wait_ge(pe_s.sem, upto(pe_works, K))
                if upto(dve_works, K):
                    act.wait_ge(dve_s.sem, upto(dve_works, K))
                fins = None
                va, av = upto(to_act, K), upto(to_dve, K)
                if kind == "sm" and n == 1:
                    act.wait_ge(v2a.sem, va + 1)
                    for x_, y_ in ((slice(0, P), slice(0, 64)), (slice(0, NB), slice(64, 80))):
                        fn(zl[x_, y_], az[x_, y_], ACT.Exp, scale=-1.0)
                        fn(zb[x_, y_], zt[x_, y_], ACT.Tanh, scale=0.5)
                    fn(bias[:, 16:20], bias[:, 16:20], ACT.Exp)
                    fn(zl[:, 0:64], zl[:, 0:64], ACT.Ln, bias=1.0)
                    fn(zl[0:NB, 64:80], zl[0:NB, 64:80], ACT.Ln, a2v, bias=1.0)
                    fins = act.activation(rsum[:, 0:1], eps6[:, 0:1], ACT.Copy)
                elif kind == "sm" and n == 2:
                    act.wait_ge(v2a.sem, va + 1)
                    fn(bsc[:, :, 0:4], bsc[:, :, 0:4], ACT.Exp)
                    fn(edc, dcol, ACT.Exp)
                    fn(kdf, kdf, ACT.Exp)
                    fn(edl, edl, ACT.Exp, a2v)
                    with nc.allow_non_contiguous_dma(reason="8 values of a token"):
                        store(out["fl_p"][0, :, 0, :].rearrange("(t p) h -> p t h", p=P), fltok[:, :, :])
                        store(out["fl_s"][:, 0, 0, :], zsam[0:NB, 8:16])
                    fins = act.activation(rsum[:, 0:1], eps6[:, 0:1], ACT.Copy)
                elif kind == "fst":
                    def copy():
                        fn(srow[0:NB, n % 2, :], s0[0:NB, :], ACT.Copy)
                    if n == 3:
                        act.wait_ge(qs_out, 16)
                    copy()
                    if n == 1:
                        store(qscr, srow[0:NB, 1, :], qs_out)
                    else:
                        dst = out["fk_s" if n == 2 else "fv_s"]
                        store(dst.rearrange("b t l h d -> b (t l h d)"), srow[0:NB, n % 2, :], ss_st)
                    fins = act.activation(rsum[:, 0:1], eps6[:, 0:1], ACT.Copy)
                elif kind == "fvt":
                    fn(vt[:, n - 1, :], s0, ACT.Copy)
                    store(out["fv_p"][0, (n - 1) * P:n * P].rearrange("t l h d -> t (l h d)"), vt[:, n - 1, :], vt_out)
                    fins = act.activation(rsum[:, 0:1], eps6[:, 0:1], ACT.Copy)
                elif kind == "fkt":
                    if n >= 3:
                        act.wait_ge(stg_out[(n - 1) % 2], 16)
                    fn(stg[:, (n - 1) % 2, :], s0, ACT.Copy)
                    sent(n - 1, out["fk_p"][0, (n - 1) * P:n * P].rearrange("t l h d -> t (l h d)"), stg[:, (n - 1) % 2, :])
                    fins = act.activation(rsum[:, 0:1], eps6[:, 0:1], ACT.Copy)
                elif kind == "fox":
                    if n <= FOX:
                        w = ((n - 1) % QT + 1) * P
                        act.wait_ge(v2a.sem, va + 1)
                        fn(fP[:, 0:w], s0[:, 0:w], ACT.Exp, a2v, scale=FD ** -0.5, bias=nmx[:, 0:1], accum_out=rsum[:, 0:1])
                    w = ((n - 2) % QT + 1) if 2 <= n <= FOX + 1 else 1
                    if 2 <= n <= FOX + 1:
                        fins = act.activation(fPT[:, 0:w, :], s1[:, 0:w * P].rearrange("p (a b) -> p a b", a=w), ACT.Copy)
                    else:
                        fins = act.activation(rsum[:, 1:2], eps6[:, 0:1], ACT.Copy)
                elif kind in ("l2", "gp"):
                    last = 8 if kind == "l2" else 4
                    if n == 0 and kind == "l2":
                        act.wait_ge(ev_all.sem, count(dve_tile, mt_of("gx")))
                    if n:
                        fn(both(lrs), sd[:, 0:2, 0:TH], ACT.Sqrt, a2v, scale=1.0 if kind == "l2" else 1.0 / P, bias=eps6[:, 0:1])
                    if n < last:
                        fins = act.activation(lsq, gx_tile(n) if kind == "l2" else oB[:, n, :], ACT.Square)
                    else:
                        fins = act.activation(rsum[:, 0:1], eps6[:, 0:1], ACT.Copy)
                elif kind == "gdn":
                    c = s[2]
                    s4 = [x.rearrange("p (a b) -> p a b", a=GH) for x in (s0, s1, s2)]
                    if n == 0:
                        if c == 0:
                            fox_stored(act)
                        for h in range(GH):
                            o = slice(h * P, (h + 1) * P)
                            fn(gR[:, h, :], s0[:, o], ACT.Copy, scale=bed[:, 4 * c + h:4 * c + h + 1])
                            fn(gkd[:, h, :], s0[:, o], ACT.Copy, scale=kdf[:, 4 * c + h:4 * c + h + 1])
                        act.wait_ge(v2a.sem, va + 1)
                        fn(gQ[:, :, :], gQ[:, :, :], ACT.Exp, a2v, scale=-1.0)
                        act.wait_ge(v2a.sem, va + 2)
                        fn(gqd[:, :, :], s4[2], ACT.Exp, a2v)
                        fins = act.activation(gXT[:, :, :], gM[:, :, :], ACT.Exp)
                    elif n <= 13:
                        fins = act.activation(gQ[:, :, :], s4[0], ACT.Copy)
                    elif n == 15:
                        fins = act.activation(gW[:, :, :], s4[1], ACT.Copy, scale=-1.0)
                    elif n == 16:
                        fins = act.activation(gM[:, :, :], s4[0], ACT.Copy)
                    else:
                        fins = act.activation(oB[:, :, c * P:(c + 1) * P], s4[2], ACT.Copy)
                elif kind == "cln":
                    if n < 5:
                        if n == 1:
                            act.wait_ge(v2a.sem, va + 1)
                        fins = act.activation(lsq, oC[:, n - 1, :], ACT.Square)
                    else:
                        fn(both(lrs), sd[:, 2:4, 0:TH], ACT.Sqrt, a2v, scale=1.0 / BD, bias=eps5[:, 0:1])
                        for c in range(KB):
                            if c != 1:
                                act.wait_ge(v2a.sem, va + (1 if c == 0 else c))
                            fn(lsq if c % 2 == 0 else lrs, oC[:, c, :], ACT.Tanh, a2v)
                        fins = act.activation(rsum[:, 0:1], eps6[:, 0:1], ACT.Copy)
                elif kind == "gs" and n == 0:
                    act.wait_ge(qs_out, 16)
                    act.wait_ge(ss_st, 32)
                    act.wait_ge(vt_out, 64)
                    for b in range(2):
                        act.wait_ge(stg_out[b], 16 * used[b])
                    act.dma_start(ssam[:, :, :], a["state_gdn"].rearrange("b l h k v -> k (b l h) v")).then_inc(ss_in, 16)
                    store(out["S_p"].rearrange("b l h k v -> k (b l h) v"), gS[:, :, :], gs_out)
                elif kind == "gs" and n == 12:
                    store(out["S_s"].rearrange("b l h k v -> k (b l h) v"), ssam[:, :, :], ss_out)
                elif kind == "ds":
                    if n == 2:
                        act.wait_ge(v2a.sem, va + 1)
                        fn(pn[:, :, :], pn[:, :, :], ACT.Exp)
                        fn(sc[:, :, :], sc[:, :, :], ACT.Exp, a2v)
                        fins = act.activation(rsum[:, 0:1], eps6[:, 0:1], ACT.Copy)
                elif kind in ("ex", "ef"):
                    src, c0, nc_, w, wp, dp, ds_ = exports[kind][n - 1]
                    st_ = stg if kind == "ex" else mstg
                    j = (n - 1) % 2
                    if kind == "ex" and n == 1:
                        act.wait_ge(gs_out, 16)
                    if used[j]:
                        act.wait_ge(stg_out[j], 16 * used[j])
                    fn(st_[0:w, j, 0:nc_ * P], s0[0:w, 0:nc_ * P], ACT.Copy)
                    sent(j, dp, st_[0:wp, j, 0:nc_ * P])
                    sent(j, ds_, st_[wp:w, j, 0:nc_ * P])
                    fins = act.activation(rsum[:, 0:1], eps6[:, 0:1], ACT.Copy)
                elif kind == "ml" and n == 0:
                    for j in range(2):
                        act.wait_ge(stg_out[j], 16 * used[j])
                    act.dma_start(mrow[:, :, :], a["mem_prompt"][0].rearrange("(t p) d -> p t d", p=P)).then_inc(mem_in, 16)
                    act.dma_start(kvc[:, :, :, :].rearrange("p b t n -> p (b t) n"),
                                  a["cache_mem_k"].rearrange("b l (t p) h d -> p (b l t) (h d)", p=P)).then_inc(mk_in, 16)
                elif kind == "xm":
                    if n == 1:
                        fn(mv[:, :, :], sd[:, 0:2, :], ACT.Copy)
                        fn(xstg[:, :, :], sd[:, 2:4, :], ACT.Copy)
                        store(out["mv_p"][0, 0].rearrange("(t p) h d -> p t (h d)", p=P), mv[:, :, :])
                        store(out["mk_p"][0, 0].rearrange("(t p) h d -> p t (h d)", p=P), xstg[:, :, :])
                        fins = act.activation(rsum[:, 0:1], eps6[:, 0:1], ACT.Copy)
                    else:
                        fins = act.activation(qrow[0:NB, :], s0[0:NB, :], ACT.Copy)
                elif kind == "x":
                    if 3 <= n <= NB + 2:
                        b = n - 3
                        act.dma_start(kvc[:, b, :, :], a["cache_mem_v"][b, 0].rearrange("(t p) h d -> p t (h d)", p=P))\
                            .then_inc(mv_in[b % 2], 16)
                    if n <= XU:
                        act.wait_ge(v2a.sem, va + 1)
                        fn(xP, s0[:, 0:MEM], ACT.Exp, a2v, scale=P ** -0.5, bias=nmx[:, 0:1], accum_out=rsum[:, 0:1])
                    if 2 <= n <= XU + 1:
                        fins = act.activation(xPT[:, :, :], s1[:, 0:MEM].rearrange("p (a b) -> p a b", a=2), ACT.Copy)
                    elif n == 1:
                        fins = act.activation(rsum[:, 1:2], eps6[:, 0:1], ACT.Copy)
                elif kind == "xd":
                    if n == 2:
                        act.wait_ge(v2a.sem, va + 1)
                        fn(xsc[:, :, :, :], xsc[:, :, :, :], ACT.Exp, a2v, scale=P ** -0.5)
                        fins = act.activation(rsum[:, 0:1], eps6[:, 0:1], ACT.Copy)
                elif kind == "y":
                    w = P if n - 1 < 8 else NB
                    j, t = (n - 1) % 2, (n - 1) // 2
                    if used[j]:
                        act.wait_ge(stg_out[j], 16 * used[j])
                    fn(mstg[0:w, j, :], s0[0:w, :], ACT.Copy)
                    dst = out["y_p"][0, t * P:(t + 1) * P, j * 512:(j + 1) * 512] if t < QT else out["y_s"][:, 0, j * 512:(j + 1) * 512]
                    sent(j, dst, mstg[0:w, j, :])
                    fins = act.activation(rsum[:, 0:1], eps6[:, 0:1], ACT.Copy)
                if act_works(s):
                    own(fins, act_s)

            split(0)
            done = [0]
            spl = [0]
            for e in TIMELINE:
                if e[0] == "norm":
                    i = ["mix", "mem", "cross", "ffn", "fin"].index(e[1])
                    norm(i, memT if i == 1 else xT, MEM if i == 1 else T, None)
                    if i == 0:
                        store(xscr, xT[:, :, :].rearrange("p a b -> p (a b)"), xs_out)
                elif e[0] == "flush" or (e[0] == "piece" and e[2] == 0):
                    p = e[1] if e[0] == "piece" else None
                    if p is not None and p + 1 < NP_:
                        split(p + 1)
                    while done[0] < len(MT_LAST) and (MT_LAST[done[0]] < (p if p is not None else cur + 1)):
                        evac(done[0])
                        done[0] += 1
                    if p is not None:
                        cur = p
                elif e[0] == "piece":
                    cur = e[1]
                elif e[0] == "split":
                    src, n = {"brC": (oC, 4), "brB": (oB, 4), "brD": (oD, 4), "brX": (oX, 4), "merged": (xT, 8)}[e[1]]
                    act.wait_ge(piece_done.sem, cur if e[1] not in ("merged", "brX") else cur + 1)
                    act.wait_ge(ev_all.sem, count(dve_tile, done[0] - 1))
                    if upto(dve_works, side_at[0]):
                        act.wait_ge(dve_s.sem, upto(dve_works, side_at[0]))
                    for k in range(n):
                        fn((xh if n == 8 else oh)[:, k, :], src[:, k, :], ACT.Copy, sp_hi)
                    spl[0] += n
                    if e[1] == "merged":
                        act.wait_ge(sp_lo.sem, spl[0])
                        act.wait_ge(xs_out, 16)
                        act.dma_start(xT[:, :, :].rearrange("p a b -> p (a b)"), xscr).then_inc(xs_in, 16)
                elif e[0] == "side":
                    side(e[1], e[2])
                    side_at[0] = e[1] + 1
            for st_, k in ((out_sem, out_total[0]),):
                act.wait_ge(st_, k)
            for j in range(2):
                act.wait_ge(stg_out[j], 16 * used[j])
            act.wait_ge(ss_out, 16)
            act.wait_ge(gs_out, 16)
            act.wait_ge(ss_st, 32)
            act.wait_ge(vt_out, 64)

        @block.vector
        def _(dve):
            def own(ins, st=dve_c):
                st.by(ins)
                dve.wait_ge(st.sem, st.n)

            def tt(o, x, y, op, st=dve_c):
                own(dve.tensor_tensor(o, x, y, op), st)

            def ts(o, x, s1_, s2_=None, op0=MUL, op1=None, st=dve_c):
                own(dve.tensor_scalar(o, x, s1_, s2_, op0, op1) if op1 else dve.tensor_scalar(o, x, s1_, None, op0), st)

            def stt(o, x, s_, y, op0, op1, st=dve_c):
                own(dve.scalar_tensor_tensor(out=o, in0=x, scalar=s_, in1=y, op0=op0, op1=op1), st)

            def cp(o, x, st=dve_c):
                own(dve.tensor_copy(o, x), st)

            def red(o, x, op, st=dve_c):
                own(dve.tensor_reduce(o, x, AX, op), st)

            def conv(x, y, width, wcol, hist, w_last):
                ts(y, x[:, 3:3 + T], w_last)
                for j in range(width - 1):
                    stt(y[:, 0:SEQ], x[:, 4 - width + j:4 - width + j + SEQ], wcol(j), y[:, 0:SEQ], MUL, ADD)
                    past = hist(j)
                    ys = y[:, SEQ:T] if len(past.shape) == 2 else y[:, SEQ:T].rearrange("p (n b) -> p n b", b=2)
                    stt(ys, past, wcol(j), ys, MUL, ADD)


            def evac(m):
                p = MT_LAST[m]
                kind, idx = PIECES[p][3:5]
                s = idx % 2
                if MT_ACT[m]:
                    dve.wait_ge(mt_act.sem, mt_a[m])
                else:
                    dve.wait_ge(piece_done.sem, p + 1)
                x = bulk(m)
                if kind == "cg":
                    if idx == 0:
                        dve.wait_ge(xs_out, 16)
                        own(dve.memset(glu[:, :, 0:CFW - 1], 0.0))
                    stt(glu[:, idx, CFW - 1:CFW - 1 + T], pairB[:, s, :], 1.0, pairA[:, s, :], ADD, MUL)
                    cp(tail_cf[:, idx, :], glu[:, idx, SEQ:SEQ + 38], ev_all)
                elif kind == "gx":
                    cp(tail_gx[:, idx, :], cb[:, s, SEQ:SEQ + 11])
                    if idx == 0:
                        dve.wait_ge(pe_s.sem, upto(pe_works, ITEMS.index(("fvt", 4))))
                    if idx >= 4:
                        at = ITEMS.index(("fox", 8 * (idx % 4) + 9 if idx == 4 else FOX - 1))
                        dve.wait_ge(pe_s.sem, upto(pe_works, at + 1))

                    gh = cols[:, B_GS:B_GS + 4, 0:72].rearrange("p n (b r) -> p n b r", b=2)

                    def hist(j):
                        return gh[:, :, :, j * 12 + idx]

                    conv(cb[:, s, :], gx_tile(idx), GCW, lambda j: col(V_GW + 12 * j + idx), hist, col(V_GW + 36 + idx))
                    cp(fl8[:, 0:1], fl8[:, 1:2], ev_y)
                    dve.wait_ge(ev_t.sem, count(second_tile, m))
                    stt(gx_tile(idx), pairB[:, s, :], 1.0, gx_tile(idx), ADD, MUL, ev_all)
                elif kind == "ah":
                    tt(both(cb[:, s, 3:3 + T]), both(pairA[:, s, :]), x, MUL, mt_dve)
                    cp(tail_sc[:, idx, :], cb[:, s, SEQ + 1:SEQ + 11])
                    conv(cb[:, s, :], pairB[:, s, :], SCW, lambda j: col(V_SW + 4 * j + idx),
                         lambda j: cols[:, B_SS, 0:64].rearrange("p (b r) -> p b r", b=NB)[:, :, 4 * j + idx], col(V_SW + 8 + idx))
                    cp(fl8[:, 0:1], fl8[:, 1:2], ev_all)
                elif kind == "ab":
                    tt(both(tmp), both(pairB[:, s, :]), x, MUL, mt_dve)
                    dve.wait_ge(ev_t.sem, count(second_tile, m))
                    tt(ol[:, idx, :], tmp, oh[:, idx, :].bitcast(F32), SUB, ev_all)
                elif kind.startswith("br"):
                    if kind == "brA":
                        stt(both(xT[:, idx, :]), both(pairB[:, s, :]), 1.0, x, ADD, MUL, mt_dve)
                        cp(fl8[:, 0:1], fl8[:, 1:2], ev_all)
                    else:
                        stt(both(tmp), both(pairB[:, s, :]), 1.0, x, ADD, MUL, mt_dve)
                        tt(xT[:, idx, :], xT[:, idx, :], tmp, ADD, ev_all)
                elif kind == "gz":
                    stt(pairA[:, s, :], pairB[:, s, :], 1.0, pairA[:, s, :], ADD, MUL)
                    tt(oB[:, idx, :], oB[:, idx, :], pairA[:, s, :], MUL, ev_all)
                elif kind in ("wo", "co", "fo"):
                    if kind == "wo" and idx == 0:
                        dve.wait_ge(xs_in, 16)
                    stt(both(xT[:, idx, :]), x, 0.5 if kind == "wo" else 1.0, both(xT[:, idx, :]), MUL, ADD, mt_dve)
                    cp(fl8[:, 0:1], fl8[:, 1:2], ev_all)
                elif kind == "fg":
                    cp(tail_ff[:, idx, :], cb[:, s, SEQ + 1:SEQ + 11])
                    fh = cols[:, B_FS:B_FS + 4, 0:88].rearrange("p n (b r) -> p n b r", b=2)

                    def hist(j):
                        return fh[:, :, :, j * KF + idx]
                    conv(cb[:, s, :], pairA[:, s, :], FCW, lambda j: cols[:, B_FW, KF * j + idx:KF * j + idx + 1], hist,
                         cols[:, B_FW, 2 * KF + idx:2 * KF + idx + 1])
                    cp(fl8[:, 0:1], fl8[:, 1:2], ev_y)
                    dve.wait_ge(ev_t.sem, count(second_tile, m))
                    stt(pairA[:, s, :], pairB[:, s, :], 1.0, pairA[:, s, :], ADD, MUL, ev_all)
                elif kind == "fu":
                    tt(both(tmp), both(pairA[:, s, :]), x, MUL, mt_dve)
                    dve.wait_ge(ev_t.sem, count(second_tile, m))
                    tt(hl[:, idx, :], tmp, hh[:, idx, :].bitcast(F32), SUB, ev_all)

            def norm(i, src, width, gain):
                dve.wait_ge(n_rt.sem, i + 1)
                own(dve.reciprocal(lrs[:, 0:width], lrs[:, 0:width]))
                hb = memh if width == MEM else xh
                lb = meml if width == MEM else xl
                for k in range(KD + 1):
                    if k < KD:
                        stt(xT[:, k, :] if i == 4 else sqb[:, k % 2, 0:width], src[:, k, :], col(gain + k), lrs[:, 0:width],
                            MUL, MUL, n_tmp)
                    if k and i < 4:
                        dve.wait_ge(n_hi.sem, KD * i + k)
                        tt(lb[:, k - 1, :], sqb[:, (k - 1) % 2, 0:width], hb[:, k - 1, :].bitcast(F32), SUB, n_lo)

            tap_at = {}

            def tap(n):
                j, c = divmod(n, KB)
                w = cols[:, B_CW, 0:124].rearrange("p (j c) -> p j c", c=KB)[:, :, c]
                g = glu[:, c, :]
                if j == 0:
                    own(dve.tensor_scalar(oC[:, c, :], g[:, 30:30 + T], w[:, 30:31], col(V_CB + c), MUL, ADD))
                    hs = cols[:, B_CS:B_CS + NB, 0:120].rearrange("p b (j c) -> p b j c", c=KB)[:, :, :, c]
                    tt(htmp, hs, w[:, None, 0:30].to_broadcast([P, NB, 30]), MUL)
                    red(fl8, htmp, ADD)
                    tt(oC[:, c, SEQ:T], oC[:, c, SEQ:T], fl8, ADD)
                    return
                if c in tap_at:
                    dve.wait_ge(dve_c.sem, tap_at[c])
                dve_c.by(dve.scalar_tensor_tensor(out=oC[:, c, 0:SEQ], in0=g[:, j - 1:j - 1 + SEQ], scalar=w[:, j - 1:j],
                                                  in1=oC[:, c, 0:SEQ], op0=MUL, op1=ADD))
                tap_at[c] = dve_c.n

            def reduce_page(i):
                dve.wait_ge(prod_done.sem, i + 1)
                page_free.by(dve.tensor_reduce(sc[:, i, :], kring[:, i % 4, :].rearrange("p (h d) -> p h d", h=FH), AX, ADD))

            def side(K, s):
                kind, n = s[0], s[1]
                if not dve_works(s):
                    return
                if upto(pe_works, K):
                    dve.wait_ge(pe_s.sem, upto(pe_works, K))
                if upto(act_works, K):
                    dve.wait_ge(act_s.sem, upto(act_works, K))
                av = upto(to_dve, K)

                def fin():
                    cp(fl8[:, 0:1], fl8[:, 1:2], dve_s)

                if kind == "sm" and n == 1:
                    zps = s3[:, 0:80]
                    z4 = zt[:, 0:64].rearrange("p (t c) -> p t c", t=QT)
                    tt(z4, zps[:, 0:64].rearrange("p (t c) -> p t c", t=QT), spread(bias[:, 0:16], QT, 1), ADD)
                    tt(zt[0:NB, 64:80], zps[0:NB, 64:80], bias[0:NB, 0:16], ADD)
                    stt(az[:, 0:64], zt[:, 0:64], -1.0, zt[:, 0:64], MUL, MAX)
                    stt(az[0:NB, 64:80], zt[0:NB, 64:80], -1.0, zt[0:NB, 64:80], MUL, MAX, v2a)
                    dve.wait_ge(a2v.sem, av + 1)
                    for r, at, g_, b_, f_ in ((P, 0, gtok[:, :, :], btok[:, :, :], fltok[:, :, :]),
                                              (NB, 64, zsam[0:NB, 0:4], zsam[0:NB, 4:8], zsam[0:NB, 8:16])):
                        def view(x, c0, c1):
                            if r == P:
                                return x[:, 0:64].rearrange("p (t c) -> p t c", t=QT)[:, :, c0:c1]
                            return x[0:r, at + c0:at + c1]
                        ea = bias[0:r, 16:20]
                        stt(g_, view(zt, 0, 4), 0.0, view(zl, 0, 4), MAX, ADD)
                        stt(g_, g_, -1.0, spread(ea, QT, 1) if r == P else ea, MUL, MUL)
                        ts(b_, view(zb, 4, 8), 0.5, 0.5, MUL, ADD)
                        stt(f_, view(zt, 8, 16), 0.0, view(zl, 8, 16), MIN, SUB)
                    tt(exs[0:NB, :, :], spread(zsam[0:NB, :], NB, 1), spread(ident[0:NB, 0:NB], 16, 2), MUL, dve_s)
                elif kind == "sm" and n == 2:
                    cp(bsc[:, :, :], s1[:, 0:P].rearrange("p (b c) -> p b c", b=NB))
                    cp(dcol, s2[:, 0:16])
                    cp(edl, s2[:, 16:32])
                    tt(kdf, edl, dcol, SUB, v2a)
                    cp(cneg[0:FH, :], s0[0:FH, :])
                    own(dve.tensor_tensor_scan(cneg[0:FH, :], ones[0:FH, 0:1].to_broadcast([FH, SEQ]), cneg[0:FH, :], 0.0, MUL, ADD))
                    ts(cneg[0:FH, :], cneg[0:FH, :], -float(FD) ** 0.5)
                    dve.wait_ge(a2v.sem, av + 1)
                    tt(bed, edc, btok[:, :, :].rearrange("p a b -> p (a b)"), MUL, dve_s)
                elif kind == "fox":
                    if n <= FOX:
                        w = ((n - 1) % QT + 1) * P
                        red(nmx[:, 1:2], s0[:, 0:w], MAX)
                        ts(nmx[:, 0:1], nmx[:, 1:2], -FD ** -0.5, st=v2a)
                        dve.wait_ge(a2v.sem, av + 1)
                        own(dve.reciprocal(nmx[:, 1:2], rsum[:, 0:1]))
                        ts(fP[:, 0:w], fP[:, 0:w], nmx[:, 1:2])
                    if n >= 3:
                        h, q = divmod(n - 3, QT)
                        r = slice(FD * (h % 2), FD * (h % 2) + FD)
                        cp(oD[r, h // 2, q * P:(q + 1) * P], s2[r, 0:P])
                    fin()
                elif kind in ("l2", "gp"):
                    t = gx_tile(n - 1) if kind == "l2" else oB[:, n - 1, :]
                    dve.wait_ge(a2v.sem, av + 1)
                    own(dve.reciprocal(lrs, lrs))
                    if kind == "l2":
                        stt(t, t, P ** -0.5 if n <= 4 else 1.0, lrs, MUL, MUL, dve_s)
                    else:
                        stt(t, t, col(V_GN), lrs, MUL, MUL, dve_s)
                elif kind == "gdn":
                    c = s[2]
                    cc = slice(c * P, (c + 1) * P)
                    lv = lambda j: spread(cs(I_LVL + j), GH, 1)
                    b4 = lambda x: x.rearrange("p (a b) -> p a b", a=GH)
                    if n == 0:
                        if c == 0:
                            fox_stored(dve)
                            own(dve.memset(gS[:, :, :], 0.0))
                        for dst, op, in ((gQ, MAX), (gM, MIN)):
                            for h in range(GH):
                                (v2a if h == GH - 1 else dve_c).by(dve.tensor_scalar(
                                    dst[:, h, :], s2[:, h * P:(h + 1) * P], dcol[:, 4 * c + h:4 * c + h + 1], 0.0, SUB, op))
                        tt(gvb[:, :, :], b4(s1), spread(btok[:, c, :], P, 2), MUL)
                        dve.wait_ge(a2v.sem, av + 2)
                        tt(gqd[:, :, :], gqd[:, :, :], qkv[:, 8:12, cc], MUL, dve_s)
                    elif n == 1:
                        for h in range(GH):
                            stt(gN[:, h, :], s0[:, h * P:(h + 1) * P], btok[:, c, h:h + 1], gQ[:, h, :], MUL, MUL)
                        tt(gN[:, :, :], gN[:, :, :], spread(cs(I_NEGLOW), GH, 1), MUL)
                        tt(gM[:, :, :], gN[:, :, :], lv(0), MUL, dve_s)
                    elif n == 2:
                        tt(gQK[:, :, :], b4(s0), gXT[:, :, :], MUL)
                        tt(gQK[:, :, :], gQK[:, :, :], spread(cs(I_UP), GH, 1), MUL)
                        tt(gXT[:, :, :], b4(s1), spread(ident, GH, 1), ADD)
                        tt(gX[:, :, :], gM[:, :, :], spread(ident, GH, 1), ADD)
                        tt(gM[:, :, :], gN[:, :, :], lv(1), MUL, dve_s)
                    elif n <= 14:
                        l = n // 2 - 1
                        if l < LEVELS - 1:
                            dve_c.by(dve.tensor_tensor(gX[:, :, :], gX[:, :, :], b4(s2), ADD))
                            dve_c.by(dve.tensor_tensor(gM[:, :, :], gN[:, :, :], lv(l + 1), MUL))
                        tt(gXT[:, :, :], gXT[:, :, :], b4(s1), ADD, dve_s)
                    elif n == 17:
                        for h in range(GH):
                            (dve_s if h == GH - 1 else dve_c).by(dve.scalar_tensor_tensor(
                                out=gS[:, h, :], in0=gS[:, h, :], scalar=edl[:, 4 * c + h:4 * c + h + 1],
                                in1=s1[:, h * P:(h + 1) * P], op0=MUL, op1=ADD))
                elif kind == "cln":
                    if n == 0:
                        fin()
                    elif n == 1:
                        for c in range(KB):
                            stt(both(oC[:, c, :]), sd[:, 0:2, 0:TH], -1.0 / BD, both(oC[:, c, :]), MUL, ADD,
                                v2a if c == KB - 1 else dve_c)
                        fin()
                    else:
                        dve.wait_ge(a2v.sem, av + 1)
                        own(dve.reciprocal(lrs, lrs))
                        for c in range(KB):
                            tt(oC[:, c, :], oC[:, c, :], lrs, MUL)
                            ts(oC[:, c, :], oC[:, c, :], col(V_LG + c), col(V_LB + c), MUL, ADD, v2a if c == KB - 1 else dve_c)
                        for c in range(KB):
                            dve.wait_ge(a2v.sem, av + 2 + c)
                            stt(oC[:, c, :], lsq if c % 2 == 0 else lrs, 1.0, oC[:, c, :], ADD, MUL, v2a if c < 2 else dve_c)
                        fin()
                elif kind == "gs":
                    def bh(x):
                        return x.rearrange("p (b h) -> p h b", h=GH)
                    if n == 0:
                        cp(bh(kc), qkv[:, 0:4, SEQ:T])
                        cp(qkp[:, :, 0].rearrange("p (b h) -> p h b", h=GH), qkv[:, 8:12, SEQ:T])
                        cp(qkp[:, :, 1], kc)
                        cp(bh(vc), qkv[:, 4:8, SEQ:T])
                        tt(kqs, kc, qkp[:, :, 0], MUL, dve_s)
                    elif n == 2:
                        aa, bb = bsc[:, :, 0:4], bsc[:, :, 4:8]
                        b3 = lambda x: x.rearrange("p (b h) -> p b h", h=GH)
                        pr_ = s0[:, 0:64].rearrange("p (b h t) -> p b h t", h=GH, t=2)
                        tt(b3(dl), pr_[:, :, :, 1], aa, MUL)
                        tt(dl, vc, dl, SUB)
                        tt(b3(dl), b3(dl), bb, MUL)
                        tt(b3(oo), pr_[:, :, :, 0], aa, MUL)
                        tt(kqs, dl, s1[:, 0:32], MUL)
                        tt(oo, oo, kqs, ADD)
                        cp(oB[:, :, SEQ:T], bh(oo), dve_s)
                    else:
                        g = n - 3
                        if n == 3:
                            dve.wait_ge(ss_in, 16)
                            cp(drow_[0:32, :], s2[0:32, 0:P])
                            cp(krow[0:32, :], s2[0:32, P:2 * P])
                        else:
                            for h in range(GH):
                                u = 4 * (g - 1) + h
                                stt(ssam[:, u, :], ssam[:, u, :], bsc[:, g - 1, h:h + 1], s0[:, h * P:(h + 1) * P], MUL, ADD)
                        if g < NB:
                            tt(blk[0:32, :, :], spread(drow_[0:32, :], 4, 1), spread(ident[0:32, 4 * g:4 * g + 4], P, 2), MUL)
                        fin()
                elif kind == "dc":
                    if n == 0:
                        dve.wait_ge(lf_in, 16)
                        red(tot, lf[:, :, :].rearrange("p t h -> p h t"), ADD)
                        tt(totm[:, :, :], spread(tot, NB, 1), spread(cst[:, N_CST * P:N_CST * P + NB], FH, 2), MUL, dve_s)
                    elif n == 1:
                        cp(offs, s0[:, 0:FH])
                        for h in range(FH):
                            own(dve.tensor_tensor_scan(cpg[:, h, :], ones, lf[:, :, h], offs[:, h:h + 1], MUL, ADD))
                        tt(cq[:, :, :], s1[:, 0:64].rearrange("p (b h) -> p b h", b=NB), bsc[:, :, 8:16], ADD, dve_s)
                    else:
                        for j in range(2):
                            o = sc[:, :, 4 * j:4 * j + 4].rearrange("p i h -> p h i")
                            stt(o, o, FD ** -0.5, sd[:, 2 + j, :].rearrange("p (h i) -> p h i", h=4), MUL, SUB)
                        o = sc[:, :, :].rearrange("p (b j) h -> p b j h", b=NB)
                        tt(o, o, cq[:, :, None, :].to_broadcast([P, NB, PAGES, FH]), ADD, dve_s)
                elif kind == "ds":
                    s4 = sc[:, :, :].rearrange("p (b j) h -> p b j h", b=NB)
                    if n == 0:
                        red(mx64[:, :, :], s4.rearrange("p b j h -> p b h j"), MAX)
                        tt(qk32[:, :, :], fs[:, 0:4, :], fs[:, 4:8, :], MUL, dve_s)
                    elif n == 1:
                        red(m1[0:64, :], s0[0:64, 0:P], MAX)
                        ts(dg64[0:64, :], ident[0:64, 0:64], m1[0:64, 0:1], st=dve_c)
                        for j in range(2):
                            ts(pn[:, :, :].rearrange("p b (c t) -> p b c t", t=2)[:, :, :, j],
                               s1[:, 32 * j:32 * j + 32].rearrange("p (c b) -> p b c", c=4), FD ** -0.5,
                               st=dve_s if j else dve_c)
                    elif n == 2:
                        tt(mb[:, :, :], s2[:, 0:64].rearrange("p (b h) -> p b h", b=NB), pn[:, :, :], MAX)
                        tt(pn[:, :, :], pn[:, :, :], mb[:, :, :], SUB)
                        tt(s4, s4, mb[:, :, None, :].to_broadcast([P, NB, PAGES, FH]), SUB, v2a)
                        dve.wait_ge(a2v.sem, av + 1)
                        red(rs64[:, :, :], s4.rearrange("p b j h -> p b h j"), ADD, dve_s)
                    else:
                        tt(rd64[:, :, :], s3[:, 0:64].rearrange("p (b h) -> p b h", b=NB), pn[:, :, :], ADD)
                        own(dve.reciprocal(rd64[:, :, :], rd64[:, :, :]), dve_s)
                elif kind == "df":
                    dve.wait_ge(v_used.sem, NB * PAGES)
                    for j in range(2):
                        r = slice(FD * j, FD * j + FD)
                        o = oD[r, :, SEQ:T]
                        p4 = lambda x: x[r, :, :].rearrange("p b (c t) -> p c b t", t=2)[:, :, :, j]
                        tt(o, fs[r, 8:12, :], p4(pn), MUL)
                        tt(o, o, s3[r, 0:64].rearrange("p (b c t) -> p c b t", b=NB, t=2)[:, :, :, j], ADD)
                        tt(o, o, p4(rd64), MUL)
                    fin()
                elif kind == "ml":
                    for j in range(4):
                        cp(memT[:, 2 * j:2 * j + 2, :], sd[:, j, :].rearrange("p (k m) -> p k m", k=2), dve_s if j == 3 else dve_c)
                elif kind == "x":
                    if n <= XU:
                        red(nmx[:, 1:2], s0[:, 0:MEM], MAX)
                        ts(nmx[:, 0:1], nmx[:, 1:2], -P ** -0.5, st=v2a)
                        dve.wait_ge(a2v.sem, av + 1)
                        own(dve.reciprocal(nmx[:, 1:2], rsum[:, 0:1]))
                        ts(xP, xP, nmx[:, 1:2])
                    if 2 <= n <= NB + 1:
                        b = n - 2
                        if b == 0:
                            dve.wait_ge(mk_in, 16)
                        tt(kvc[:, b, :, :], kvc[:, b, :, :], spread(s3, 2, 1), MUL)
                        red(xsc[:, b, :, :], kvc[:, b, :, :].rearrange("p t (h d) -> p t h d", h=XH), ADD)
                    if n >= 3:
                        h, q = divmod(n - 3, QT)
                        cp(oX[:, h, q * P:(q + 1) * P], s2[:, 0:P])
                    fin()
                elif kind == "xd":
                    x4_ = xsc[:, :, :, :]
                    if n == 0:
                        red(xmx[:, :, :], x4_.rearrange("p b t h -> p b h t"), MAX, dve_s)
                    elif n == 1:
                        red(xm1[0:32, :], s0[0:32, 0:P], MAX)
                        ts(xdg[0:32, :], ident[0:32, 0:32], xm1[0:32, 0:1], st=dve_s)
                    elif n == 2:
                        tt(x4_, x4_, s1[:, 0:32].rearrange("p (b h) -> p b h", b=NB)[:, :, None, :].to_broadcast([P, NB, 2, XH]), SUB, v2a)
                        dve.wait_ge(a2v.sem, av + 1)
                        red(xrs[:, :, :], x4_.rearrange("p b t h -> p b h t"), ADD, dve_s)
                    else:
                        own(dve.reciprocal(xrd[:, :, :].rearrange("p b h -> p (b h)"), s2[:, 0:32]))
                        tt(oX[:, :, SEQ:T], s3[:, 0:32].rearrange("p (b h) -> p h b", b=NB), xrd[:, :, :].rearrange("p b h -> p h b"), MUL, dve_s)

            dve.wait_ge(pool_made.sem, 6)
            for j in range(5):
                dve.wait_ge(pro_pe.sem, j + 1)
                n = min(4, N_BLK - 4 * j)
                cp(cols[:, 4 * j:4 * j + n, :], sd[:, j % 4, 0:n * P].rearrange("p (n m) -> p n m", n=n), pro_dve)
            for j in range(9):
                dve.wait_ge(pro_pe.sem, 6 + j)
                o = sd[:, (5 + j) % 4, :]
                if j < KD:
                    cp(xT[:, j, 0:SEQ], o, pro_dve)
                else:
                    cp(xT[:, :, SEQ:T], o[:, 0:KD * NB].rearrange("p (k b) -> p k b", k=KD), pro_dve)
            ts(cols[:, B_VEC, V_GW:V_GW + 48], cols[:, B_VEC, V_GW:V_GW + 48], 0.5)
            ts(cols[:, B_VEC, V_LG:V_LG + 8], cols[:, B_VEC, V_LG:V_LG + 8], 0.5)
            ts(cols[:, B_FW, 0:66], cols[:, B_FW, 0:66], 0.5)
            done, spl = [0], [0]
            for e in TIMELINE:
                if e[0] == "norm":
                    i = ["mix", "mem", "cross", "ffn", "fin"].index(e[1])
                    norm(i, memT if i == 1 else xT, MEM if i == 1 else T, [V_MIX, V_MEM, V_CROSS, V_FFN, V_FIN][i])
                elif e[0] == "flush" or (e[0] == "piece" and e[2] == 0):
                    p = e[1] if e[0] == "piece" else None
                    while done[0] < len(MT_LAST) and (MT_LAST[done[0]] < (p if p is not None else cur + 1)):
                        if dve_tile[done[0]]:
                            evac(done[0])
                        done[0] += 1
                    if p is not None:
                        cur = p
                elif e[0] == "piece":
                    cur = e[1]
                elif e[0] == "split":
                    src, n = {"brC": (oC, 4), "brB": (oB, 4), "brD": (oD, 4), "brX": (oX, 4), "merged": (xT, 8)}[e[1]]
                    for k in range(n):
                        dve.wait_ge(sp_hi.sem, spl[0] + 1)
                        tt((xl if n == 8 else ol)[:, k, :], src[:, k, :], (xh if n == 8 else oh)[:, k, :].bitcast(F32), SUB, sp_lo)
                        spl[0] += 1
                elif e[0] == "side":
                    side(e[1], e[2])
                elif e[0] == "tap":
                    tap(e[1])
                elif e[0] == "k" and e[1] > 0:
                    reduce_page(e[1] - 1)
                elif e[0] == "kend":
                    reduce_page(N_PAGE - 1)


_INS = ["x_prompt", "x_sample", "cache_fox_k", "cache_fox_v", "cache_fox_logf", "cache_mem_k", "cache_mem_v",
        "state_sconv", "state_gdn_conv", "state_gdn", "state_conf_conv", "state_ffn_conv", "page_table", "mem_prompt",
        "norm_mix", "w_in", "w_branch", "w_out", "sconv_w", "gdn_conv_w", "gdn_a_log", "gdn_dt_bias", "gdn_norm",
        "conf_dw_w", "conf_dw_b", "conf_ln_g", "conf_ln_b", "fox_fbias", "norm_cross", "norm_mem", "w_cq", "w_ckv", "w_co",
        "norm_ffn", "w_ffn_in", "ffn_conv_w", "w_ffn_out", "norm_final"]
_OUTS = [("y_p", (1, SEQ, D)), ("y_s", (NB, 1, D)),
         ("fk_p", (1, SEQ, 1, FH, FD)), ("fv_p", (1, SEQ, 1, FH, FD)), ("fl_p", (1, SEQ, 1, FH)),
         ("mk_p", (1, 1, MEM, XH, P)), ("mv_p", (1, 1, MEM, XH, P)),
         ("sc_p", (1, 1, SCW - 1, BD)), ("gc_p", (1, 1, GCW - 1, 3 * BD)), ("S_p", (1, 1, GH, P, P)),
         ("cf_p", (1, 1, CFW - 1, BD)), ("ff_p", (1, 1, FCW - 1, FF)),
         ("fk_s", (NB, 1, 1, FH, FD)), ("fv_s", (NB, 1, 1, FH, FD)), ("fl_s", (NB, 1, 1, FH)),
         ("sc_s", (NB, 1, SCW - 1, BD)), ("gc_s", (NB, 1, GCW - 1, 3 * BD)), ("S_s", (NB, 1, GH, P, P)),
         ("cf_s", (NB, 1, CFW - 1, BD)), ("ff_s", (NB, 1, FCW - 1, FF))]


def kernel(**inputs):
    import concourse.bacc as bacc
    from concourse.bass_utils import run_bass_kernel_spmd

    nc = bacc.Bacc("TRN2", target_bir_lowering=False, num_devices=1, dynamic_dma_scratch_size=1024)
    arrays, a, out = {}, {}, {}
    for name in _INS:
        x = np.ascontiguousarray(inputs[name])
        arrays[f"in_{name}"] = x
        a[name] = nc.dram_tensor(f"in_{name}", x.shape, mybir.dt.from_np(x.dtype), kind="ExternalInput").ap()
    r = np.arange(P)[:, None]
    arrays["in_cst"] = np.concatenate([constants(), (r // PAGES == np.arange(NB)[None]).astype(np.float32)], axis=1)
    a["cst"] = nc.dram_tensor("in_cst", arrays["in_cst"].shape, F32, kind="ExternalInput").ap()
    for name, shape in _OUTS:
        out[name] = nc.dram_tensor(f"out_{name}", shape, F32, kind="ExternalOutput").ap()
    build(nc, a, out)
    res = run_bass_kernel_spmd(nc, [arrays], core_ids=[0])
    return tuple(res.results[0][f"out_{name}"] for name, _ in _OUTS)
```

```python
from contextlib import ExitStack

import numpy as np

import concourse.bass as bass
from concourse import mybir

F32 = mybir.dt.float32
F32R = mybir.dt.float32r
I32 = mybir.dt.int32
ALU = mybir.AluOpType
ACT = mybir.ActivationFunctionType
AX = mybir.AxisListType.X
MUL, ADD, SUB, MAX, MIN = ALU.mult, ALU.add, ALU.subtract, ALU.max, ALU.min

P = 128
D = 1024
KD = D // P
SEQ, NB = 512, 8
T = SEQ + NB
TH = T // 2
QT = SEQ // P
BD = 512
KB = BD // P
SCW, GCW, CFW, FCW = 3, 4, 31, 3
GH = 4
FH, FD = 8, 64
XH = 4
MEM = 256
FF = 2816
KF = FF // P
PAGES = 16
NEG = -1e30
LEVELS = 7

C_AH, C_AB, C_AC, C_GQ = 0, BD, 2 * BD, 3 * BD
C_GZ = 6 * BD
C_GA = 7 * BD
C_CV = C_GA + 2 * GH
C_CG = C_CV + BD
C_FQ = C_CG + BD
C_FF = C_FQ + 3 * BD
C_GATE = C_FF + FH
N_IN = C_GATE + 4 * D

(I_ID, I_ONE, I_UP, I_NEGLOW, I_CAUSAL, I_LO, I_HI, I_PAGE, I_LVL) = range(9)
N_CST = I_LVL + LEVELS

V_MIX, V_CROSS, V_FFN, V_FIN, V_MEM, V_CB, V_LG, V_LB, V_GN, V_SW, V_GW = 0, 8, 16, 24, 32, 40, 44, 48, 52, 53, 65
B_VEC, B_CW, B_FW, B_SS, B_GS, B_CS, B_FS = 0, 1, 2, 3, 4, 8, 16
N_BLK = 20


def constants():
    r, c = np.arange(P)[:, None], np.arange(P)[None, :]
    out = np.zeros((P, N_CST, P), np.float32)
    out[:, I_ID] = r == c
    out[:, I_ONE] = 1.0
    out[:, I_UP] = r <= c
    out[:, I_NEGLOW] = -(r > c).astype(np.float32)
    out[:, I_CAUSAL] = np.where(c > r, np.float32(NEG), np.float32(0))
    out[:, I_LO] = r < FD
    out[:, I_HI] = r >= FD
    out[:, I_PAGE] = (r // PAGES == c // PAGES) & (r < c)
    for n in range(LEVELS):
        s = 1 << n
        out[:, I_LVL + n] = (r // (2 * s) == c // (2 * s)) & ((r // s) % 2 == 1) & ((c // s) % 2 == 0)
    return out.reshape(P, N_CST * P)


def plan():
    units, pieces = [], []

    def unit(w, row, kt, col, kind, idx, first=True, last=True):
        units.append((w, row, kt, col))
        for h in range(2):
            pieces.append((len(units) - 1, h, kt, kind, idx + h, first, last))

    for n, kind in enumerate(("fq", "fk", "fv")):
        for h in range(2):
            unit("w_in", 0, KD, C_FQ + n * BD + h * 256, kind, 2 * h)
    for h in range(2):
        unit("w_in", 0, KD, C_CV + h * 256, "cv", 2 * h)
        unit("w_in", 0, KD, C_CG + h * 256, "cg", 2 * h)
    for h in range(2):
        unit("w_in", 0, KD, C_AC + h * 256, "ac", 2 * h)
        unit("w_in", 0, KD, C_AH + h * 256, "ah", 2 * h)
        unit("w_in", 0, KD, C_AB + h * 256, "ab", 2 * h)
    for n in range(6):
        unit("w_in", 0, KD, C_GQ + n * 256, "gx", 2 * n)
    for n, br in enumerate("ACDB"):
        if br == "B":
            for h in range(2):
                unit("w_in", 0, KD, C_GZ + h * 256, "gz", 2 * h)
        b = "ABCD".index(br)
        for h in range(4):
            unit("w_in", 0, KD, C_GATE + b * D + h * 256, "gate" + br, 2 * h)
            unit("w_branch", b * BD, KB, h * 256, "br" + br, 2 * h)
    for h in range(4):
        unit("w_out", 0, KD, h * 256, "wo", 2 * h)
    for h in range(4):
        unit("w_ckv", 0, KD, h * 256, "kv", 2 * h)
    for h in range(2):
        unit("w_cq", 0, KD, h * 256, "cq", 2 * h)
    for h in range(4):
        unit("w_co", 0, KB, h * 256, "co", 2 * h)
    for h in range(KF // 2):
        unit("w_ffn_in", 0, KD, h * 256, "fg", 2 * h)
        unit("w_ffn_in", 0, KD, FF + h * 256, "fu", 2 * h)
    for h in range(4):
        for k in range(0, KF, KD):
            unit("w_ffn_out", k * P, min(KD, KF - k), h * 256, "fo", 2 * h, k == 0, k + KD >= KF)
    return units, pieces


UNITS, PIECES = plan()
NP_ = len(PIECES)
PIECE_MT = []
MT_LAST = []
for _p, (_u, _h, _k, _kind, _idx, _first, _last) in enumerate(PIECES):
    if _first:
        PIECE_MT.append(len(MT_LAST))
        MT_LAST.append(_p)
    else:
        PIECE_MT.append(PIECE_MT[_p - 2])
        MT_LAST[PIECE_MT[_p]] = _p
BY_ACT = {"fq", "fk", "fv", "cv", "cg", "gx", "ac", "gateA", "gateB", "gateC", "gateD", "gz", "kv", "cq", "fg"}
MT_KIND = [PIECES[p][3] for p in MT_LAST]
MT_ACT = [k in BY_ACT for k in MT_KIND]


def first_piece(kind):
    return min(p for p, x in enumerate(PIECES) if x[3] == kind)


def last_piece(kind):
    return max(p for p, x in enumerate(PIECES) if x[3] == kind)


GROUPS = 32
FOX = 4 * FH
XU = QT * XH // 2
TAPS_TICK, K_TICK = 2, 3
V_FILLED, V_BARE = 2, 2
SIDE = ([("AFTER", "fq")] + [("sm", n) for n in range(4)]
        + [("AFTER", "fv")]
        + [("fst", n) for n in range(4)] + [("KSTART",)]
        + [("fvt", n) for n in range(5)] + [("fkt", n) for n in range(5)]
        + [("fox", n) for n in range(FOX + 3)]
        + [x for n in range(8) for x in (("AFTER", "gx", n), ("l2", n))] + [("l2", 8)]
        + [("AFTER", "gx")]
        + [("gs", n) for n in range(13)]
        + [("TAPS",)]
        + [("cln", n) for n in range(6)] + [("BEFORE", "gateC")]
        + [("gdn", n, 0) for n in range(-1, 18)]
        + [("REDUCES",)]
        + [("dc", n) for n in range(3)] + [("ds", n) for n in range(4)] + [("VSTART",)]
        + [("gdn", n, c) for c in range(1, 4) for n in range(-1, 18)]
        + [("PAGES",), ("df", 0), ("df", 1)] + [("BEFORE", "gateD")]
        + [("gp", n) for n in range(5)] + [("BEFORE", "gz")]
        + [("ex", n) for n in range(6)] + [("ml", n) for n in range(3)] + [("BEFORE", "wo")]
        + [("AFTER", "cq")]
        + [("xm", n) for n in range(3)] + [("x", n) for n in range(XU + 3)] + [("xd", n) for n in range(4)]
        + [("BEFORE", "co")]
        + [("AFTER", "fu")] + [("ef", n) for n in range(7)]
        + [("BEFORE", "END")] + [("y", n) for n in range(11)])


MARKS = ("AFTER", "BEFORE", "TAPS", "REDUCES", "KSTART", "VSTART", "PAGES")
N_TAP = KB * CFW
N_PAGE = PAGES * NB


def timeline():
    out, pos, step_n, tile, at_piece, bg = [], [0], [0], [0], [-1], {"tap": None, "k": None, "v": None}
    size = {"tap": N_TAP, "k": N_PAGE, "v": N_PAGE}

    def background(kind, n):
        for _ in range(n):
            if bg[kind] is not None and bg[kind] < size[kind]:
                if kind == "v" and bg[kind] % PAGES == 0 and _ > 0 and n < 10:
                    return
                out.append((kind, bg[kind]))
                bg[kind] += 1

    def step(done, filled=True):
        while pos[0] < len(SIDE):
            s = SIDE[pos[0]]
            if s[0] == "AFTER":
                if done <= (last_piece(s[1]) if len(s) == 2 else first_piece(s[1]) + s[2]) + 1:
                    return
            elif s[0] in ("TAPS", "REDUCES", "PAGES"):
                background({"TAPS": "tap", "REDUCES": "k", "PAGES": "v"}[s[0]], 10 ** 6)
                if s[0] == "REDUCES":
                    out.append(("kend",))
            elif s[0] == "KSTART":
                bg["k"] = 0
                out.append(("kstart",))
            elif s[0] == "VSTART":
                bg["v"] = 0
                out.append(("vstart",))
            elif s[0] != "BEFORE":
                background("v", V_FILLED if filled else V_BARE)
                out.append(("side", step_n[0], s))
                step_n[0] += 1
                pos[0] += 1
                return
            elif s[1] == "END":
                return
            pos[0] += 1

    def evac(upto_piece):
        while tile[0] < len(MT_LAST) and MT_LAST[tile[0]] <= upto_piece:
            out.append(("evac", tile[0]))
            out.append(("evac2", tile[0]))
            tile[0] += 1

    def through(mark):
        at = SIDE.index(mark)
        if pos[0] <= at and any(s[0] == "AFTER" for s in SIDE[pos[0]:at]):
            evac(at_piece[0])
        while pos[0] < at and any(s[0] not in ("AFTER", "BEFORE") for s in SIDE[pos[0]:at]):
            step(10 ** 6, False)

    def norm(i, to=KD + 1):
        out.append(("nsum", i))
        out.extend(("napply", i, k) for k in range(to))

    norm(0)
    for p in range(NP_):
        kind = PIECES[p][3]
        if p == first_piece(kind) and ("BEFORE", kind) in SIDE:
            through(("BEFORE", kind))
        if kind in ("wo", "kv", "co", "fg", "fo") and p == first_piece(kind):
            evac(p - 1)
        if p == first_piece("wo"):
            out.append(("split", "merged"))
        if p == first_piece("wo") + 2:
            norm(1)
        if p == first_piece("kv"):
            out.append(("nsum", 2))
        if p == first_piece("co"):
            out.append(("split", "brX"))
        if p == first_piece("fg"):
            norm(3)
        if bg["tap"] is None and p > last_piece("cg") + 1:
            bg["tap"] = 0
        for h in range(2):
            at_piece[0] = p - 1 + h
            out.append(("piece", p, h))
            if kind in ("gateC", "gateB", "gateD") and p == first_piece(kind) and h == 0:
                evac(p - 1)
                out.append(("split", "br" + kind[-1]))
            step(p)
            if h == 0:
                evac(p - 1)
            if kind == "kv" and h == 1:
                out.append(("napply", 2, p - first_piece("kv")))
                if p == last_piece("kv"):
                    out.append(("napply", 2, KD))
            background("tap", TAPS_TICK)
            background("k", 1 + h if K_TICK == 3 else 1)
    evac(NP_ - 1)
    through(("BEFORE", "END"))
    pos[0] = SIDE.index(("BEFORE", "END")) + 1
    norm(4, KD)
    for n in range(pos[0], len(SIDE)):
        step(10 ** 6)
    return out


TIMELINE = timeline()
ITEMS = [e[2] for e in TIMELINE if e[0] == "side"]
assert len(ITEMS) == len([s for s in SIDE if s[0] not in MARKS])
assert [e[1] for e in TIMELINE if e[0] == "k"] == list(range(N_PAGE))
assert [e[1] for e in TIMELINE if e[0] == "v"] == list(range(N_PAGE))
assert TIMELINE.index(("tap", N_TAP - 1)) < TIMELINE.index(("piece", first_piece("brA") + 6, 0))


def pe_works(s):
    kind, n = s[0], s[1]
    return n < {"sm": 3, "fst": 3, "fvt": 4, "fkt": 4, "fox": FOX + 2, "l2": 8, "gdn": 17, "cln": 5, "gp": 4, "dc": 2,
                "ds": 3, "df": 1, "ex": 5, "xm": 2, "x": XU + 2, "xd": 3, "ef": 6, "y": 10,
                "gs": 11, "ml": 2}[kind] and not (kind in ("gs", "ml") and n == 0)


def act_works(s):
    kind, n = s[0], s[1]
    if kind in ("sm", "fst", "fvt", "fkt", "ex", "ef", "y", "fox"):
        return n > 0
    if kind == "gdn":
        return n == 0 or n >= 3 and n % 2 == 1 or n == 16
    if kind == "ds":
        return n == 2
    if kind == "x":
        return n > 0 and n < XU + 2
    if kind == "xm":
        return n > 0
    if kind == "xd":
        return n == 2
    if kind == "cln":
        return n > 0
    return kind in ("l2", "gp")


def dve_works(s):
    kind, n = s[0], s[1]
    if kind == "gdn":
        return n in (0, 1, 17) or n <= 14 and n >= 2 and n % 2 == 0
    if kind in ("fox", "l2", "gp", "x"):
        return n > 0
    if kind == "sm":
        return n > 1
    if kind == "df":
        return n == 1
    if kind == "gs":
        return n < 12 and n != 1
    if kind == "cln":
        return n in (0, 1, 5)
    if kind == "ml":
        return n == 2
    return kind in ("dc", "ds", "df", "xd")


def to_act(s):
    kind, n = s[0], s[1]
    if kind == "fox":
        return int(1 <= n <= FOX)
    if kind == "x":
        return int(1 <= n <= XU)
    return {("sm", 2): 1, ("sm", 3): 1, ("gdn", 0): 2, ("cln", 1): 1, ("cln", 5): 3, ("ds", 2): 1, ("xd", 2): 1}.get((kind, n), 0)


def to_dve(s):
    kind, n = s[0], s[1]
    if kind == "fox":
        return int(1 <= n <= FOX)
    if kind == "x":
        return int(1 <= n <= XU)
    if kind == "l2" or kind == "gp":
        return int(n > 0)
    return {("sm", 2): 1, ("sm", 3): 1, ("gdn", 0): 2, ("cln", 5): 5, ("ds", 2): 1, ("xd", 2): 1}.get((kind, n), 0)


def upto(what, k):
    return sum(int(what(s)) for s in ITEMS[:k])


class Stage:

    def __init__(self, sem):
        self.sem, self.n = sem, 0

    def by(self, ins):
        ins.then_inc(self.sem, 1)
        self.n += 1


def build(nc, a, out):
    ctx = ExitStack()
    with ctx:
        def sb(name, shape, dt=F32):
            return ctx.enter_context(nc.sbuf_tensor(name, shape, dt))

        def ps(name, shape):
            return ctx.enter_context(nc.psum_tensor(name, shape, F32))

        def sem(name):
            return ctx.enter_context(nc.semaphore(name))

        def stage(name):
            return Stage(sem(name))

        cst = sb("cst", [P, N_CST * P + NB])
        cols = sb("cols", [P, N_BLK, P])
        xT = sb("xT", [P, KD, T])
        xh_at = -(-nc.sbuf_base // 32) * 32
        xh, xl = sb("xh", [P, KD, T], F32R), sb("xl", [P, KD, T], F32R)
        oh, ol = sb("oh", [P, KB, T], F32R), sb("ol", [P, KB, T], F32R)
        raw = sb("raw", [P, 2, KD, 256])
        wh, wl = sb("wh", [P, 2, KD, P], F32R), sb("wl", [P, 2, KD, P], F32R)
        OD, OB, OC, QKV, G, DEC = 0, 2080, 4160, 6240, 12480, 18624
        DEC_N = 4 * 512 + 512 + PAGES * NB * FH
        SQ = DEC + DEC_N
        PR = SQ + 2 * T
        SM = PR + 4 * T + 2 * 524 + T
        ptr_, ptc = sb("ptr", [1, PAGES * NB], I32), sb("ptc", [P, 1], I32)
        base = -(-nc.sbuf_base // 32) * 32
        ar = sb("ar", [P, SM + 694])

        def v(at, *shape):
            n = int(np.prod(shape))
            x = ar[:, at:at + n]
            if len(shape) == 2:
                x = x.rearrange("p (a b) -> p a b", a=shape[0])
            if len(shape) == 3:
                x = x.rearrange("p (a b c) -> p a b c", a=shape[0], b=shape[1])
            return x

        oD, oB, oC = v(OD, KB, T), v(OB, KB, T), v(OC, KB, T)
        qkv = v(QKV, 12, T)
        fq, fk, fv = qkv[:, 0:4, :], qkv[:, 4:8, :], qkv[:, 8:12, :]

        def gx_tile(n):
            return qkv[:, (8 + n) % 12, :]

        kring = v(DEC, 4, 512)
        qb = v(DEC + 2048, 512)
        sc = v(DEC + 2560, PAGES * NB, FH)
        lsq, lrs = v(SQ, T), v(SQ + T, T)
        pairA, pairB = v(PR, 2, T), v(PR + 2 * T, 2, T)
        cb = v(PR + 4 * T, 2, 524)
        tmp = v(PR + 4 * T + 1048, T)
        sm_at = [SM]

        def small(n, *shape):
            at = sm_at[0]
            sm_at[0] += n
            assert sm_at[0] <= SM + 694
            return v(at, *(shape or (n,)))

        glu = xT[:, :, :].rearrange("p a b -> p (a b)")[:, KD * T - 4 * 550:].rearrange("p (a b) -> p a b", a=4)
        tail_gx, tail_cf = small(132, 12, 11), small(152, 4, 38)
        tail_sc = cols[:, B_SS, 64:104].rearrange("p (a b) -> p a b", a=KB)
        fs = small(96, 12, 8)
        gtok, btok = small(16, 4, 4), small(16, 4, 4)
        fltok = small(32, 4, 8)
        zsam = small(16)
        bsc = small(128, 8, 16)
        bias = small(20)
        eps6, eps5 = small(1), small(1)
        dcol, edc, edl, kdf, bed = (small(16) for _ in range(5))
        nmx, rsum = small(2), small(2)
        fl8 = cols[:, B_SS, 104:112]
        htmp = v(PR + 4 * T + 1048, NB, 30)

        ident, ones = cst[:, 0:P], cst[:, P:2 * P]

        def cs(n):
            return cst[:, n * P:(n + 1) * P]

        def col(n):
            return cols[:, B_VEC, n:n + 1]

        pb = ps("pb", [P, 2, 2, 512])
        sd = ps("sd", [P, 4, 512])
        s0, s1, s2, s3 = (sd[:, n, :] for n in range(4))

        xscr = nc.dram_tensor("x_scratch", (P, KD * T), F32, kind="Internal").ap()
        vscr = nc.dram_tensor("v_scratch", (NB * FH * (512 + FD),), F32, kind="Internal").ap()
        qscr = nc.dram_tensor("q_scratch", (NB, 512), F32, kind="Internal").ap()

        id_in = sem("id_in")
        par_in, x_in, small_in, mem_in, lf_in, pt_in = (sem(n) for n in (
            "par_in", "x_in", "small_in", "mem_in", "lf_in", "pt_in"))
        raw_in = [sem(f"raw_in{n}") for n in range(2)]
        page_in = [sem(f"page_in{n}") for n in range(4)]
        qb_in, xs_out, xs_in, qs_out = sem("qb_in"), sem("xs_out"), sem("xs_in"), sem("qs_out")
        out_sem = sem("out_sem")
        stg_out = [sem(f"stg_out{n}") for n in range(2)]
        ss_in, ss_out, mv_in = sem("ss_in"), sem("ss_out"), [sem(f"mv_in{n}") for n in range(2)]
        pool_c, act_c, dve_c = stage("pool_chain"), stage("act_chain"), stage("dve_chain")
        pool_made = stage("pool_made")
        hi, lo = stage("hi_ready"), stage("lo_ready")
        piece_done, mt_act, mt_dve = stage("piece_done"), stage("mt_act"), stage("mt_dve")
        ev_y, ev_t, ev_all = stage("conv_ready"), stage("act_second"), stage("dve_tile_done")
        pe_s, act_s, dve_s = stage("pe_side"), stage("act_side"), stage("dve_side")
        v2a, a2v = stage("dve_to_act"), stage("act_to_dve")
        prod_done, page_free, v_used = stage("prod_done"), stage("page_free"), stage("v_used")
        n_sq, n_pe, n_rt, n_tmp, n_hi = (stage(n) for n in ("norm_sq", "norm_pe", "norm_root", "norm_tmp", "norm_hi"))
        n_lo, sp_hi, sp_lo = stage("norm_lo"), stage("split_hi"), stage("split_lo")
        wsm_hi, wsm_lo, v_rows = stage("gate_weights_hi"), stage("gate_weights_lo"), stage("v_rows")
        vs_out, v64_in = [sem(f"vs_out{n}") for n in range(2)], sem("v64_in")
        kprod, kred, q8_in = stage("k_times_q"), stage("k_reduced"), sem("q8_in")
        pro_pe, pro_dve = stage("pro_pe"), stage("pro_dve")
        ss_st, vt_out, gs_out, mk_in = sem("row_stores"), sem("vt_out"), sem("gs_out"), sem("mk_in")
        side_at, out_total = [0], [16 * 8]
        mt_a = [sum(MT_ACT[:m + 1]) for m in range(len(MT_ACT))]
        mt_d = [m + 1 - mt_a[m] for m in range(len(MT_ACT))]
        dve_tile = [k in ("cg", "gx", "ac", "ah", "ab", "gz", "wo", "co", "fg", "fu", "fo") and k != "ac" or k.startswith("br")
                    for k in MT_KIND]
        conv_tile = [k in ("gx", "fg") for k in MT_KIND]
        second_tile = [k in ("gx", "fg", "ab", "fu") for k in MT_KIND]

        def count(flags, m):
            return sum(int(x) for x in flags[:m + 1])

        def mt_of(kind, idx=None):
            return max(m for m, k in enumerate(MT_KIND) if k == kind and (idx is None or PIECES[MT_LAST[m]][4] == idx))

        def n_of(flags, m):
            return sum(int(x) for x in flags[:m])

        pv = v(QKV, N_BLK, P)
        xrow = v(0, 5, D)
        wsm = v(G, KD, 16)
        wsh = nc.alloc_sbuf_tensor_at("wsh", [P, KD, 16], F32R, offset=base + 4 * (G + 128))
        wsl = nc.alloc_sbuf_tensor_at("wsl", [P, KD, 16], F32R, offset=base + 4 * (G + 256))
        zrow = v(G + 1024, T)
        vt = v(G, QT, 512)
        fP, fPT = v(G + 2048, 512), v(G + 2560, QT, P)
        stg = v(G + 4096, 2, 512)
        cneg, srow = v(G + 5120, 512), v(G + 3072, 2, 512)
        gR, gkd, gvb, gQK, gqd, gN, gX, gXT, gQ, gM, gW, gS = (v(G + 512 * n, GH, P) for n in range(12))
        ssam = v(G, NB * GH, P)
        g2 = G + 4096
        kc, qkp, vc, kqs, dl, oo = (v(g2, 32), v(g2 + 32, 32, 2), v(g2 + 96, 32), v(g2 + 128, 32), v(g2 + 160, 32), v(g2 + 192, 32))
        krow, drow_, blk = v(g2 + 256, P), v(g2 + 384, P), v(g2 + 512, 4, P)
        lf, cpg = v(DEC, P, FH), v(DEC + 1024, FH, P)
        g3 = DEC + 2048
        tot, totm, offs, cq = v(g3, 8), v(g3 + 8, NB, FH), v(g3 + 72, 8), v(g3 + 80, NB, FH)
        qk32, m1, pn, rd64 = v(g3 + 144, 4, NB), v(g3 + 176, 1), v(g3 + 192, NB, FH), v(g3 + 256, NB, FH)
        vrow, v64 = v(SQ, 2, 512), v(g3, 2, FD)
        mx64, mb, rs64, dg64 = v(g3 + 320, NB, FH), v(g3 + 384, NB, FH), v(g3 + 448, NB, FH), v(SQ, 64)
        mkT, mvT, mv = v(0, XH, MEM), v(1024, XH, MEM), v(2048, 2, 512)
        qc, oX = v(3072, XH, T), v(5152, XH, T)
        memT, mrow = v(7744, KD, MEM), v(9792, 2, D)
        xP, xPT = v(7744, 2, MEM), v(8256, 4, P)
        kvc = v(11840, NB, 2, 512)
        xstg, qrow = v(20032, 2, 512), v(21056, 512)
        xsc = v(21568, NB, 2, XH)
        x4 = 21632
        xmx, xm1, xdg, xrs, xrd = v(x4, NB, XH), v(x4 + 32, 1), v(x4 + 64, 32), v(x4 + 96, NB, XH), v(x4 + 128, NB, XH)
        xnm, xsum = v(x4 + 160, 4), v(x4 + 164, 2)
        mstg = v(PR + 4 * T, 2, 512)
        qx = nc.alloc_sbuf_tensor_at("qx", [P, NB, 512], F32, offset=xh_at)
        tail_ff = v(SM, KF, 10)
        hh = nc.alloc_sbuf_tensor_at("hh", [P, KF, T], F32R, offset=base)
        hl = nc.alloc_sbuf_tensor_at("hl", [P, KF, T], F32R, offset=base + 4 * T * KF)

        def sel(h):
            return ident[0:NB, h:h + 1].to_broadcast([NB, P])

        sqb = pairA
        memh = oh[:, :, :].rearrange("p a b -> p (a b)")[:, 0:KD * MEM].rearrange("p (a b) -> p a b", a=KD)
        meml = ol[:, :, :].rearrange("p a b -> p (a b)")[:, 0:KD * MEM].rearrange("p (a b) -> p a b", a=KD)
        zt, az, zl, zb, exs = v(SQ, 80), v(SQ + 80, 80), v(SQ + 160, 80), v(SQ + 240, 80), v(SQ + 320, NB, 16)
        exports = {
            "ex": [(tail_gx, 4 * j, 4, 11, 3, out["gc_p"][0, 0, :, 512 * j:512 * j + 512],
                    out["gc_s"][:, 0, GCW - 2, 512 * j:512 * j + 512]) for j in range(3)]
            + [(tail_sc, 0, 4, 10, 2, out["sc_p"][0, 0], out["sc_s"][:, 0, SCW - 2]),
               (tail_cf, 0, 4, 38, 30, out["cf_p"][0, 0], out["cf_s"][:, 0, CFW - 2])],
            "ef": [(tail_ff, 4 * j, min(4, KF - 4 * j), 10, 2, out["ff_p"][0, 0, :, 512 * j:min(512 * (j + 1), FF)],
                    out["ff_s"][:, 0, FCW - 2, 512 * j:min(512 * (j + 1), FF)]) for j in range(6)]}

        def both(x):
            return x.rearrange("p (a b) -> p a b", a=2)

        def bulk(m):
            return pb[:, m % 2, :, 0:TH]

        def spread(x, n, axis):
            return x[:, None, :].to_broadcast([x.shape[0], n, x.shape[1]]) if axis == 1 else \
                x[:, :, None].to_broadcast([x.shape[0], x.shape[1], n])

        def fox_stored(eng):
            eng.wait_ge(qs_out, 16)
            eng.wait_ge(ss_st, 32)
            eng.wait_ge(vt_out, 64)
            for b in range(2):
                eng.wait_ge(stg_out[b], 32)

        W = {"w_in": a["w_in"][0], "w_branch": a["w_branch"][0].rearrange("i r c -> (i r) c"), "w_out": a["w_out"][0],
             "w_ckv": a["w_ckv"][0], "w_cq": a["w_cq"][0], "w_co": a["w_co"][0], "w_ffn_in": a["w_ffn_in"][0],
             "w_ffn_out": a["w_ffn_out"][0]}

        block = ctx.enter_context(nc.Block())

        @block.sync
        def _(sp):
            sp.dma_start(cst[:, 0:2 * P], a["cst"][:, 0:2 * P]).then_inc(id_in, 16)
            for t in range(QT):
                sp.dma_start(xrow[:, t, :], a["x_prompt"][0, t * P:(t + 1) * P, :]).then_inc(x_in, 16)
            sp.dma_start(xrow[0:NB, QT, :], a["x_sample"].rearrange("b t d -> (b t) d")).then_inc(x_in, 16)
            sp.dma_start(cst[:, 2 * P:], a["cst"][:, 2 * P:]).then_inc(par_in, 16)
            sp.wait_ge(pool_made.sem, 1)
            rows = [(V_MIX, "norm_mix"), (V_CROSS, "norm_cross"), (V_FFN, "norm_ffn"), (V_MEM, "norm_mem"),
                    (V_CB, "conf_dw_b"), (V_LG, "conf_ln_g"), (V_LB, "conf_ln_b"), (V_GN, "gdn_norm")]
            for at, name in rows:
                src = a[name].rearrange("l (r c) -> (l r) c", c=P)
                sp.dma_start(pv[at:at + src.shape[0], B_VEC, :], src).then_inc(par_in, 16)
            sp.dma_start(pv[V_FIN:V_FIN + 8, B_VEC, :], a["norm_final"].rearrange("(r c) -> r c", c=P)).then_inc(par_in, 16)
            for at, b, name in ((V_SW, B_VEC, "sconv_w"), (V_GW, B_VEC, "gdn_conv_w"), (0, B_CW, "conf_dw_w"),
                                (0, B_FW, "ffn_conv_w")):
                src = a[name].rearrange("l w (r c) -> (l w r) c", c=P)
                sp.dma_start(pv[at:at + src.shape[0], b, :], src).then_inc(par_in, 16)
            for b, n, name in ((B_SS, 1, "state_sconv"), (B_GS, 4, "state_gdn_conv"), (B_CS, 8, "state_conf_conv"),
                               (B_FS, 4, "state_ffn_conv")):
                src = a[name].rearrange("b l w (r c) -> (b l w r) c", c=P)
                m = src.shape[0] // n
                sp.dma_start(pv[0:m, b:b + n, :], src.rearrange("(n m) c -> m n c", n=n)).then_inc(par_in, 16)
            with nc.allow_non_contiguous_dma(reason="16 columns of w_in, and vectors read by all partitions"):
                sp.wait_ge(pool_made.sem, 2)
                sp.dma_start(bias[:, 0:4], a["gdn_dt_bias"].to_broadcast([P, 4])).then_inc(small_in, 16)
                sp.dma_start(bias[:, 8:16], a["fox_fbias"].to_broadcast([P, 8])).then_inc(small_in, 16)
                sp.dma_start(bias[:, 16:20], a["gdn_a_log"].to_broadcast([P, 4])).then_inc(small_in, 16)
            def unit(u):
                w, row, kt, c = UNITS[u]
                if u >= 2:
                    sp.wait_ge(lo.sem, 2 * u - 2)
                sp.dma_start(raw[:, u % 2, 0:kt, :], W[w][row:row + kt * P, c:c + 256].rearrange("(k p) n -> p k n", p=P))\
                    .then_inc(raw_in[u % 2], 16)

            def page(cache, i):
                n = sp.value_load(ptr_[0:1, i:i + 1], min_val=0, max_val=a[cache].shape[0] - 1)
                sp.dma_start(kring[:, i % 4, :], a[cache][bass.ds(n, 1)].rearrange("a p l h d -> (a p) (l h d)"))\
                    .then_inc(page_in[i % 4], 16)

            unit(0)
            unit(1)
            sp.wait_ge(pt_in, 32)
            for i in range(2):
                page("cache_fox_k", i)
            for e in TIMELINE:
                if e[0] == "piece" and e[2] == 1 and PIECES[e[1]][1] == 0 and PIECES[e[1]][0] + 2 < len(UNITS):
                    unit(PIECES[e[1]][0] + 2)
                elif e[0] == "k" and e[1] + 2 < N_PAGE:
                    if e[1] >= 2:
                        sp.wait_ge(page_free.sem, e[1] - 1)
                    page("cache_fox_k", e[1] + 2)
                elif e[0] == "vstart":
                    sp.wait_ge(pe_s.sem, upto(pe_works, ITEMS.index(("dc", 1)) + 1))
                    for i in range(3):
                        page("cache_fox_v", i)
                elif e[0] == "v" and e[1] + 3 < N_PAGE:
                    if e[1] >= 1:
                        sp.wait_ge(v_used.sem, e[1])
                    page("cache_fox_v", e[1] + 3)
            sp.dma_start(out["sc_s"][:, 0, 0:SCW - 2], a["state_sconv"][:, 0, 1:]).then_inc(out_sem, 16)
            sp.dma_start(out["gc_s"][:, 0, 0:GCW - 2], a["state_gdn_conv"][:, 0, 1:]).then_inc(out_sem, 16)
            sp.dma_start(out["cf_s"][:, 0, 0:CFW - 2], a["state_conf_conv"][:, 0, 1:]).then_inc(out_sem, 16)
            sp.dma_start(out["ff_s"][:, 0, 0:FCW - 2], a["state_ffn_conv"][:, 0, 1:]).then_inc(out_sem, 16)

        @block.gpsimd
        def _(pool):
            def own(ins, st=pool_c):
                st.by(ins)
                pool.wait_ge(st.sem, st.n)

            own(pool.memset(pv[:, :, :], 0.0), pool_made)
            own(pool.memset(bias[:, :], 0.0), pool_made)
            own(pool.memset(cb[:, :, 0:3], 0.0), pool_made)
            own(pool.memset(eps6[:, :], 1e-6), pool_made)
            own(pool.memset(eps5[:, :], 1e-5), pool_made)
            own(pool.memset(fl8, 0.0), pool_made)
            pages = PAGES * NB
            pool.dma_start(ptr_[:, :], a["page_table"].rearrange("(o b) j -> o (b j)", o=1)).then_inc(pt_in, 16)
            pool.dma_start(ptc[:, :], a["page_table"].rearrange("b (j o) -> (b j) o", o=1)).then_inc(pt_in, 16)
            pool.wait_ge(pt_in, 32)

            def split(p):
                u, half, kt = PIECES[p][:3]
                pool.wait_ge(hi.sem, p + 1)
                lo.by(pool.tensor_tensor(wl[:, p % 2, 0:kt, :], raw[:, u % 2, 0:kt, half * P:(half + 1) * P],
                                         wh[:, p % 2, 0:kt, :].bitcast(F32), SUB))

            def product(i):
                if i % PAGES == 0:
                    if i == 0:
                        pool.wait_ge(qs_out, 16)
                    pool.dma_start(qb[:, :], qscr[i // PAGES:i // PAGES + 1, :].to_broadcast([P, 512])).then_inc(qb_in, 16)
                    pool.wait_ge(qb_in, 16 * (i // PAGES + 1))
                pool.wait_ge(page_in[i % 4], 16 * (i // 4 + 1))
                own(pool.tensor_tensor(kring[:, i % 4, :], kring[:, i % 4, :], qb[:, :], MUL), prod_done)

            split(0)
            for e in TIMELINE:
                if e[0] == "piece" and e[2] == 0 and e[1] + 1 < NP_:
                    split(e[1] + 1)
                elif e[0] == "k":
                    product(e[1])
                elif e[0] == "kend":
                    pool.wait_ge(page_free.sem, N_PAGE)
                    pool.indirect_dma_start(lf[:, :, :].rearrange("p a b -> p (a b)"), None,
                                            a["cache_fox_logf"].rearrange("n p l h -> n (p l h)"),
                                            bass.IndirectOffsetOnAxis(ap=ptc[:, 0:1], axis=0)).then_inc(lf_in, 16)
                elif e[0] == "side" and e[2] == ("x", 0):
                    pool.wait_ge(qs_out, 32)
                    pool.wait_ge(mt_act.sem, mt_a[mt_of("cq")])
                    pool.dma_start(qx[:, :, :].rearrange("p b n -> p (b n)"),
                                   qscr.rearrange("b n -> (b n)")[None, :].to_broadcast([P, NB * 512])).then_inc(q8_in, 16)
                    pool.wait_ge(q8_in, 16)
                    pool.wait_ge(mk_in, 16)
                    for b in range(NB):
                        kprod.by(pool.tensor_tensor(kvc[:, b, :, :], kvc[:, b, :, :], spread(qx[:, b, :], 2, 1), MUL))

        @block.tensor
        def _(pe):
            def mm(o, l, r, start=True, stop=True):
                return pe.matmul(o, l, r, start=start, stop=stop, skip_group_check=True)

            def tr(o, i):
                n = i.shape[0]
                return pe.transpose(o, i, ident[0:n, 0:n])

            pe.wait_ge(id_in, 16)
            pe.wait_ge(x_in, 16 * 5)
            for j in range(14):
                if j >= 4:
                    pe.wait_ge(pro_dve.sem, j - 3)
                o = sd[:, j % 4, :]
                if j == 0:
                    for k in range(KD):
                        last = tr(o[:, k * NB:(k + 1) * NB], xrow[0:NB, QT, k * P:(k + 1) * P])
                elif j <= KD:
                    for t in range(QT):
                        last = tr(o[:, t * P:(t + 1) * P], xrow[:, t, (j - 1) * P:j * P])
                else:
                    if j == 9:
                        pe.wait_ge(par_in, 16 * 18)
                    for b in range(4 * (j - 9), min(4 * (j - 9) + 4, N_BLK)):
                        last = tr(o[:, (b % 4) * P:(b % 4 + 1) * P], pv[:, b, :])
                pro_pe.by(last)

            def norm_sum(i):
                if i > 0:
                    pe.wait_ge(act_s.sem, upto(act_works, side_n[0]))
                    pe.wait_ge(dve_s.sem, upto(dve_works, side_n[0]))
                    pe.wait_ge(n_rt.sem, i)
                for k in range(KD):
                    pe.wait_ge(n_sq.sem, KD * i + k + 1)
                    for h in range(1 if i == 1 else 2):
                        w = MEM if i == 1 else TH
                        o = pb[:, 0, h, 0:w] if i == 0 else sd[:, h, 0:w]
                        last = mm(o, ones, sqb[:, k % 2, h * w:(h + 1) * w], k == 0, k == KD - 1)
                    n_pe.by(last)
                sums[0] = i + 1

            side_n, sums = [0], [0]
            ready = {}

            def rhs_ready(kind):
                if kind == "brA":
                    pe.wait_ge(ev_all.sem, count(dve_tile, mt_of("ab")))
                elif kind in ("brC", "brB", "brD", "co"):
                    pe.wait_ge(sp_lo.sem, {"brC": 4, "brD": 8, "brB": 12, "co": 12 + KD + 4}[kind])
                elif kind == "wo":
                    pe.wait_ge(sp_lo.sem, 12 + KD)
                elif kind == "fo":
                    pe.wait_ge(ev_all.sem, count(dve_tile, mt_of("fu")))

            norm_of = {"fq": 0, "kv": 1, "cq": 2, "fg": 3}

            def piece(p, h):
                u, half, kt, kind, idx, first, last_ = PIECES[p]
                m = PIECE_MT[p]
                if h == 0:
                    pe.wait_ge(hi.sem, p + 1)
                    pe.wait_ge(lo.sem, p + 1)
                    if kind not in ready:
                        ready[kind] = p
                        rhs_ready(kind)
                    if first and m >= 2:
                        if MT_ACT[m - 2]:
                            pe.wait_ge(mt_act.sem, mt_a[m - 2])
                        else:
                            pe.wait_ge(mt_dve.sem, mt_d[m - 2])
                    if p == 0:
                        pe.wait_ge(n_rt.sem, 1)
                if kind == "kv" and h == 1:
                    return
                w = MEM if kind == "kv" else TH
                c = slice(0, MEM) if kind == "kv" else slice(h * TH, (h + 1) * TH)
                k0 = UNITS[u][1] // P if kind == "fo" else 0
                for k in range(kt):
                    if h == 0 and kind in norm_of and ready[kind] == p:
                        pe.wait_ge(n_lo.sem, KD * norm_of[kind] + k + 1)
                    if kind == "kv":
                        xa, xb = memh[:, k, :], meml[:, k, :]
                    elif kind.startswith("br") or kind == "co":
                        xa, xb = oh[:, k, c], ol[:, k, c]
                    elif kind == "fo":
                        xa, xb = hh[:, k0 + k, c], hl[:, k0 + k, c]
                    else:
                        xa, xb = xh[:, k, c], xl[:, k, c]
                    o = pb[:, m % 2, h, 0:w]
                    mm(o, wh[:, p % 2, k, :], xa, first and k == 0, False)
                    mm(o, wh[:, p % 2, k, :], xb, False, False)
                    last = mm(o, wl[:, p % 2, k, :], xa, False, last_ and k == kt - 1)
                if h == 1 or kind == "kv":
                    piece_done.by(last)

            def side(K, s):
                kind, n = s[0], s[1]
                side_n[0] = K + 1
                if not pe_works(s):
                    return
                if sums[0] > 1:
                    pe.wait_ge(n_rt.sem, sums[0])
                if upto(act_works, K + 1):
                    pe.wait_ge(act_s.sem, upto(act_works, K + 1))
                if upto(dve_works, K + 1):
                    pe.wait_ge(dve_s.sem, upto(dve_works, K + 1))
                last = None
                if kind == "sm" and n == 0:
                    pe.wait_ge(wsm_lo.sem, 1)
                    for h in range(2):
                        c = slice(h * TH, (h + 1) * TH)
                        for k in range(KD):
                            o = sd[0:16, 2 + h, 0:TH]
                            mm(o, wsh[:, k, :], xh[:, k, c], k == 0, False)
                            mm(o, wsh[:, k, :], xl[:, k, c], False, False)
                            last = mm(o, wsl[:, k, :], xh[:, k, c], False, k == KD - 1)
                elif kind == "sm" and n == 1:
                    for t in range(5):
                        w = P if t < QT else NB
                        last = tr(s1[0:w, t * 16:t * 16 + 16], zrow[0:16, t * P:t * P + w])
                elif kind == "sm" and n == 2:
                    for t in range(QT):
                        tr(s0[0:FH, t * P:(t + 1) * P], fltok[:, t, :])
                    mm(s3[:, 0:P], ones[0:NB, :], exs[0:NB, :])
                    mm(s2[:, 0:16], cs(I_UP), gtok[:, :, :].rearrange("p a b -> p (a b)"))
                    last = mm(s2[:, 16:32], ones, gtok[:, :, :].rearrange("p a b -> p (a b)"))
                elif kind == "fst" and n < 3:
                    if n == 0:
                        pe.wait_ge(mt_act.sem, mt_a[mt_of("fv")])
                    for c in range(4):
                        last = tr(s0[0:NB, c * P:(c + 1) * P], fs[:, 4 * n + c, :])
                elif kind in ("fvt", "fkt") and n < QT:
                    src = fv if kind == "fvt" else fk
                    for c in range(4):
                        last = tr(s0[:, c * P:(c + 1) * P], src[:, c, n * P:(n + 1) * P])
                elif kind == "fox":
                    if n < FOX:
                        h, q = divmod(n, QT)
                        r = slice(FD * (h % 2), FD * (h % 2) + FD)
                        w = (q + 1) * P
                        mm(s0[:, 0:w], fq[r, h // 2, q * P:(q + 1) * P], fk[r, h // 2, 0:w], True, False)
                        mm(s0[:, 0:w], sel(h), cneg[0:FH, 0:w], False, False)
                        last = mm(s0[:, q * P:w], ident, cs(I_CAUSAL), False, True)
                    if 1 <= n <= FOX:
                        for b in range((n - 1) % QT + 1):
                            last = tr(s1[:, b * P:(b + 1) * P], fP[:, b * P:(b + 1) * P])
                    if 2 <= n <= FOX + 1:
                        h, q = divmod(n - 2, QT)
                        for b in range(q + 1):
                            last = mm(s2[FD * (h % 2):FD * (h % 2) + FD, 0:P], vt[:, b, h * FD:(h + 1) * FD], fPT[:, b, :], b == 0, b == q)
                elif kind in ("l2", "gp"):
                    if n < (8 if kind == "l2" else 4):
                        for h in range(2):
                            last = mm(sd[:, h, 0:TH], ones, lsq[:, h * TH:(h + 1) * TH])
                elif kind == "gdn":
                    c = s[2]
                    cc = slice(c * P, (c + 1) * P)
                    if n == -1 and c == 0:
                        pe.wait_ge(ev_all.sem, count(dve_tile, mt_of("gx")))
                    for h in range(GH):
                        o = slice(h * P, (h + 1) * P)
                        q_, k_, v_ = (gx_tile(4 * j + h)[:, cc] for j in range(3))
                        if n == -1:
                            tr(s0[:, o], k_)
                            tr(s1[:, o], v_)
                            last = mm(s2[:, o], gtok[:, c, h:h + 1].to_broadcast([P, P]), cs(I_UP))
                        elif n == 0:
                            last = mm(s0[:, o], k_, k_)
                        elif n == 1:
                            mm(s0[:, o], k_, q_)
                            last = tr(s1[:, o], gM[:, h, :])
                        elif 2 <= n <= 12 and n % 2 == 0:
                            last = mm(s0[:, o], gM[:, h, :], gXT[:, h, :])
                        elif 3 <= n <= 13:
                            last = mm(s1[:, o], gX[:, h, :], gQ[:, h, :])
                            if n < 13:
                                last = mm(s2[:, o], gQ[:, h, :], gX[:, h, :])
                        elif n == 14:
                            mm(s0[:, o], gXT[:, h, :], gvb[:, h, :], h == 0, False)
                            last = mm(s1[:, o], gR[:, h, :], gXT[:, h, :])
                        elif n == 15:
                            last = mm(s0[:, o], gW[:, h, :], gS[:, h, :], False, h == GH - 1)
                        elif n == 16:
                            mm(s2[:, o], gS[:, h, :], gqd[:, h, :], True, False)
                            mm(s2[:, o], gM[:, h, :], gQK[:, h, :], False, True)
                            last = mm(s1[:, o], gkd[:, h, :], gM[:, h, :])
                elif kind == "cln":
                    for c in (range(KB) if n == 0 else [n - 1] if n < 5 else []):
                        src = oC[:, c, :] if n == 0 else lsq
                        for h in range(2):
                            last = mm(sd[:, (0 if n == 0 else 2) + h, 0:TH], ones, src[:, h * TH:(h + 1) * TH], c == 0, c == KB - 1)
                elif kind == "gs":
                    if n == 1:
                        pe.wait_ge(ss_in, 16)
                        for u in range(32):
                            mm(s0[:, 2 * u:2 * u + 2], ssam[:, u, :], qkp[:, u, :])
                        last = mm(s1[:, 0:32], ones, kqs)
                    elif n == 2:
                        tr(s2[0:32, 0:P], dl)
                        last = tr(s2[0:32, P:2 * P], kc)
                    elif 3 <= n <= 10:
                        last = mm(s0[:, :], krow[0:32, :], blk[0:32, :, :].rearrange("p a b -> p (a b)"))
                elif kind == "dc" and n == 0:
                    mm(s0[:, 0:FH], cs(I_PAGE), tot)
                    last = mm(s1[:, 0:64], ones, totm[:, :, :].rearrange("p a b -> p (a b)"))
                elif kind == "dc" and n == 1:
                    for h in range(FH):
                        last = tr(sd[:, 2 + h // 4, (h % 4) * P:(h % 4 + 1) * P], cpg[:, h, :])
                elif kind == "ds" and n == 0:
                    tr(s0[0:64, 0:P], mx64[:, :, :].rearrange("p a b -> p (a b)"))
                    f = qk32[:, :, :].rearrange("p a b -> p (a b)")
                    mm(s1[:, 0:32], cs(I_LO), f)
                    last = mm(s1[:, 32:64], cs(I_HI), f)
                elif kind == "ds" and n == 1:
                    last = mm(s2[:, 0:64], ones[0:64, :], dg64[0:64, :])
                elif kind == "ds" and n == 2:
                    last = mm(s3[:, 0:64], ones, rs64[:, :, :].rearrange("p a b -> p (a b)"))
                elif kind == "df" and n == 0:
                    pe.wait_ge(v64_in, 32)
                    last = tr(s3[:, 0:64], v64[0:NB * FH, :, :].rearrange("p a b -> p (a b)"))
                elif kind in ("ex", "ef") and pe_works(s):
                    src, c0, nc_, w = exports[kind][n][:4]
                    for c in range(nc_):
                        last = tr(s0[0:w, c * P:(c + 1) * P], src[:, c0 + c, :])
                elif kind == "ml" and n == 1:
                    pe.wait_ge(mem_in, 16)
                    for k in range(KD):
                        for t in range(2):
                            last = tr(sd[:, k // 2, ((k % 2) * 2 + t) * P:((k % 2) * 2 + t + 1) * P], mrow[:, t, k * P:(k + 1) * P])
                elif kind == "xm" and n == 0:
                    pe.wait_ge(mt_act.sem, mt_a[mt_of("cq")])
                    for t in range(2):
                        for h in range(XH):
                            tr(sd[:, t, h * P:(h + 1) * P], mvT[:, h, t * P:(t + 1) * P])
                            last = tr(sd[:, 2 + t, h * P:(h + 1) * P], mkT[:, h, t * P:(t + 1) * P])
                elif kind == "xm" and n == 1:
                    for h in range(XH):
                        last = tr(s0[0:NB, h * P:(h + 1) * P], qc[:, h, SEQ:T])
                elif kind == "x":
                    if n < XU:
                        q, h = n // 2, 2 * (n % 2)
                        for j in range(2):
                            last = mm(s0[:, j * MEM:(j + 1) * MEM], qc[:, h + j, q * P:(q + 1) * P], mkT[:, h + j, :])
                    if 1 <= n <= XU:
                        for j in range(2):
                            for t in range(2):
                                last = tr(s1[:, (2 * j + t) * P:(2 * j + t + 1) * P], xP[:, j, t * P:(t + 1) * P])
                    if 2 <= n <= XU + 1:
                        h = 2 * (n % 2)
                        for j in range(2):
                            for t in range(2):
                                last = mm(s2[:, j * P:(j + 1) * P], mv[:, t, (h + j) * P:(h + j + 1) * P], xPT[:, 2 * j + t, :],
                                          t == 0, t == 1)
                elif kind == "xd" and n == 0:
                    last = tr(s0[0:32, 0:P], xmx[:, :, :].rearrange("p a b -> p (a b)"))
                elif kind == "xd" and n == 1:
                    last = mm(s1[:, 0:32], ones[0:32, :], xdg[0:32, :])
                elif kind == "xd" and n == 2:
                    mm(s2[:, 0:32], ones, xrs[:, :, :].rearrange("p a b -> p (a b)"))
                    for b in range(NB):
                        if b < 2:
                            pe.wait_ge(mv_in[b], 16 * NB // 2)
                        for h in range(XH):
                            for t in range(2):
                                last = mm(s3[:, b * 8 + 2 * h:b * 8 + 2 * h + 2], kvc[:, b, t, h * P:(h + 1) * P],
                                          xsc[:, b, t, 2 * (h // 2):2 * (h // 2) + 2], t == 0, t == 1)
                elif kind == "y" and n < 10:
                    if n == 0:
                        pe.wait_ge(n_tmp.sem, 5 * KD)
                    for c in range(4):
                        k = (n % 2) * 4 + c
                        t = n // 2
                        w = P if t < QT else NB
                        last = tr(s0[0:w, c * P:(c + 1) * P], xT[:, k, t * P:t * P + w])
                pe_s.by(last)

            def page(i):
                if i == 0:
                    pe.wait_ge(dve_s.sem, upto(dve_works, ITEMS.index(("ds", 3)) + 1))
                elif i % PAGES == 0:
                    pe.wait_ge(v_rows.sem, i // PAGES)
                pe.wait_ge(page_in[i % 4], 16 * (N_PAGE // 4 + i // 4 + 1))
                v_used.by(mm(s3[0:FH, :], sc[:, i, :], kring[:, i % 4, :], i % PAGES == 0, i % PAGES == PAGES - 1))

            for e in TIMELINE:
                if e[0] == "nsum":
                    norm_sum(e[1])
                elif e[0] == "piece":
                    piece(e[1], e[2])
                elif e[0] == "side":
                    side(e[1], e[2])
                elif e[0] == "v":
                    page(e[1])

        @block.scalar
        def _(act):
            def own(ins, st=act_c):
                st.by(ins)
                act.wait_ge(st.sem, st.n)

            def fn(o, i, f, st=act_c, **kw):
                own(act.activation(o, i, f, **kw), st)

            def split(p):
                u, half, kt = PIECES[p][:3]
                if half == 0:
                    act.wait_ge(raw_in[u % 2], 16 * (u // 2 + 1))
                if p >= 2:
                    act.wait_ge(piece_done.sem, p - 1)
                    act.wait_ge(lo.sem, p - 1)
                fn(wh[:, p % 2, 0:kt, :], raw[:, u % 2, 0:kt, half * P:(half + 1) * P], ACT.Copy, hi)

            def evac(m, second):
                p = MT_LAST[m]
                kind, idx = PIECES[p][3:5]
                s = idx % 2
                if second and not second_tile[m]:
                    return
                if second and kind in ("gx", "fg"):
                    y = gx_tile(idx) if kind == "gx" else pairA[:, s, :]
                    act.wait_ge(ev_y.sem, count(conv_tile, m))
                    fn(pairB[:, s, :], y, ACT.Tanh, ev_t)
                    return
                if second:
                    act.wait_ge(mt_dve.sem, mt_d[m])
                    fn(oh[:, idx, :] if kind == "ab" else hh[:, idx, :], tmp, ACT.Copy, ev_t)
                    return
                if not MT_ACT[m]:
                    return
                if m >= 2:
                    act.wait_ge(ev_all.sem, count(dve_tile, m - 2))
                act.wait_ge(piece_done.sem, p + 1)
                x = bulk(m)
                if kind in ("fq", "fk", "fv"):
                    j = 4 * ("fq", "fk", "fv").index(kind) + idx
                    c = FD ** -0.5 if kind == "fq" else 1.0
                    act_c.by(act.activation(both(qkv[:, j, :]), x, ACT.Copy, scale=c))
                    fn(fs[:, j, :], pb[:, m % 2, 1, TH - NB:TH], ACT.Copy, mt_act, scale=c)
                elif kind == "cv":
                    fn(both(pairA[:, s, :]), x, ACT.Copy, mt_act, scale=0.5)
                elif kind == "cg" or kind.startswith("gate"):
                    fn(both(pairB[:, s, :]), x, ACT.Tanh, mt_act, scale=0.5)
                elif kind in ("gx", "fg"):
                    fn(both(cb[:, s, 3:3 + T]), x, ACT.Copy, mt_act)
                elif kind == "ac":
                    fn(both(pairA[:, s, :]), x, ACT.Copy, mt_act)
                elif kind == "gz":
                    fn(both(pairA[:, s, :]), x, ACT.Copy, scale=0.5)
                    fn(both(pairB[:, s, :]), x, ACT.Tanh, mt_act, scale=0.5)
                elif kind == "kv":
                    o = mkT[:, idx, :] if idx < XH else mvT[:, idx - XH, :]
                    fn(o, pb[:, m % 2, 0, 0:MEM], ACT.Copy, mt_act)
                elif kind == "cq":
                    fn(both(qc[:, idx, :]), x, ACT.Copy, mt_act, scale=P ** -0.5)

            def norm_sum(i, src, width):
                for k in range(KD):
                    if k >= 2:
                        act.wait_ge(n_pe.sem, KD * i + k - 1)
                    if i == 0:
                        act.wait_ge(pro_dve.sem, k + 2)
                    if k == 0 and i == 0:
                        act.wait_ge(pool_made.sem, 6)
                    elif k == 0 and i == 1:
                        act.wait_ge(dve_s.sem, upto(dve_works, ITEMS.index(("ml", 2)) + 1))
                        act.wait_ge(ev_all.sem, count(dve_tile, mt_of("brB")))
                        act.wait_ge(piece_done.sem, last_piece("brB") + 1)
                    elif k == 0:
                        act.wait_ge(ev_all.sem, count(dve_tile, mt_of({2: "wo", 3: "co", 4: "fo"}[i])))
                        act.wait_ge(n_lo.sem, KD * i)
                    st = n_sq
                    own(act.activation(sqb[:, k % 2, 0:width], src[:, k, :], ACT.Square), st)
                act.wait_ge(n_pe.sem, KD * (i + 1))
                x = pb[:, 0, :, 0:TH] if i == 0 else s0[:, 0:MEM] if i == 1 else sd[:, 0:2, 0:TH]
                r = lrs[:, 0:MEM] if i == 1 else lrs
                fn(r if i == 1 else both(r), x, ACT.Ln, scale=1.0 / D, bias=eps6[:, 0:1])
                fn(r, r, ACT.Exp, n_rt, scale=-0.5)

            def norm_apply(i, k, width):
                if i == 4 or k == KD:
                    return
                act.wait_ge(n_tmp.sem, KD * i + k + 1)
                o = memh[:, k, :] if i == 1 else xh[:, k, :]
                fn(o, sqb[:, k % 2, 0:width], ACT.Copy, n_hi)

            def store(dst, src, st=out_sem):
                act.dma_start(dst, src).then_inc(st, 16)

            used = [0, 0]

            def staged(n, copy):
                if used[n % 2]:
                    act.wait_ge(stg_out[n % 2], 16 * used[n % 2])
                copy()

            def sent(n, dst, src):
                used[n % 2] += 1
                store(dst, src, stg_out[n % 2])

            def side(K, s):
                kind, n = s[0], s[1]
                works = act_works(s) or s in (("gs", 12), ("ml", 0)) or (kind == "x" and n > 0)
                if not works:
                    return
                if upto(pe_works, K):
                    act.wait_ge(pe_s.sem, upto(pe_works, K))
                if upto(dve_works, K):
                    act.wait_ge(dve_s.sem, upto(dve_works, K))
                fins = None
                va, av = upto(to_act, K), upto(to_dve, K)
                if kind == "sm" and n == 1:
                    fins = act.activation(both(zrow[0:16, :]), sd[0:16, 2:4, 0:TH], ACT.Copy)
                elif kind == "sm" and n == 2:
                    act.wait_ge(v2a.sem, va + 1)
                    for x_, y_ in ((slice(0, P), slice(0, 64)), (slice(0, NB), slice(64, 80))):
                        fn(zl[x_, y_], az[x_, y_], ACT.Exp, scale=-1.0)
                        fn(zb[x_, y_], zt[x_, y_], ACT.Tanh, scale=0.5)
                    fn(bias[:, 16:20], bias[:, 16:20], ACT.Exp)
                    fn(zl[:, 0:64], zl[:, 0:64], ACT.Ln, bias=1.0)
                    fn(zl[0:NB, 64:80], zl[0:NB, 64:80], ACT.Ln, a2v, bias=1.0)
                    fins = act.activation(rsum[:, 0:1], eps6[:, 0:1], ACT.Copy)
                elif kind == "sm" and n == 3:
                    act.wait_ge(v2a.sem, va + 1)
                    fn(bsc[:, :, 0:4], bsc[:, :, 0:4], ACT.Exp)
                    fn(edc, dcol, ACT.Exp)
                    fn(kdf, kdf, ACT.Exp)
                    fn(edl, edl, ACT.Exp, a2v)
                    with nc.allow_non_contiguous_dma(reason="8 values of a token"):
                        store(out["fl_p"][0, :, 0, :].rearrange("(t p) h -> p t h", p=P), fltok[:, :, :])
                        store(out["fl_s"][:, 0, 0, :], zsam[0:NB, 8:16])
                    fins = act.activation(rsum[:, 0:1], eps6[:, 0:1], ACT.Copy)
                elif kind == "fst":
                    def copy():
                        fn(srow[0:NB, n % 2, :], s0[0:NB, :], ACT.Copy)
                    if n == 3:
                        act.wait_ge(qs_out, 16)
                    copy()
                    if n == 1:
                        store(qscr, srow[0:NB, 1, :], qs_out)
                    else:
                        dst = out["fk_s" if n == 2 else "fv_s"]
                        store(dst.rearrange("b t l h d -> b (t l h d)"), srow[0:NB, n % 2, :], ss_st)
                    fins = act.activation(rsum[:, 0:1], eps6[:, 0:1], ACT.Copy)
                elif kind == "fvt":
                    fn(vt[:, n - 1, :], s0, ACT.Copy)
                    store(out["fv_p"][0, (n - 1) * P:n * P].rearrange("t l h d -> t (l h d)"), vt[:, n - 1, :], vt_out)
                    fins = act.activation(rsum[:, 0:1], eps6[:, 0:1], ACT.Copy)
                elif kind == "fkt":
                    if n >= 3:
                        act.wait_ge(stg_out[(n - 1) % 2], 16)
                    fn(stg[:, (n - 1) % 2, :], s0, ACT.Copy)
                    sent(n - 1, out["fk_p"][0, (n - 1) * P:n * P].rearrange("t l h d -> t (l h d)"), stg[:, (n - 1) % 2, :])
                    fins = act.activation(rsum[:, 0:1], eps6[:, 0:1], ACT.Copy)
                elif kind == "fox":
                    if n <= FOX:
                        w = ((n - 1) % QT + 1) * P
                        act.wait_ge(v2a.sem, va + 1)
                        fn(fP[:, 0:w], s0[:, 0:w], ACT.Exp, a2v, bias=nmx[:, 0:1], accum_out=rsum[:, 0:1])
                    w = ((n - 2) % QT + 1) if 2 <= n <= FOX + 1 else 1
                    if 2 <= n <= FOX + 1:
                        fins = act.activation(fPT[:, 0:w, :], s1[:, 0:w * P].rearrange("p (a b) -> p a b", a=w), ACT.Copy)
                    else:
                        fins = act.activation(rsum[:, 1:2], eps6[:, 0:1], ACT.Copy)
                elif kind in ("l2", "gp"):
                    last = 8 if kind == "l2" else 4
                    if n == 0 and kind == "l2":
                        fox_stored(act)
                        act.dma_start(ssam[:, :, :], a["state_gdn"].rearrange("b l h k v -> k (b l h) v")).then_inc(ss_in, 16)
                    if n == 0 and kind == "gp":
                        store(out["S_p"].rearrange("b l h k v -> k (b l h) v"), gS[:, :, :], gs_out)
                    if n < 8 and kind == "l2":
                        act.wait_ge(ev_all.sem, count(dve_tile, mt_of("gx", n)))
                    if n:
                        fn(both(lrs), sd[:, 0:2, 0:TH], ACT.Ln, scale=1.0 if kind == "l2" else 1.0 / P, bias=eps6[:, 0:1])
                        fn(lrs, lrs, ACT.Exp, a2v, scale=-0.5)
                    if n < last:
                        fins = act.activation(lsq, gx_tile(n) if kind == "l2" else oB[:, n, :], ACT.Square)
                    else:
                        fins = act.activation(rsum[:, 0:1], eps6[:, 0:1], ACT.Copy)
                elif kind == "gdn":
                    c = s[2]
                    s4 = [x.rearrange("p (a b) -> p a b", a=GH) for x in (s0, s1, s2)]
                    if n == 0:
                        if c == 0:
                            act.wait_ge(ss_out, 16)
                        for h in range(GH):
                            o = slice(h * P, (h + 1) * P)
                            fn(gR[:, h, :], s0[:, o], ACT.Copy, scale=bed[:, 4 * c + h:4 * c + h + 1])
                            fn(gkd[:, h, :], s0[:, o], ACT.Copy, scale=kdf[:, 4 * c + h:4 * c + h + 1])
                        act.wait_ge(v2a.sem, va + 1)
                        fn(gQ[:, :, :], gQ[:, :, :], ACT.Exp, a2v, scale=-1.0)
                        act.wait_ge(v2a.sem, va + 2)
                        fn(gqd[:, :, :], s4[2], ACT.Exp, a2v)
                        fins = act.activation(gXT[:, :, :], gM[:, :, :], ACT.Exp)
                    elif n <= 13:
                        fins = act.activation(gQ[:, :, :], s4[0], ACT.Copy)
                    elif n == 15:
                        fins = act.activation(gW[:, :, :], s4[1], ACT.Copy, scale=-1.0)
                    elif n == 16:
                        fins = act.activation(gM[:, :, :], s4[0], ACT.Copy)
                    else:
                        fins = act.activation(oB[:, :, c * P:(c + 1) * P], s4[2], ACT.Copy)
                elif kind == "cln":
                    if n < 5:
                        if n == 1:
                            act.wait_ge(v2a.sem, va + 1)
                        fins = act.activation(lsq, oC[:, n - 1, :], ACT.Square)
                    else:
                        fn(both(lrs), sd[:, 2:4, 0:TH], ACT.Ln, scale=1.0 / BD, bias=eps5[:, 0:1])
                        fn(lrs, lrs, ACT.Exp, a2v, scale=-0.5)
                        for c in range(KB):
                            if c != 1:
                                act.wait_ge(v2a.sem, va + (1 if c == 0 else c))
                            fn(lsq if c % 2 == 0 else lrs, oC[:, c, :], ACT.Tanh, a2v)
                        fins = act.activation(rsum[:, 0:1], eps6[:, 0:1], ACT.Copy)
                elif kind == "gs" and n == 12:
                    store(out["S_s"].rearrange("b l h k v -> k (b l h) v"), ssam[:, :, :], ss_out)
                elif kind == "ds":
                    if n == 2:
                        act.wait_ge(v2a.sem, va + 1)
                        fn(pn[:, :, :], pn[:, :, :], ACT.Exp)
                        fn(sc[:, :, :], sc[:, :, :], ACT.Exp, a2v)
                        fins = act.activation(rsum[:, 0:1], eps6[:, 0:1], ACT.Copy)
                elif kind in ("ex", "ef"):
                    src, c0, nc_, w, wp, dp, ds_ = exports[kind][n - 1]
                    st_ = stg if kind == "ex" else mstg
                    j = (n - 1) % 2
                    if used[j]:
                        act.wait_ge(stg_out[j], 16 * used[j])
                    fn(st_[0:w, j, 0:nc_ * P], s0[0:w, 0:nc_ * P], ACT.Copy)
                    sent(j, dp, st_[0:wp, j, 0:nc_ * P])
                    sent(j, ds_, st_[wp:w, j, 0:nc_ * P])
                    fins = act.activation(rsum[:, 0:1], eps6[:, 0:1], ACT.Copy)
                elif kind == "ml" and n == 0:
                    act.wait_ge(gs_out, 16)
                    for j in range(2):
                        act.wait_ge(stg_out[j], 16 * used[j])
                    act.dma_start(mrow[:, :, :], a["mem_prompt"][0].rearrange("(t p) d -> p t d", p=P)).then_inc(mem_in, 16)
                    act.dma_start(kvc[:, :, :, :].rearrange("p b t n -> p (b t) n"),
                                  a["cache_mem_k"].rearrange("b l (t p) h d -> p (b l t) (h d)", p=P)).then_inc(mk_in, 16)
                elif kind == "xm":
                    if n == 1:
                        fn(mv[:, :, :], sd[:, 0:2, :], ACT.Copy)
                        fn(xstg[:, :, :], sd[:, 2:4, :], ACT.Copy)
                        store(out["mv_p"][0, 0].rearrange("(t p) h d -> p t (h d)", p=P), mv[:, :, :])
                        store(out["mk_p"][0, 0].rearrange("(t p) h d -> p t (h d)", p=P), xstg[:, :, :])
                        fins = act.activation(rsum[:, 0:1], eps6[:, 0:1], ACT.Copy)
                    else:
                        own(act.activation(qrow[0:NB, :], s0[0:NB, :], ACT.Copy), act_s)
                        store(qscr, qrow[0:NB, :], qs_out)
                        return
                elif kind == "x":
                    if 3 <= n <= NB + 2:
                        b = n - 3
                        act.wait_ge(kred.sem, b + 1)
                        act.dma_start(kvc[:, b, :, :], a["cache_mem_v"][b, 0].rearrange("(t p) h d -> p t (h d)", p=P))\
                            .then_inc(mv_in[b % 2], 16)
                    if n <= XU:
                        act.wait_ge(v2a.sem, va + 1)
                        for j in range(2):
                            (a2v if j else act_c).by(act.activation(
                                xP[:, j, :], s0[:, j * MEM:(j + 1) * MEM], ACT.Exp, bias=xnm[:, j:j + 1], accum_out=xsum[:, j:j + 1]))
                    if 2 <= n <= XU + 1:
                        fins = act.activation(xPT[:, :, :], s1.rearrange("p (a b) -> p a b", a=4), ACT.Copy)
                    elif n == 1:
                        fins = act.activation(rsum[:, 1:2], eps6[:, 0:1], ACT.Copy)
                elif kind == "xd":
                    if n == 2:
                        act.wait_ge(v2a.sem, va + 1)
                        fn(xsc[:, :, :, :], xsc[:, :, :, :], ACT.Exp, a2v)
                        fins = act.activation(rsum[:, 0:1], eps6[:, 0:1], ACT.Copy)
                elif kind == "y":
                    w = P if n - 1 < 8 else NB
                    j, t = (n - 1) % 2, (n - 1) // 2
                    if used[j]:
                        act.wait_ge(stg_out[j], 16 * used[j])
                    fn(mstg[0:w, j, :], s0[0:w, :], ACT.Copy)
                    dst = out["y_p"][0, t * P:(t + 1) * P, j * 512:(j + 1) * 512] if t < QT else out["y_s"][:, 0, j * 512:(j + 1) * 512]
                    sent(j, dst, mstg[0:w, j, :])
                    fins = act.activation(rsum[:, 0:1], eps6[:, 0:1], ACT.Copy)
                if act_works(s):
                    own(fins, act_s)

            with nc.allow_non_contiguous_dma(reason="16 columns of w_in"):
                act.dma_start(wsm[:, :, 0:8], W["w_in"][:, C_GA:C_GA + 8].rearrange("(k p) n -> p k n", p=P)).then_inc(small_in, 16)
                act.dma_start(wsm[:, :, 8:16], W["w_in"][:, C_FF:C_FF + 8].rearrange("(k p) n -> p k n", p=P)).then_inc(small_in, 16)
            act.wait_ge(small_in, 16 * 5)
            fn(wsh[:, :, :], wsm[:, :, :], ACT.Copy, wsm_hi)
            split(0)
            done = [0]
            spl = [0]
            for e in TIMELINE:
                if e[0] == "nsum":
                    norm_sum(e[1], memT if e[1] == 1 else xT, MEM if e[1] == 1 else T)
                    if e[1] == 0:
                        store(xscr, xT[:, :, :].rearrange("p a b -> p (a b)"), xs_out)
                elif e[0] == "napply":
                    norm_apply(e[1], e[2], MEM if e[1] == 1 else T)
                elif e[0] == "piece":
                    cur = e[1]
                    if e[2] == 0 and cur + 1 < NP_:
                        split(cur + 1)
                elif e[0] in ("evac", "evac2"):
                    evac(e[1], e[0] == "evac2")
                    if e[0] == "evac2":
                        done[0] = e[1] + 1
                elif e[0] == "split":
                    src, n = {"brC": (oC, 4), "brB": (oB, 4), "brD": (oD, 4), "brX": (oX, 4), "merged": (xT, 8)}[e[1]]
                    act.wait_ge(piece_done.sem, cur if e[1] not in ("merged", "brX") else cur + 1)
                    act.wait_ge(ev_all.sem, count(dve_tile, done[0] - 1))
                    if upto(dve_works, side_at[0]):
                        act.wait_ge(dve_s.sem, upto(dve_works, side_at[0]))
                    for k in range(n):
                        fn((xh if n == 8 else oh)[:, k, :], src[:, k, :], ACT.Copy, sp_hi)
                    spl[0] += n
                    if e[1] == "merged":
                        act.wait_ge(sp_lo.sem, spl[0])
                        act.wait_ge(xs_out, 16)
                        act.dma_start(xT[:, :, :].rearrange("p a b -> p (a b)"), xscr).then_inc(xs_in, 16)
                elif e[0] == "side":
                    side(e[1], e[2])
                    side_at[0] = e[1] + 1
                elif e[0] == "v" and e[1] % PAGES == PAGES - 1:
                    b = e[1] // PAGES
                    act.wait_ge(v_used.sem, e[1] + 1)
                    if b >= 2:
                        act.wait_ge(vs_out[b % 2], 16 * (b // 2))
                    fn(vrow[0:FH, b % 2, :], s3[0:FH, :], ACT.Copy, v_rows)
                    at = b * FH * (512 + FD)
                    store(vscr[at:at + FH * 512].rearrange("(h n) -> h n", h=FH), vrow[0:FH, b % 2, :], vs_out[b % 2])
                    if b == NB - 1:
                        for j in range(2):
                            act.wait_ge(vs_out[j], 16 * NB // 2)
                        for j in range(2):
                            act.dma_start(v64[0:NB * FH, j, :], vscr.rearrange("(r n) -> r n", n=512 + FD)[:, 0:FD]).then_inc(v64_in, 16)
            for st_, k in ((out_sem, out_total[0]),):
                act.wait_ge(st_, k)
            for j in range(2):
                act.wait_ge(stg_out[j], 16 * used[j])
            act.wait_ge(ss_out, 16)
            act.wait_ge(gs_out, 16)
            act.wait_ge(ss_st, 32)
            act.wait_ge(vt_out, 64)

        @block.vector
        def _(dve):
            def own(ins, st=dve_c):
                st.by(ins)
                dve.wait_ge(st.sem, st.n)

            def tt(o, x, y, op, st=dve_c):
                own(dve.tensor_tensor(o, x, y, op), st)

            def ts(o, x, s1_, s2_=None, op0=MUL, op1=None, st=dve_c):
                own(dve.tensor_scalar(o, x, s1_, s2_, op0, op1) if op1 else dve.tensor_scalar(o, x, s1_, None, op0), st)

            def stt(o, x, s_, y, op0, op1, st=dve_c):
                own(dve.scalar_tensor_tensor(out=o, in0=x, scalar=s_, in1=y, op0=op0, op1=op1), st)

            def cp(o, x, st=dve_c):
                own(dve.tensor_copy(o, x), st)

            def red(o, x, op, st=dve_c):
                own(dve.tensor_reduce(o, x, AX, op), st)

            def conv(x, y, width, wcol, hist, w_last):
                ts(y, x[:, 3:3 + T], w_last)
                for j in range(width - 1):
                    stt(y[:, 0:SEQ], x[:, 4 - width + j:4 - width + j + SEQ], wcol(j), y[:, 0:SEQ], MUL, ADD)
                    past = hist(j)
                    ys = y[:, SEQ:T] if len(past.shape) == 2 else y[:, SEQ:T].rearrange("p (n b) -> p n b", b=2)
                    stt(ys, past, wcol(j), ys, MUL, ADD)


            def evac(m, second):
                p = MT_LAST[m]
                kind, idx = PIECES[p][3:5]
                s = idx % 2
                if second and not second_tile[m]:
                    return
                if second:
                    dve.wait_ge(ev_t.sem, count(second_tile, m))
                    if kind == "gx":
                        stt(gx_tile(idx), pairB[:, s, :], 1.0, gx_tile(idx), ADD, MUL, ev_all)
                    elif kind == "fg":
                        stt(pairA[:, s, :], pairB[:, s, :], 1.0, pairA[:, s, :], ADD, MUL, ev_all)
                    else:
                        h_, l_ = (oh, ol) if kind == "ab" else (hh, hl)
                        tt(l_[:, idx, :], tmp, h_[:, idx, :].bitcast(F32), SUB, ev_all)
                    return
                if MT_ACT[m]:
                    dve.wait_ge(mt_act.sem, mt_a[m])
                else:
                    dve.wait_ge(piece_done.sem, p + 1)
                x = bulk(m)
                if kind == "cg":
                    if idx == 0:
                        dve.wait_ge(xs_out, 16)
                        own(dve.memset(glu[:, :, 0:CFW - 1], 0.0))
                    stt(glu[:, idx, CFW - 1:CFW - 1 + T], pairB[:, s, :], 1.0, pairA[:, s, :], ADD, MUL)
                    cp(tail_cf[:, idx, :], glu[:, idx, SEQ:SEQ + 38], ev_all)
                elif kind == "gx":
                    cp(tail_gx[:, idx, :], cb[:, s, SEQ:SEQ + 11])
                    if idx == 0:
                        dve.wait_ge(pe_s.sem, upto(pe_works, ITEMS.index(("fvt", 4))))
                    if idx >= 4:
                        at = ITEMS.index(("fox", 8 * (idx % 4) + 9 if idx == 4 else FOX - 1))
                        dve.wait_ge(pe_s.sem, upto(pe_works, at + 1))

                    gh = cols[:, B_GS:B_GS + 4, 0:72].rearrange("p n (b r) -> p n b r", b=2)

                    def hist(j):
                        return gh[:, :, :, j * 12 + idx]

                    conv(cb[:, s, :], gx_tile(idx), GCW, lambda j: col(V_GW + 12 * j + idx), hist, col(V_GW + 36 + idx))
                    cp(fl8[:, 0:1], fl8[:, 1:2], ev_y)
                elif kind == "ah":
                    tt(both(cb[:, s, 3:3 + T]), both(pairA[:, s, :]), x, MUL, mt_dve)
                    cp(tail_sc[:, idx, :], cb[:, s, SEQ + 1:SEQ + 11])
                    conv(cb[:, s, :], pairB[:, s, :], SCW, lambda j: col(V_SW + 4 * j + idx),
                         lambda j: cols[:, B_SS, 0:64].rearrange("p (b r) -> p b r", b=NB)[:, :, 4 * j + idx], col(V_SW + 8 + idx))
                    cp(fl8[:, 0:1], fl8[:, 1:2], ev_all)
                elif kind == "ab":
                    tt(both(tmp), both(pairB[:, s, :]), x, MUL, mt_dve)
                elif kind.startswith("br"):
                    if kind == "brA":
                        stt(both(xT[:, idx, :]), both(pairB[:, s, :]), 1.0, x, ADD, MUL, mt_dve)
                        cp(fl8[:, 0:1], fl8[:, 1:2], ev_all)
                    else:
                        stt(both(tmp), both(pairB[:, s, :]), 1.0, x, ADD, MUL, mt_dve)
                        tt(xT[:, idx, :], xT[:, idx, :], tmp, ADD, ev_all)
                elif kind == "gz":
                    stt(pairA[:, s, :], pairB[:, s, :], 1.0, pairA[:, s, :], ADD, MUL)
                    tt(oB[:, idx, :], oB[:, idx, :], pairA[:, s, :], MUL, ev_all)
                elif kind in ("wo", "co", "fo"):
                    if kind == "wo" and idx == 0:
                        dve.wait_ge(xs_in, 16)
                    stt(both(xT[:, idx, :]), x, 0.5 if kind == "wo" else 1.0, both(xT[:, idx, :]), MUL, ADD, mt_dve)
                    cp(fl8[:, 0:1], fl8[:, 1:2], ev_all)
                elif kind == "fg":
                    cp(tail_ff[:, idx, :], cb[:, s, SEQ + 1:SEQ + 11])
                    fh = cols[:, B_FS:B_FS + 4, 0:88].rearrange("p n (b r) -> p n b r", b=2)

                    def hist(j):
                        return fh[:, :, :, j * KF + idx]
                    conv(cb[:, s, :], pairA[:, s, :], FCW, lambda j: cols[:, B_FW, KF * j + idx:KF * j + idx + 1], hist,
                         cols[:, B_FW, 2 * KF + idx:2 * KF + idx + 1])
                    cp(fl8[:, 0:1], fl8[:, 1:2], ev_y)
                elif kind == "fu":
                    tt(both(tmp), both(pairA[:, s, :]), x, MUL, mt_dve)

            def norm_apply(i, k, src, width, gain):
                hb = memh if width == MEM else xh
                lb = meml if width == MEM else xl
                if k < KD:
                    stt(xT[:, k, :] if i == 4 else sqb[:, k % 2, 0:width], src[:, k, :], col(gain + k), lrs[:, 0:width],
                        MUL, MUL, n_tmp)
                if k and i < 4:
                    dve.wait_ge(n_hi.sem, KD * i + k)
                    tt(lb[:, k - 1, :], sqb[:, (k - 1) % 2, 0:width], hb[:, k - 1, :].bitcast(F32), SUB, n_lo)

            tap_at = {}

            def tap(n):
                j, c = divmod(n, KB)
                w = cols[:, B_CW, 0:124].rearrange("p (j c) -> p j c", c=KB)[:, :, c]
                g = glu[:, c, :]
                if j == 0:
                    own(dve.tensor_scalar(oC[:, c, :], g[:, 30:30 + T], w[:, 30:31], col(V_CB + c), MUL, ADD))
                    hs = cols[:, B_CS:B_CS + NB, 0:120].rearrange("p b (j c) -> p b j c", c=KB)[:, :, :, c]
                    tt(htmp, hs, w[:, None, 0:30].to_broadcast([P, NB, 30]), MUL)
                    red(fl8, htmp, ADD)
                    tt(oC[:, c, SEQ:T], oC[:, c, SEQ:T], fl8, ADD)
                    return
                if c in tap_at:
                    dve.wait_ge(dve_c.sem, tap_at[c])
                dve_c.by(dve.scalar_tensor_tensor(out=oC[:, c, 0:SEQ], in0=g[:, j - 1:j - 1 + SEQ], scalar=w[:, j - 1:j],
                                                  in1=oC[:, c, 0:SEQ], op0=MUL, op1=ADD))
                tap_at[c] = dve_c.n

            def reduce_page(i):
                dve.wait_ge(prod_done.sem, i + 1)
                page_free.by(dve.tensor_reduce(sc[:, i, :], kring[:, i % 4, :].rearrange("p (h d) -> p h d", h=FH), AX, ADD))

            def side(K, s):
                kind, n = s[0], s[1]
                if not dve_works(s):
                    return
                if upto(pe_works, K):
                    dve.wait_ge(pe_s.sem, upto(pe_works, K))
                if upto(act_works, K):
                    dve.wait_ge(act_s.sem, upto(act_works, K))
                av = upto(to_dve, K)

                def fin():
                    cp(fl8[:, 0:1], fl8[:, 1:2], dve_s)

                if kind == "sm" and n == 2:
                    zps = s1[:, 0:80]
                    z4 = zt[:, 0:64].rearrange("p (t c) -> p t c", t=QT)
                    tt(z4, zps[:, 0:64].rearrange("p (t c) -> p t c", t=QT), spread(bias[:, 0:16], QT, 1), ADD)
                    tt(zt[0:NB, 64:80], zps[0:NB, 64:80], bias[0:NB, 0:16], ADD)
                    stt(az[:, 0:64], zt[:, 0:64], -1.0, zt[:, 0:64], MUL, MAX)
                    stt(az[0:NB, 64:80], zt[0:NB, 64:80], -1.0, zt[0:NB, 64:80], MUL, MAX, v2a)
                    dve.wait_ge(a2v.sem, av + 1)
                    for r, at, g_, b_, f_ in ((P, 0, gtok[:, :, :], btok[:, :, :], fltok[:, :, :]),
                                              (NB, 64, zsam[0:NB, 0:4], zsam[0:NB, 4:8], zsam[0:NB, 8:16])):
                        def view(x, c0, c1):
                            if r == P:
                                return x[:, 0:64].rearrange("p (t c) -> p t c", t=QT)[:, :, c0:c1]
                            return x[0:r, at + c0:at + c1]
                        ea = bias[0:r, 16:20]
                        stt(g_, view(zt, 0, 4), 0.0, view(zl, 0, 4), MAX, ADD)
                        stt(g_, g_, -1.0, spread(ea, QT, 1) if r == P else ea, MUL, MUL)
                        ts(b_, view(zb, 4, 8), 0.5, 0.5, MUL, ADD)
                        stt(f_, view(zt, 8, 16), 0.0, view(zl, 8, 16), MIN, SUB)
                    tt(exs[0:NB, :, :], spread(zsam[0:NB, :], NB, 1), spread(ident[0:NB, 0:NB], 16, 2), MUL, dve_s)
                elif kind == "sm" and n == 3:
                    cp(bsc[:, :, :], s3[:, 0:P].rearrange("p (b c) -> p b c", b=NB))
                    cp(dcol, s2[:, 0:16])
                    cp(edl, s2[:, 16:32])
                    tt(kdf, edl, dcol, SUB, v2a)
                    cp(cneg[0:FH, :], s0[0:FH, :])
                    own(dve.tensor_tensor_scan(cneg[0:FH, :], ones[0:FH, 0:1].to_broadcast([FH, SEQ]), cneg[0:FH, :], 0.0, MUL, ADD))
                    ts(cneg[0:FH, :], cneg[0:FH, :], -1.0)
                    dve.wait_ge(a2v.sem, av + 1)
                    tt(bed, edc, btok[:, :, :].rearrange("p a b -> p (a b)"), MUL, dve_s)
                elif kind == "fox":
                    if n <= FOX:
                        w = ((n - 1) % QT + 1) * P
                        v2a.by(dve.tensor_reduce(nmx[:, 0:1], s0[:, 0:w], AX, MAX, negate=True))
                    if n >= 3:
                        h, q = divmod(n - 3, QT)
                        r = slice(FD * (h % 2), FD * (h % 2) + FD)
                        (dve_c if n <= FOX else dve_s).by(dve.tensor_copy(oD[r, h // 2, q * P:(q + 1) * P], s2[r, 0:P]))
                    if n <= FOX:
                        dve.wait_ge(a2v.sem, av + 1)
                        own(dve.reciprocal(nmx[:, 1:2], rsum[:, 0:1]))
                        ts(fP[:, 0:w], fP[:, 0:w], nmx[:, 1:2], st=dve_s)
                elif kind in ("l2", "gp"):
                    t = gx_tile(n - 1) if kind == "l2" else oB[:, n - 1, :]
                    dve.wait_ge(a2v.sem, av + 1)
                    if kind == "l2":
                        stt(t, t, P ** -0.5 if n <= 4 else 1.0, lrs, MUL, MUL, dve_s)
                    else:
                        stt(t, t, col(V_GN), lrs, MUL, MUL, dve_s)
                elif kind == "gdn":
                    c = s[2]
                    cc = slice(c * P, (c + 1) * P)
                    lv = lambda j: spread(cs(I_LVL + j), GH, 1)
                    b4 = lambda x: x.rearrange("p (a b) -> p a b", a=GH)
                    if n == 0:
                        if c == 0:
                            dve.wait_ge(ss_out, 16)
                            own(dve.memset(gS[:, :, :], 0.0))
                        for dst, op, in ((gQ, MAX), (gM, MIN)):
                            for h in range(GH):
                                (v2a if h == GH - 1 else dve_c).by(dve.tensor_scalar(
                                    dst[:, h, :], s2[:, h * P:(h + 1) * P], dcol[:, 4 * c + h:4 * c + h + 1], 0.0, SUB, op))
                        tt(gvb[:, :, :], b4(s1), spread(btok[:, c, :], P, 2), MUL)
                        dve.wait_ge(a2v.sem, av + 2)
                        tt(gqd[:, :, :], gqd[:, :, :], qkv[:, 8:12, cc], MUL, dve_s)
                    elif n == 1:
                        for h in range(GH):
                            stt(gN[:, h, :], s0[:, h * P:(h + 1) * P], btok[:, c, h:h + 1], gQ[:, h, :], MUL, MUL)
                        tt(gN[:, :, :], gN[:, :, :], spread(cs(I_NEGLOW), GH, 1), MUL)
                        tt(gM[:, :, :], gN[:, :, :], lv(0), MUL, dve_s)
                    elif n == 2:
                        tt(gQK[:, :, :], b4(s0), gXT[:, :, :], MUL)
                        tt(gQK[:, :, :], gQK[:, :, :], spread(cs(I_UP), GH, 1), MUL)
                        tt(gXT[:, :, :], b4(s1), spread(ident, GH, 1), ADD)
                        tt(gX[:, :, :], gM[:, :, :], spread(ident, GH, 1), ADD)
                        tt(gM[:, :, :], gN[:, :, :], lv(1), MUL, dve_s)
                    elif n <= 14:
                        l = n // 2 - 1
                        if l < LEVELS - 1:
                            dve_c.by(dve.tensor_tensor(gX[:, :, :], gX[:, :, :], b4(s2), ADD))
                            dve_c.by(dve.tensor_tensor(gM[:, :, :], gN[:, :, :], lv(l + 1), MUL))
                        tt(gXT[:, :, :], gXT[:, :, :], b4(s1), ADD, dve_s)
                    elif n == 17:
                        for h in range(GH):
                            (dve_s if h == GH - 1 else dve_c).by(dve.scalar_tensor_tensor(
                                out=gS[:, h, :], in0=gS[:, h, :], scalar=edl[:, 4 * c + h:4 * c + h + 1],
                                in1=s1[:, h * P:(h + 1) * P], op0=MUL, op1=ADD))
                elif kind == "cln":
                    if n == 0:
                        fin()
                    elif n == 1:
                        for c in range(KB):
                            stt(both(oC[:, c, :]), sd[:, 0:2, 0:TH], -1.0 / BD, both(oC[:, c, :]), MUL, ADD,
                                v2a if c == KB - 1 else dve_c)
                        fin()
                    else:
                        dve.wait_ge(a2v.sem, av + 1)
                        for c in range(KB):
                            tt(oC[:, c, :], oC[:, c, :], lrs, MUL)
                            ts(oC[:, c, :], oC[:, c, :], col(V_LG + c), col(V_LB + c), MUL, ADD, v2a if c == KB - 1 else dve_c)
                        for c in range(KB):
                            dve.wait_ge(a2v.sem, av + 2 + c)
                            stt(oC[:, c, :], lsq if c % 2 == 0 else lrs, 1.0, oC[:, c, :], ADD, MUL, v2a if c < 2 else dve_c)
                        fin()
                elif kind == "gs":
                    def bh(x):
                        return x.rearrange("p (b h) -> p h b", h=GH)
                    if n == 0:
                        fox_stored(dve)
                        cp(bh(kc), qkv[:, 0:4, SEQ:T])
                        cp(qkp[:, :, 0].rearrange("p (b h) -> p h b", h=GH), qkv[:, 8:12, SEQ:T])
                        cp(qkp[:, :, 1], kc)
                        cp(bh(vc), qkv[:, 4:8, SEQ:T])
                        tt(kqs, kc, qkp[:, :, 0], MUL, dve_s)
                    elif n == 2:
                        aa, bb = bsc[:, :, 0:4], bsc[:, :, 4:8]
                        b3 = lambda x: x.rearrange("p (b h) -> p b h", h=GH)
                        pr_ = s0[:, 0:64].rearrange("p (b h t) -> p b h t", h=GH, t=2)
                        tt(b3(dl), pr_[:, :, :, 1], aa, MUL)
                        tt(dl, vc, dl, SUB)
                        tt(b3(dl), b3(dl), bb, MUL)
                        tt(b3(oo), pr_[:, :, :, 0], aa, MUL)
                        tt(kqs, dl, s1[:, 0:32], MUL)
                        tt(oo, oo, kqs, ADD)
                        cp(oB[:, :, SEQ:T], bh(oo), dve_s)
                    else:
                        g = n - 3
                        if n == 3:
                            dve.wait_ge(ss_in, 16)
                            cp(drow_[0:32, :], s2[0:32, 0:P])
                            cp(krow[0:32, :], s2[0:32, P:2 * P])
                        else:
                            for h in range(GH):
                                u = 4 * (g - 1) + h
                                stt(ssam[:, u, :], ssam[:, u, :], bsc[:, g - 1, h:h + 1], s0[:, h * P:(h + 1) * P], MUL, ADD)
                        if g < NB:
                            tt(blk[0:32, :, :], spread(drow_[0:32, :], 4, 1), spread(ident[0:32, 4 * g:4 * g + 4], P, 2), MUL)
                        fin()
                elif kind == "dc":
                    if n == 0:
                        dve.wait_ge(lf_in, 16)
                        red(tot, lf[:, :, :].rearrange("p t h -> p h t"), ADD)
                        tt(totm[:, :, :], spread(tot, NB, 1), spread(cst[:, N_CST * P:N_CST * P + NB], FH, 2), MUL, dve_s)
                    elif n == 1:
                        cp(offs, s0[:, 0:FH])
                        for h in range(FH):
                            own(dve.tensor_tensor_scan(cpg[:, h, :], ones, lf[:, :, h], offs[:, h:h + 1], MUL, ADD))
                        tt(cq[:, :, :], s1[:, 0:64].rearrange("p (b h) -> p b h", b=NB), bsc[:, :, 8:16], ADD, dve_s)
                    else:
                        for j in range(2):
                            o = sc[:, :, 4 * j:4 * j + 4].rearrange("p i h -> p h i")
                            tt(o, o, sd[:, 2 + j, :].rearrange("p (h i) -> p h i", h=4), SUB)
                        o = sc[:, :, :].rearrange("p (b j) h -> p b j h", b=NB)
                        tt(o, o, cq[:, :, None, :].to_broadcast([P, NB, PAGES, FH]), ADD, dve_s)
                elif kind == "ds":
                    s4 = sc[:, :, :].rearrange("p (b j) h -> p b j h", b=NB)
                    if n == 0:
                        red(mx64[:, :, :], s4.rearrange("p b j h -> p b h j"), MAX)
                        tt(qk32[:, :, :], fs[:, 0:4, :], fs[:, 4:8, :], MUL, dve_s)
                    elif n == 1:
                        red(m1[0:64, :], s0[0:64, 0:P], MAX)
                        ts(dg64[0:64, :], ident[0:64, 0:64], m1[0:64, 0:1], st=dve_c)
                        for j in range(2):
                            cp(pn[:, :, :].rearrange("p b (c t) -> p b c t", t=2)[:, :, :, j],
                               s1[:, 32 * j:32 * j + 32].rearrange("p (c b) -> p b c", c=4), dve_s if j else dve_c)
                    elif n == 2:
                        tt(mb[:, :, :], s2[:, 0:64].rearrange("p (b h) -> p b h", b=NB), pn[:, :, :], MAX)
                        tt(pn[:, :, :], pn[:, :, :], mb[:, :, :], SUB)
                        tt(s4, s4, mb[:, :, None, :].to_broadcast([P, NB, PAGES, FH]), SUB, v2a)
                        dve.wait_ge(a2v.sem, av + 1)
                        red(rs64[:, :, :], s4.rearrange("p b j h -> p b h j"), ADD, dve_s)
                    else:
                        tt(rd64[:, :, :], s3[:, 0:64].rearrange("p (b h) -> p b h", b=NB), pn[:, :, :], ADD)
                        own(dve.reciprocal(rd64[:, :, :], rd64[:, :, :]), dve_s)
                elif kind == "df":
                    for j in range(2):
                        r = slice(FD * j, FD * j + FD)
                        o = oD[r, :, SEQ:T]
                        p4 = lambda x: x[r, :, :].rearrange("p b (c t) -> p c b t", t=2)[:, :, :, j]
                        tt(o, fs[r, 8:12, :], p4(pn), MUL)
                        tt(o, o, s3[r, 0:64].rearrange("p (b c t) -> p c b t", b=NB, t=2)[:, :, :, j], ADD)
                        tt(o, o, p4(rd64), MUL)
                    fin()
                elif kind == "ml":
                    for j in range(4):
                        cp(memT[:, 2 * j:2 * j + 2, :], sd[:, j, :].rearrange("p (k m) -> p k m", k=2), dve_s if j == 3 else dve_c)
                elif kind == "x":
                    if n <= XU:
                        own(dve.tensor_reduce(xnm[:, 0:2], s0.rearrange("p (a b) -> p a b", a=2), AX, MAX, negate=True), v2a)
                        if n >= 3:
                            q, h = (n - 3) // 2, 2 * ((n - 3) % 2)
                            cp(oX[:, h:h + 2, q * P:(q + 1) * P], s2[:, 0:2 * P].rearrange("p (a b) -> p a b", a=2))
                        dve.wait_ge(a2v.sem, av + 1)
                        own(dve.reciprocal(xnm[:, 2:4], xsum[:, 0:2]))
                        tt(xP[:, :, :], xP[:, :, :], spread(xnm[:, 2:4], MEM, 2), MUL, dve_s)
                    else:
                        q, h = (n - 3) // 2, 2 * ((n - 3) % 2)
                        cp(oX[:, h:h + 2, q * P:(q + 1) * P], s2[:, 0:2 * P].rearrange("p (a b) -> p a b", a=2), dve_s)
                    if 2 <= n <= NB + 1:
                        b = n - 2
                        dve.wait_ge(kprod.sem, b + 1)
                        red(xsc[:, b, :, :], kvc[:, b, :, :].rearrange("p t (h d) -> p t h d", h=XH), ADD, kred)
                elif kind == "xd":
                    x4_ = xsc[:, :, :, :]
                    if n == 0:
                        dve.wait_ge(kred.sem, NB)
                    if n == 0:
                        red(xmx[:, :, :], x4_.rearrange("p b t h -> p b h t"), MAX, dve_s)
                    elif n == 1:
                        red(xm1[0:32, :], s0[0:32, 0:P], MAX)
                        ts(xdg[0:32, :], ident[0:32, 0:32], xm1[0:32, 0:1], st=dve_s)
                    elif n == 2:
                        tt(x4_, x4_, s1[:, 0:32].rearrange("p (b h) -> p b h", b=NB)[:, :, None, :].to_broadcast([P, NB, 2, XH]), SUB, v2a)
                        dve.wait_ge(a2v.sem, av + 1)
                        red(xrs[:, :, :], x4_.rearrange("p b t h -> p b h t"), ADD, dve_s)
                    else:
                        own(dve.reciprocal(xrd[:, :, :].rearrange("p b h -> p (b h)"), s2[:, 0:32]))
                        for j in range(2):
                            tt(oX[:, :, SEQ:T].rearrange("p (c j) b -> p c j b", j=2)[:, :, j],
                               s3[:, 0:64].rearrange("p (b c j i) -> p c j i b", b=NB, j=2, i=2)[:, :, j, j],
                               xrd[:, :, :].rearrange("p b (c j) -> p c j b", j=2)[:, :, j], MUL, dve_s if j else dve_c)

            dve.wait_ge(pool_made.sem, 6)
            for j in range(14):
                dve.wait_ge(pro_pe.sem, j + 1)
                o = sd[:, j % 4, :]
                if j == 0:
                    src, dst = o[:, 0:KD * NB].rearrange("p (k b) -> p k b", k=KD), xT[:, :, SEQ:T]
                elif j <= KD:
                    src, dst = o, xT[:, j - 1, 0:SEQ]
                else:
                    b = 4 * (j - 9)
                    n = min(4, N_BLK - b)
                    src, dst = o[:, 0:n * P].rearrange("p (n m) -> p n m", n=n), cols[:, b:b + n, :]
                pro_dve.by(dve.tensor_copy(dst, src))
            dve.wait_ge(pro_dve.sem, 14)
            ts(cols[:, B_VEC, V_GW:V_GW + 48], cols[:, B_VEC, V_GW:V_GW + 48], 0.5)
            ts(cols[:, B_VEC, V_LG:V_LG + 8], cols[:, B_VEC, V_LG:V_LG + 8], 0.5)
            ts(cols[:, B_FW, 0:66], cols[:, B_FW, 0:66], 0.5)
            dve.wait_ge(wsm_hi.sem, 1)
            tt(wsl[:, :, :], wsm[:, :, :], wsh[:, :, :].bitcast(F32), SUB, wsm_lo)
            spl = [0]
            for e in TIMELINE:
                if e[0] == "nsum":
                    dve.wait_ge(n_rt.sem, e[1] + 1)
                elif e[0] == "napply":
                    i = e[1]
                    norm_apply(i, e[2], memT if i == 1 else xT, MEM if i == 1 else T, [V_MIX, V_MEM, V_CROSS, V_FFN, V_FIN][i])
                elif e[0] in ("evac", "evac2") and dve_tile[e[1]]:
                    evac(e[1], e[0] == "evac2")
                elif e[0] == "split":
                    src, n = {"brC": (oC, 4), "brB": (oB, 4), "brD": (oD, 4), "brX": (oX, 4), "merged": (xT, 8)}[e[1]]
                    for k in range(n):
                        dve.wait_ge(sp_hi.sem, spl[0] + 1)
                        tt((xl if n == 8 else ol)[:, k, :], src[:, k, :], (xh if n == 8 else oh)[:, k, :].bitcast(F32), SUB, sp_lo)
                        spl[0] += 1
                elif e[0] == "side":
                    side(e[1], e[2])
                elif e[0] == "tap":
                    tap(e[1])
                elif e[0] == "k" and e[1] > 0:
                    reduce_page(e[1] - 1)
                elif e[0] == "kend":
                    reduce_page(N_PAGE - 1)


_INS = ["x_prompt", "x_sample", "cache_fox_k", "cache_fox_v", "cache_fox_logf", "cache_mem_k", "cache_mem_v",
        "state_sconv", "state_gdn_conv", "state_gdn", "state_conf_conv", "state_ffn_conv", "page_table", "mem_prompt",
        "norm_mix", "w_in", "w_branch", "w_out", "sconv_w", "gdn_conv_w", "gdn_a_log", "gdn_dt_bias", "gdn_norm",
        "conf_dw_w", "conf_dw_b", "conf_ln_g", "conf_ln_b", "fox_fbias", "norm_cross", "norm_mem", "w_cq", "w_ckv", "w_co",
        "norm_ffn", "w_ffn_in", "ffn_conv_w", "w_ffn_out", "norm_final"]
_OUTS = [("y_p", (1, SEQ, D)), ("y_s", (NB, 1, D)),
         ("fk_p", (1, SEQ, 1, FH, FD)), ("fv_p", (1, SEQ, 1, FH, FD)), ("fl_p", (1, SEQ, 1, FH)),
         ("mk_p", (1, 1, MEM, XH, P)), ("mv_p", (1, 1, MEM, XH, P)),
         ("sc_p", (1, 1, SCW - 1, BD)), ("gc_p", (1, 1, GCW - 1, 3 * BD)), ("S_p", (1, 1, GH, P, P)),
         ("cf_p", (1, 1, CFW - 1, BD)), ("ff_p", (1, 1, FCW - 1, FF)),
         ("fk_s", (NB, 1, 1, FH, FD)), ("fv_s", (NB, 1, 1, FH, FD)), ("fl_s", (NB, 1, 1, FH)),
         ("sc_s", (NB, 1, SCW - 1, BD)), ("gc_s", (NB, 1, GCW - 1, 3 * BD)), ("S_s", (NB, 1, GH, P, P)),
         ("cf_s", (NB, 1, CFW - 1, BD)), ("ff_s", (NB, 1, FCW - 1, FF))]


def kernel(**inputs):
    import concourse.bacc as bacc
    from concourse.bass_utils import run_bass_kernel_spmd

    nc = bacc.Bacc("TRN2", target_bir_lowering=False, num_devices=1, dynamic_dma_scratch_size=1024)
    arrays, a, out = {}, {}, {}
    for name in _INS:
        x = np.ascontiguousarray(inputs[name])
        arrays[f"in_{name}"] = x
        a[name] = nc.dram_tensor(f"in_{name}", x.shape, mybir.dt.from_np(x.dtype), kind="ExternalInput").ap()
    r = np.arange(P)[:, None]
    arrays["in_cst"] = np.concatenate([constants(), (r // PAGES == np.arange(NB)[None]).astype(np.float32)], axis=1)
    a["cst"] = nc.dram_tensor("in_cst", arrays["in_cst"].shape, F32, kind="ExternalInput").ap()
    for name, shape in _OUTS:
        out[name] = nc.dram_tensor(f"out_{name}", shape, F32, kind="ExternalOutput").ap()
    build(nc, a, out)
    res = run_bass_kernel_spmd(nc, [arrays], core_ids=[0])
    return tuple(res.results[0][f"out_{name}"] for name, _ in _OUTS)
```

```python
from contextlib import ExitStack

import numpy as np

import concourse.bass as bass
from concourse import mybir

F32 = mybir.dt.float32
F32R = mybir.dt.float32r
I32 = mybir.dt.int32
ALU = mybir.AluOpType
ACT = mybir.ActivationFunctionType
AX = mybir.AxisListType.X
MUL, ADD, SUB, MAX, MIN = ALU.mult, ALU.add, ALU.subtract, ALU.max, ALU.min

P = 128
D = 1024
KD = D // P
SEQ, NB = 512, 8
T = SEQ + NB
TH = T // 2
QT = SEQ // P
BD = 512
KB = BD // P
SCW, GCW, CFW, FCW = 3, 4, 31, 3
GH = 4
FH, FD = 8, 64
XH = 4
MEM = 256
FF = 2816
KF = FF // P
PAGES = 16
NEG = -1e30
LEVELS = 7

C_AH, C_AB, C_AC, C_GQ = 0, BD, 2 * BD, 3 * BD
C_GZ = 6 * BD
C_GA = 7 * BD
C_CV = C_GA + 2 * GH
C_CG = C_CV + BD
C_FQ = C_CG + BD
C_FF = C_FQ + 3 * BD
C_GATE = C_FF + FH

(I_ID, I_ONE, I_UP, I_NEGLOW, I_CAUSAL, I_LO, I_HI, I_PAGE, I_LVL) = range(9)
N_CST = I_LVL + LEVELS

V_MIX, V_CROSS, V_FFN, V_FIN, V_MEM, V_CB, V_LG, V_LB, V_GN, V_SW, V_GW = 0, 8, 16, 24, 32, 40, 44, 48, 52, 53, 65
B_VEC, B_CW, B_FW, B_SS, B_GS, B_CS, B_FS = 0, 1, 2, 3, 4, 8, 16
N_BLK = 20


def constants():
    r, c = np.arange(P)[:, None], np.arange(P)[None, :]
    out = np.zeros((P, N_CST, P), np.float32)
    out[:, I_ID] = r == c
    out[:, I_ONE] = 1.0
    out[:, I_UP] = r <= c
    out[:, I_NEGLOW] = -(r > c).astype(np.float32)
    out[:, I_CAUSAL] = np.where(c > r, np.float32(NEG), np.float32(0))
    out[:, I_LO] = r < FD
    out[:, I_HI] = r >= FD
    out[:, I_PAGE] = (r // PAGES == c // PAGES) & (r < c)
    for n in range(LEVELS):
        s = 1 << n
        out[:, I_LVL + n] = (r // (2 * s) == c // (2 * s)) & ((r // s) % 2 == 1) & ((c // s) % 2 == 0)
    return out.reshape(P, N_CST * P)


def plan():
    units, pieces = [], []

    def unit(w, row, kt, col, kind, idx, first=True, last=True):
        units.append((w, row, kt, col))
        for h in range(2):
            pieces.append((len(units) - 1, h, kt, kind, idx + h, first, last))

    for n, kind in enumerate(("fq", "fk", "fv")):
        for h in range(2):
            unit("w_in", 0, KD, C_FQ + n * BD + h * 256, kind, 2 * h)
    for h in range(2):
        unit("w_in", 0, KD, C_CV + h * 256, "cv", 2 * h)
        unit("w_in", 0, KD, C_CG + h * 256, "cg", 2 * h)
    for h in range(2):
        unit("w_in", 0, KD, C_AC + h * 256, "ac", 2 * h)
        unit("w_in", 0, KD, C_AH + h * 256, "ah", 2 * h)
        unit("w_in", 0, KD, C_AB + h * 256, "ab", 2 * h)
    for n in range(6):
        unit("w_in", 0, KD, C_GQ + n * 256, "gx", 2 * n)
    for n, br in enumerate("ACDB"):
        if br == "B":
            for h in range(2):
                unit("w_in", 0, KD, C_GZ + h * 256, "gz", 2 * h)
        b = "ABCD".index(br)
        for h in range(4):
            unit("w_in", 0, KD, C_GATE + b * D + h * 256, "gate" + br, 2 * h)
            unit("w_branch", b * BD, KB, h * 256, "br" + br, 2 * h)
    for h in range(4):
        unit("w_out", 0, KD, h * 256, "wo", 2 * h)
    for h in range(4):
        unit("w_ckv", 0, KD, h * 256, "kv", 2 * h)
    for h in range(2):
        unit("w_cq", 0, KD, h * 256, "cq", 2 * h)
    for h in range(4):
        unit("w_co", 0, KB, h * 256, "co", 2 * h)
    for h in range(KF // 2):
        unit("w_ffn_in", 0, KD, h * 256, "fg", 2 * h)
        unit("w_ffn_in", 0, KD, FF + h * 256, "fu", 2 * h)
    for h in range(4):
        for k in range(0, KF, KD):
            unit("w_ffn_out", k * P, min(KD, KF - k), h * 256, "fo", 2 * h, k == 0, k + KD >= KF)
    return units, pieces


UNITS, PIECES = plan()
NP_ = len(PIECES)
LOW_BY_DVE = ("kv", "cq")
PIECE_MT = []
MT_LAST = []
for _p, (_u, _h, _k, _kind, _idx, _first, _last) in enumerate(PIECES):
    if _first:
        PIECE_MT.append(len(MT_LAST))
        MT_LAST.append(_p)
    else:
        PIECE_MT.append(PIECE_MT[_p - 2])
        MT_LAST[PIECE_MT[_p]] = _p
BY_ACT = {"fq", "fk", "fv", "cv", "cg", "gx", "ac", "gateA", "gateB", "gateC", "gateD", "gz", "kv", "cq", "fg"}
MT_KIND = [PIECES[p][3] for p in MT_LAST]
MT_ACT = [k in BY_ACT for k in MT_KIND]


def first_piece(kind):
    return min(p for p, x in enumerate(PIECES) if x[3] == kind)


def last_piece(kind):
    return max(p for p, x in enumerate(PIECES) if x[3] == kind)


FOX = 4 * FH
XU = QT * XH // 2
TAPS_TICK, K_EARLY, K_LATE = 2, 1, (2, 2)
V_FILLED, V_BARE = 2, 2
SIDE = ([("AFTER", "fq")] + [("sm", n) for n in range(4)]
        + [("AFTER", "fv")]
        + [("fst", n) for n in range(4)] + [("KSTART",)]
        + [("fvt", n) for n in range(5)] + [("fkt", n) for n in range(5)]
        + [("fox", n) for n in range(FOX + 3)]
        + [x for n in range(4) for x in (("AFTER", "gx", 2 * n + 1), ("l2", n))] + [("l2", 4)]
        + [("AFTER", "gx")]
        + [("gs", n) for n in range(13)]
        + [("TAPS",)]
        + [("cln", n) for n in range(7)] + [("BEFORE", "gateC")]
        + [("gdn", n, 0) for n in range(-1, 12)]
        + [("REDUCES",)]
        + [("gdn", n, 0) for n in range(12, 18)]
        + [("dc", n) for n in range(3)] + [("ds", n) for n in range(4)] + [("VSTART",)]
        + [("gdn", n, c) for c in range(1, 4) for n in range(-1, 18)]
        + [("gp", n) for n in range(5)]
        + [("PAGES",), ("df", 0), ("df", 1)] + [("BEFORE", "gateD")]
        + [("ex", n) for n in range(6)] + [("ml", n) for n in range(3)] + [("BEFORE", "wo")]
        + [("AFTER", "cq")]
        + [("xm", n) for n in range(3)] + [("x", n) for n in range(XU + 3)] + [("xd", n) for n in range(4)]
        + [("BEFORE", "co")]
        + [("AFTER", "fu")] + [("ef", n) for n in range(7)]
        + [("BEFORE", "END")] + [("y", n) for n in range(6)])


MARKS = ("AFTER", "BEFORE", "TAPS", "REDUCES", "KSTART", "VSTART", "PAGES")
N_TAP = KB * CFW
N_PAGE = PAGES * NB


def timeline():
    out, pos, step_n, tile, at_piece, bg = [], [0], [0], [0], [-1], {"tap": None, "k": None, "v": None}
    size = {"tap": N_TAP, "k": N_PAGE, "v": N_PAGE}

    def background(kind, n):
        for done in range(n):
            if bg[kind] is not None and bg[kind] < size[kind]:
                if kind == "v" and bg[kind] % PAGES == 0 and done > 0 and n < 10:
                    return
                out.append((kind, bg[kind]))
                bg[kind] += 1

    def step(done, filled=True):
        while pos[0] < len(SIDE):
            s = SIDE[pos[0]]
            if s[0] == "AFTER":
                if done <= (last_piece(s[1]) if len(s) == 2 else first_piece(s[1]) + s[2]) + 1:
                    return
            elif s[0] in ("TAPS", "REDUCES", "PAGES"):
                background({"TAPS": "tap", "REDUCES": "k", "PAGES": "v"}[s[0]], 10 ** 6)
                if s[0] == "REDUCES":
                    out.append(("kend",))
            elif s[0] == "KSTART":
                bg["k"] = 0
                out.append(("kstart",))
            elif s[0] == "VSTART":
                bg["v"] = 0
                out.append(("vstart",))
            elif s[0] != "BEFORE":
                background("v", V_FILLED if filled else V_BARE)
                out.append(("side", step_n[0], s))
                step_n[0] += 1
                pos[0] += 1
                return
            elif s[1] == "END":
                return
            pos[0] += 1

    def evac(upto_piece):
        while tile[0] < len(MT_LAST) and MT_LAST[tile[0]] <= upto_piece:
            out.append(("evac", tile[0]))
            out.append(("evac2", tile[0]))
            tile[0] += 1

    def through(mark):
        at = SIDE.index(mark)
        if pos[0] <= at and any(s[0] == "AFTER" for s in SIDE[pos[0]:at]):
            evac(at_piece[0])
        while pos[0] < at and any(s[0] not in ("AFTER", "BEFORE") for s in SIDE[pos[0]:at]):
            step(10 ** 6, False)

    def norm(i, squares=True):
        if squares:
            out.extend(("nsq", i, k) for k in range(KD))
        out.append(("nroot", i))
        out.extend(("napply", i, k) for k in range(KD + (i != 4)))

    norm(0)
    for p in range(NP_):
        kind = PIECES[p][3]
        if p == first_piece(kind) and ("BEFORE", kind) in SIDE:
            through(("BEFORE", kind))
        if kind in ("wo", "kv", "co", "fg", "fo") and p == first_piece(kind):
            evac(p - 1)
        if p == first_piece("wo"):
            out.append(("split", "merged"))
        if p == first_piece("kv"):
            out.append(("nsq", 2, KD - 1))
            out.append(("nroot", 2))
        if p == first_piece("co"):
            out.append(("split", "brX"))
        if p == first_piece("fg"):
            out.append(("nsq", 3, KD - 1))
            norm(3, False)
        if bg["tap"] is None and p > last_piece("cg") + 1:
            bg["tap"] = 0
        for h in range(2):
            at_piece[0] = p - 1 + h
            out.append(("piece", p, h))
            if kind in ("gateC", "gateB", "gateD") and p == first_piece(kind) and h == 0:
                evac(p - 1)
                out.append(("split", "br" + kind[-1]))
            step(p)
            if h == 0:
                evac(p - 1)
            if kind == "wo":
                j = 2 * (p - first_piece("wo")) + h
                if j < 4:
                    out.extend(("nsq", 1, k) for k in (2 * j, 2 * j + 1))
                elif j == 4:
                    out.append(("nroot", 1))
                elif j < 14:
                    out.append(("napply", 1, j - 5))
                if j >= 9:
                    out.append(("nsq", 2, j - 9))
            if kind == "co" and h == 1 and p > first_piece("co"):
                out.append(("nsq", 3, p - first_piece("co") - 1))
            if kind == "fo" and h == 1 and MT_LAST[tile[0] - 1] == p - 1 and MT_KIND[tile[0] - 1] == "fo":
                out.append(("nsq", 4, PIECES[p - 1][4]))
            if kind == "kv" and h == 1:
                out.append(("napply", 2, p - first_piece("kv")))
                if p == last_piece("kv"):
                    out.append(("napply", 2, KD))
            background("tap", TAPS_TICK)
            background("k", K_EARLY if p < first_piece("gateA") else K_LATE[h])
    evac(NP_ - 1)
    through(("BEFORE", "END"))
    pos[0] = SIDE.index(("BEFORE", "END")) + 1
    out.append(("nsq", 4, KD - 1))
    norm(4, False)
    for n in range(pos[0], len(SIDE)):
        step(10 ** 6)
    return out


TIMELINE = timeline()
ITEMS = [e[2] for e in TIMELINE if e[0] == "side"]
assert len(ITEMS) == len([s for s in SIDE if s[0] not in MARKS])
assert [e[1] for e in TIMELINE if e[0] == "k"] == list(range(N_PAGE))
assert [e[1] for e in TIMELINE if e[0] == "v"] == list(range(N_PAGE))
assert TIMELINE.index(("tap", N_TAP - 1)) < TIMELINE.index(("piece", first_piece("brA") + 6, 0))


def pe_works(s):
    kind, n = s[0], s[1]
    return n < {"sm": 3, "fst": 3, "fvt": 4, "fkt": 4, "fox": FOX + 2, "l2": 4, "gdn": 17, "cln": 5, "gp": 4, "dc": 2,
                "ds": 3, "df": 1, "ex": 5, "xm": 2, "x": XU + 2, "xd": 3, "ef": 6, "y": 5,
                "gs": 11, "ml": 2}[kind] and not (kind in ("gs", "ml") and n == 0)


def act_works(s):
    kind, n = s[0], s[1]
    if kind in ("sm", "fst", "fvt", "fkt", "ex", "ef", "y", "fox"):
        return n > 0
    if kind == "gdn":
        return n == 0 or n >= 3 and n % 2 == 1 or n == 16
    if kind == "ds":
        return n == 2
    if kind == "x":
        return n > 0 and n < XU + 2
    if kind == "xm":
        return n > 0
    if kind == "xd":
        return n == 2
    if kind == "cln":
        return n > 0
    return kind in ("l2", "gp")


def dve_works(s):
    kind, n = s[0], s[1]
    if kind == "gdn":
        return n in (0, 1, 17) or n <= 14 and n >= 2 and n % 2 == 0
    if kind in ("fox", "l2", "gp", "x"):
        return n > 0
    if kind == "sm":
        return n > 1
    if kind == "df":
        return n == 1
    if kind == "gs":
        return n < 12 and n != 1
    if kind == "cln":
        return n in (0, 1, 5, 6)
    if kind == "ml":
        return n == 2
    return kind in ("dc", "ds", "df", "xd")


def to_act(s):
    kind, n = s[0], s[1]
    if kind == "fox":
        return int(1 <= n <= FOX)
    if kind == "x":
        return int(1 <= n <= XU)
    return {("sm", 2): 1, ("sm", 3): 2, ("gdn", 0): 2, ("cln", 1): 1, ("cln", 6): 2, ("ds", 2): 1, ("xd", 2): 1}.get((kind, n), 0)


def to_dve(s):
    kind, n = s[0], s[1]
    if kind == "fox":
        return int(1 <= n <= FOX)
    if kind == "x":
        return int(1 <= n <= XU)
    if kind == "l2" or kind == "gp":
        return int(n > 0)
    return {("sm", 2): 1, ("sm", 3): 2, ("gdn", 0): 2, ("cln", 5): 1, ("cln", 6): 4, ("ds", 2): 1, ("xd", 2): 1}.get((kind, n), 0)


def upto(what, k):
    return sum(int(what(s)) for s in ITEMS[:k])


class Stage:

    def __init__(self, sem):
        self.sem, self.n = sem, 0

    def by(self, ins):
        ins.then_inc(self.sem, 1)
        self.n += 1


def build(nc, a, out):
    ctx = ExitStack()
    with ctx:
        def sb(name, shape, dt=F32):
            return ctx.enter_context(nc.sbuf_tensor(name, shape, dt))

        def ps(name, shape):
            return ctx.enter_context(nc.psum_tensor(name, shape, F32))

        def sem(name):
            return ctx.enter_context(nc.semaphore(name))

        def stage(name):
            return Stage(sem(name))

        cst = sb("cst", [P, N_CST * P + NB])
        cols = sb("cols", [P, N_BLK, P])
        xT_at = -(-nc.sbuf_base // 32) * 32
        xT = sb("xT", [P, KD, T])
        xh_at = -(-nc.sbuf_base // 32) * 32
        xh, xl = sb("xh", [P, KD, T], F32R), sb("xl", [P, KD, T], F32R)
        oh, ol = sb("oh", [P, KB, T], F32R), sb("ol", [P, KB, T], F32R)
        raw = sb("raw", [P, 2, KD, 256])
        wh, wl = sb("wh", [P, 2, KD, P], F32R), sb("wl", [P, 2, KD, P], F32R)
        OD, OB, OC, QKV, G, DEC = 0, 2080, 4160, 6240, 12480, 18624
        DEC_N = 4 * 512 + 512 + PAGES * NB * FH
        SQ = DEC + DEC_N
        PR = SQ + 2 * T
        SM = PR + 4 * T + 2 * 524 + T
        ptr_, ptc = sb("ptr", [1, PAGES * NB], I32), sb("ptc", [P, 1], I32)
        base = -(-nc.sbuf_base // 32) * 32
        ar = sb("ar", [P, SM + 694])

        def v(at, *shape):
            n = int(np.prod(shape))
            x = ar[:, at:at + n]
            if len(shape) == 2:
                x = x.rearrange("p (a b) -> p a b", a=shape[0])
            if len(shape) == 3:
                x = x.rearrange("p (a b c) -> p a b c", a=shape[0], b=shape[1])
            return x

        oD, oB, oC = v(OD, KB, T), v(OB, KB, T), v(OC, KB, T)
        qkv = v(QKV, 12, T)
        fq, fk, fv = qkv[:, 0:4, :], qkv[:, 4:8, :], qkv[:, 8:12, :]

        def gx_tile(n):
            return qkv[:, (8 + n) % 12, :]

        kring = v(DEC, 4, 512)
        qb = v(DEC + 2048, 512)
        sc = v(DEC + 2560, PAGES * NB, FH)
        lsq, lrs = v(SQ, T), v(SQ + T, T)
        lsq2, lrs2 = v(SQ, 2, T), v(G + 4096, 2, T)
        pairA, pairB = v(PR, 2, T), v(PR + 2 * T, 2, T)
        cb = v(PR + 4 * T, 2, 524)
        tmp = v(PR + 4 * T + 1048, T)
        sm_at = [SM]

        def small(n, *shape):
            at = sm_at[0]
            sm_at[0] += n
            assert sm_at[0] <= SM + 694
            return v(at, *(shape or (n,)))

        glu = xT[:, :, :].rearrange("p a b -> p (a b)")[:, KD * T - 4 * 550:].rearrange("p (a b) -> p a b", a=4)
        tail_gx, tail_cf = small(132, 12, 11), small(152, 4, 38)
        tail_sc = cols[:, B_SS, 64:104].rearrange("p (a b) -> p a b", a=KB)
        fs = small(96, 12, 8)
        gtok, btok = small(16, 4, 4), small(16, 4, 4)
        fltok = small(32, 4, 8)
        zsam = small(16)
        bsc = small(128, 8, 16)
        bias = small(20)
        eps6, eps5 = small(1), small(1)
        dcol, edc, edl, kdf, bed = (small(16) for _ in range(5))
        nmx, rsum = small(2), small(2)
        fl8 = cols[:, B_SS, 104:112]
        htmp = v(PR + 4 * T + 1048, NB, 30)

        ident, ones = cst[:, 0:P], cst[:, P:2 * P]

        def cs(n):
            return cst[:, n * P:(n + 1) * P]

        def col(n):
            return cols[:, B_VEC, n:n + 1]

        pb = ps("pb", [P, 2, 2, 512])
        sd = ps("sd", [P, 4, 512])
        s0, s1, s2, s3 = (sd[:, n, :] for n in range(4))

        xscr = nc.dram_tensor("x_scratch", (P, KD * T), F32, kind="Internal").ap()
        vscr = nc.dram_tensor("v_scratch", (NB * FH * (512 + FD),), F32, kind="Internal").ap()
        qscr = nc.dram_tensor("q_scratch", (NB, 512), F32, kind="Internal").ap()

        id_in = sem("id_in")
        par_in, x_in, small_in, mem_in, lf_in, pt_in = (sem(n) for n in (
            "par_in", "x_in", "small_in", "mem_in", "lf_in", "pt_in"))
        raw_in = [sem(f"raw_in{n}") for n in range(2)]
        page_in = [sem(f"page_in{n}") for n in range(4)]
        qb_in, xs_out, xs_in, qs_out = sem("qb_in"), sem("xs_out"), sem("xs_in"), sem("qs_out")
        out_sem = sem("out_sem")
        stg_out = [sem(f"stg_out{n}") for n in range(2)]
        ss_in, ss_out, mv_in = sem("ss_in"), sem("ss_out"), [sem(f"mv_in{n}") for n in range(2)]
        pool_c, act_c, dve_c = stage("pool_chain"), stage("act_chain"), stage("dve_chain")
        pool_made = stage("pool_made")
        hi, lo = stage("hi_ready"), stage("lo_ready")
        piece_done, mt_act, mt_dve = stage("piece_done"), stage("mt_act"), stage("mt_dve")
        ev_y, ev_t, ev_all = stage("conv_ready"), stage("act_second"), stage("dve_tile_done")
        pe_s, act_s, dve_s = stage("pe_side"), stage("act_side"), stage("dve_side")
        v2a, a2v = stage("dve_to_act"), stage("act_to_dve")
        prod_done, page_free, v_used = stage("prod_done"), stage("page_free"), stage("v_used")
        n_sq, n_pe, n_rt, n_tmp, n_hi = (stage(n) for n in ("norm_sq", "norm_pe", "norm_root", "norm_tmp", "norm_hi"))
        n_lo, sp_hi, sp_lo = stage("norm_lo"), stage("split_hi"), stage("split_lo")
        wsm_hi, wsm_lo, v_rows = stage("gate_weights_hi"), stage("gate_weights_lo"), stage("v_rows")
        vs_out, v64_in = [sem(f"vs_out{n}") for n in range(2)], sem("v64_in")
        dve_v = stage("dve_other")
        kprod, kred, q8_in = stage("k_times_q"), stage("k_reduced"), sem("q8_in")
        pro_pe, pro_dve = stage("pro_pe"), stage("pro_dve")
        ss_st, vt_out, gs_out, mk_in = sem("row_stores"), sem("vt_out"), sem("gs_out"), sem("mk_in")
        side_at, out_total = [0], [16 * (8 + QT + 1)]
        mt_a = [sum(MT_ACT[:m + 1]) for m in range(len(MT_ACT))]
        mt_d = [m + 1 - mt_a[m] for m in range(len(MT_ACT))]
        dve_tile = [k in ("cg", "gx", "ac", "ah", "ab", "gz", "wo", "co", "fg", "fu", "fo") and k != "ac" or k.startswith("br")
                    for k in MT_KIND]
        conv_tile = [k in ("gx", "fg") for k in MT_KIND]
        second_tile = [k in ("gx", "fg", "ab", "fu") for k in MT_KIND]

        def count(flags, m):
            return sum(int(x) for x in flags[:m + 1])

        def mt_of(kind, idx=None):
            return max(m for m, k in enumerate(MT_KIND) if k == kind and (idx is None or PIECES[MT_LAST[m]][4] == idx))

        pv = v(QKV, N_BLK, P)
        xrow = v(0, 5, D)
        wsm = v(G, KD, 16)
        wsh = nc.alloc_sbuf_tensor_at("wsh", [P, KD, 16], F32R, offset=base + 4 * (G + 128))
        wsl = nc.alloc_sbuf_tensor_at("wsl", [P, KD, 16], F32R, offset=base + 4 * (G + 256))
        zrow = v(G + 1024, T)
        vt = v(G, QT, 512)
        fP, fPT = v(G + 2048, 512), v(G + 2560, QT, P)
        stg = v(G + 4096, 2, 512)
        cnh = nc.alloc_sbuf_tensor_at("cnh", [P, 512], F32R, offset=base + 4 * (G + 5632))
        cnl = nc.alloc_sbuf_tensor_at("cnl", [P, 512], F32R, offset=base + 4 * (G + 5120))
        mask_r = nc.alloc_sbuf_tensor_at("mask_r", [P, 2, P], F32R, offset=xT_at)
        cneg, srow = v(G + 5120, 512), v(G + 3072, 2, 512)
        gR, gkd, gvb, gQK, gqd, gN, gX, gXT, gQ, gM, gW, gS = (v(G + 512 * n, GH, P) for n in range(12))
        ssam = v(G, NB * GH, P)
        g2 = G + 4096
        kc, qkp, vc, kqs, dl, oo = (v(g2, 32), v(g2 + 32, 32, 2), v(g2 + 96, 32), v(g2 + 128, 32), v(g2 + 160, 32), v(g2 + 192, 32))
        krow, drow_, blk = v(g2 + 256, P), v(g2 + 384, P), v(g2 + 512, 4, P)
        lf, cpg = v(DEC, P, FH), v(DEC + 1024, FH, P)
        g3 = DEC + 2048
        tot, totm, offs, cq = v(g3, 8), v(g3 + 8, NB, FH), v(g3 + 72, 8), v(g3 + 80, NB, FH)
        qk32, m1, pn, rd64 = v(g3 + 144, 4, NB), v(g3 + 176, 1), v(g3 + 192, NB, FH), v(g3 + 256, NB, FH)
        vrow, v64 = cb[:, :, 3:515], v(g3, 2, FD)
        mx64, mb, rs64, dg64 = v(g3 + 320, NB, FH), v(g3 + 384, NB, FH), v(g3 + 448, NB, FH), v(SQ, 64)
        mkT, mvT, mv = v(0, XH, MEM), v(1024, XH, MEM), v(2048, 2, 512)
        qc, oX = v(3072, XH, T), v(5152, XH, T)
        memT, mrow = v(7744, KD, MEM), v(9792, 2, D)
        xP, xPT = v(7744, 2, MEM), v(8256, 4, P)
        kvc = v(11840, NB, 2, 512)
        xstg, qrow = v(20032, 2, 512), v(21056, 512)
        xsc = v(21568, NB, 2, XH)
        x4 = 21632
        xmx, xm1, xdg, xrs, xrd = v(x4, NB, XH), v(x4 + 32, 1), v(x4 + 64, 32), v(x4 + 96, NB, XH), v(x4 + 128, NB, XH)
        xnm, xsum = v(x4 + 160, 4), v(x4 + 164, 2)
        mstg = v(PR + 4 * T, 2, 512)
        qx = nc.alloc_sbuf_tensor_at("qx", [P, NB, 512], F32, offset=xh_at)
        ystg = v(0, QT + 1, 2, 512)
        tail_ff = v(SM, KF, 10)
        hh = nc.alloc_sbuf_tensor_at("hh", [P, KF, T], F32R, offset=base)
        hl = nc.alloc_sbuf_tensor_at("hl", [P, KF, T], F32R, offset=base + 4 * T * KF)

        def sel(h):
            return mask_r[0:NB, 0, h:h + 1].to_broadcast([NB, P])

        sqb = pairA
        memh = oh[:, :, :].rearrange("p a b -> p (a b)")[:, 0:KD * MEM].rearrange("p (a b) -> p a b", a=KD)
        meml = ol[:, :, :].rearrange("p a b -> p (a b)")[:, 0:KD * MEM].rearrange("p (a b) -> p a b", a=KD)
        zt, az, zl, zb, exs = v(SQ, 80), v(SQ + 80, 80), v(SQ + 160, 80), v(SQ + 240, 80), v(SQ + 320, NB, 16)
        exports = {
            "ex": [(tail_gx, 4 * j, 4, 11, 3, out["gc_p"][0, 0, :, 512 * j:512 * j + 512],
                    out["gc_s"][:, 0, GCW - 2, 512 * j:512 * j + 512]) for j in range(3)]
            + [(tail_sc, 0, 4, 10, 2, out["sc_p"][0, 0], out["sc_s"][:, 0, SCW - 2]),
               (tail_cf, 0, 4, 38, 30, out["cf_p"][0, 0], out["cf_s"][:, 0, CFW - 2])],
            "ef": [(tail_ff, 4 * j, min(4, KF - 4 * j), 10, 2, out["ff_p"][0, 0, :, 512 * j:min(512 * (j + 1), FF)],
                    out["ff_s"][:, 0, FCW - 2, 512 * j:min(512 * (j + 1), FF)]) for j in range(6)]}

        def both(x):
            return x.rearrange("p (a b) -> p a b", a=2)

        def bulk(m):
            return pb[:, m % 2, :, 0:TH]

        def spread(x, n, axis):
            return x[:, None, :].to_broadcast([x.shape[0], n, x.shape[1]]) if axis == 1 else \
                x[:, :, None].to_broadcast([x.shape[0], x.shape[1], n])

        def fox_stored(eng):
            eng.wait_ge(qs_out, 16)
            eng.wait_ge(ss_st, 32)
            eng.wait_ge(vt_out, 64)
            for b in range(2):
                eng.wait_ge(stg_out[b], 32)

        W = {"w_in": a["w_in"][0], "w_branch": a["w_branch"][0].rearrange("i r c -> (i r) c"), "w_out": a["w_out"][0],
             "w_ckv": a["w_ckv"][0], "w_cq": a["w_cq"][0], "w_co": a["w_co"][0], "w_ffn_in": a["w_ffn_in"][0],
             "w_ffn_out": a["w_ffn_out"][0]}

        block = ctx.enter_context(nc.Block())

        @block.sync
        def _(sp):
            sp.dma_start(cst[:, 0:2 * P], a["cst"][:, 0:2 * P]).then_inc(id_in, 16)
            for t in range(QT):
                sp.dma_start(xrow[:, t, :], a["x_prompt"][0, t * P:(t + 1) * P, :]).then_inc(x_in, 16)
            sp.dma_start(xrow[0:NB, QT, :], a["x_sample"].rearrange("b t d -> (b t) d")).then_inc(x_in, 16)
            sp.dma_start(cst[:, 2 * P:], a["cst"][:, 2 * P:]).then_inc(par_in, 16)
            sp.wait_ge(pool_made.sem, 1)
            rows = [(V_MIX, "norm_mix"), (V_CROSS, "norm_cross"), (V_FFN, "norm_ffn"), (V_MEM, "norm_mem"),
                    (V_CB, "conf_dw_b"), (V_LG, "conf_ln_g"), (V_LB, "conf_ln_b"), (V_GN, "gdn_norm")]
            for at, name in rows:
                src = a[name].rearrange("l (r c) -> (l r) c", c=P)
                sp.dma_start(pv[at:at + src.shape[0], B_VEC, :], src).then_inc(par_in, 16)
            sp.dma_start(pv[V_FIN:V_FIN + 8, B_VEC, :], a["norm_final"].rearrange("(r c) -> r c", c=P)).then_inc(par_in, 16)
            for at, b, name in ((V_SW, B_VEC, "sconv_w"), (V_GW, B_VEC, "gdn_conv_w"), (0, B_CW, "conf_dw_w"),
                                (0, B_FW, "ffn_conv_w")):
                src = a[name].rearrange("l w (r c) -> (l w r) c", c=P)
                sp.dma_start(pv[at:at + src.shape[0], b, :], src).then_inc(par_in, 16)
            for b, n, name in ((B_SS, 1, "state_sconv"), (B_GS, 4, "state_gdn_conv"), (B_CS, 8, "state_conf_conv"),
                               (B_FS, 4, "state_ffn_conv")):
                src = a[name].rearrange("b l w (r c) -> (b l w r) c", c=P)
                m = src.shape[0] // n
                sp.dma_start(pv[0:m, b:b + n, :], src.rearrange("(n m) c -> m n c", n=n)).then_inc(par_in, 16)
            with nc.allow_non_contiguous_dma(reason="16 columns of w_in, and vectors read by all partitions"):
                sp.wait_ge(pool_made.sem, 2)
                sp.dma_start(bias[:, 0:4], a["gdn_dt_bias"].to_broadcast([P, 4])).then_inc(small_in, 16)
                sp.dma_start(bias[:, 8:16], a["fox_fbias"].to_broadcast([P, 8])).then_inc(small_in, 16)
                sp.dma_start(bias[:, 16:20], a["gdn_a_log"].to_broadcast([P, 4])).then_inc(small_in, 16)
            def unit(u):
                w, row, kt, c = UNITS[u]
                if u >= 2:
                    sp.wait_ge(lo.sem, 2 * u - 2)
                sp.dma_start(raw[:, u % 2, 0:kt, :], W[w][row:row + kt * P, c:c + 256].rearrange("(k p) n -> p k n", p=P))\
                    .then_inc(raw_in[u % 2], 16)

            def page(cache, i):
                n = sp.value_load(ptr_[0:1, i:i + 1], min_val=0, max_val=a[cache].shape[0] - 1)
                sp.dma_start(kring[:, i % 4, :], a[cache][bass.ds(n, 1)].rearrange("a p l h d -> (a p) (l h d)"))\
                    .then_inc(page_in[i % 4], 16)

            unit(0)
            unit(1)
            sp.wait_ge(pt_in, 32)
            for i in range(3):
                page("cache_fox_k", i)
            for e in TIMELINE:
                if e[0] == "piece" and e[2] == 1 and PIECES[e[1]][1] == 0 and PIECES[e[1]][0] + 2 < len(UNITS):
                    unit(PIECES[e[1]][0] + 2)
                elif e[0] == "k" and e[1] + 3 < N_PAGE:
                    if e[1] >= 1:
                        sp.wait_ge(page_free.sem, e[1])
                    page("cache_fox_k", e[1] + 3)
                elif e[0] == "vstart":
                    sp.wait_ge(pe_s.sem, upto(pe_works, ITEMS.index(("dc", 1)) + 1))
                    for i in range(3):
                        page("cache_fox_v", i)
                elif e[0] == "v" and e[1] + 3 < N_PAGE:
                    if e[1] >= 1:
                        sp.wait_ge(v_used.sem, e[1])
                    page("cache_fox_v", e[1] + 3)
            sp.dma_start(out["sc_s"][:, 0, 0:SCW - 2], a["state_sconv"][:, 0, 1:]).then_inc(out_sem, 16)
            sp.dma_start(out["gc_s"][:, 0, 0:GCW - 2], a["state_gdn_conv"][:, 0, 1:]).then_inc(out_sem, 16)
            sp.dma_start(out["cf_s"][:, 0, 0:CFW - 2], a["state_conf_conv"][:, 0, 1:]).then_inc(out_sem, 16)
            sp.dma_start(out["ff_s"][:, 0, 0:FCW - 2], a["state_ffn_conv"][:, 0, 1:]).then_inc(out_sem, 16)

        @block.gpsimd
        def _(pool):
            def own(ins, st=pool_c):
                st.by(ins)
                pool.wait_ge(st.sem, st.n)

            own(pool.memset(pv[:, :, :], 0.0), pool_made)
            own(pool.memset(bias[:, :], 0.0), pool_made)
            own(pool.memset(cb[:, :, 0:3], 0.0), pool_made)
            own(pool.memset(eps6[:, :], 1e-6), pool_made)
            own(pool.memset(eps5[:, :], 1e-5), pool_made)
            own(pool.memset(fl8, 0.0), pool_made)
            pool.dma_start(ptr_[:, :], a["page_table"].rearrange("(o b) j -> o (b j)", o=1)).then_inc(pt_in, 16)
            pool.dma_start(ptc[:, :], a["page_table"].rearrange("b (j o) -> (b j) o", o=1)).then_inc(pt_in, 16)
            pool.wait_ge(pt_in, 32)

            def split(p):
                if PIECES[p][3] in LOW_BY_DVE:
                    return
                if p and PIECES[p - 1][3] in LOW_BY_DVE:
                    pool.wait_ge(lo.sem, p)
                u, half, kt = PIECES[p][:3]
                pool.wait_ge(hi.sem, p + 1)
                pool.tensor_tensor(wl[:, p % 2, 0:kt, :], raw[:, u % 2, 0:kt, half * P:(half + 1) * P],
                                   wh[:, p % 2, 0:kt, :].bitcast(F32), SUB).then_inc(lo.sem, 1)

            def product(i):
                if i % PAGES == 0:
                    if i == 0:
                        pool.wait_ge(qs_out, 16)
                    pool.dma_start(qb[:, :], qscr[i // PAGES:i // PAGES + 1, :].to_broadcast([P, 512])).then_inc(qb_in, 16)
                    pool.wait_ge(qb_in, 16 * (i // PAGES + 1))
                pool.wait_ge(page_in[i % 4], 16 * (i // 4 + 1))
                own(pool.tensor_tensor(kring[:, i % 4, :], kring[:, i % 4, :], qb[:, :], MUL), prod_done)

            split(0)
            for e in TIMELINE:
                if e[0] == "piece" and e[2] == 0 and e[1] + 1 < NP_:
                    split(e[1] + 1)
                elif e[0] == "k":
                    product(e[1])
                elif e[0] == "kend":
                    pool.wait_ge(page_free.sem, N_PAGE)
                    pool.indirect_dma_start(lf[:, :, :].rearrange("p a b -> p (a b)"), None,
                                            a["cache_fox_logf"].rearrange("n p l h -> n (p l h)"),
                                            bass.IndirectOffsetOnAxis(ap=ptc[:, 0:1], axis=0)).then_inc(lf_in, 16)
                elif e[0] == "side" and e[2] == ("x", 0):
                    pool.wait_ge(qs_out, 32)
                    pool.wait_ge(mt_act.sem, mt_a[mt_of("cq")])
                    pool.dma_start(qx[:, :, :].rearrange("p b n -> p (b n)"),
                                   qscr.rearrange("b n -> (b n)")[None, :].to_broadcast([P, NB * 512])).then_inc(q8_in, 16)
                    pool.wait_ge(q8_in, 16)
                    pool.wait_ge(mk_in, 16)
                    for b in range(NB):
                        kprod.by(pool.tensor_tensor(kvc[:, b, :, :], kvc[:, b, :, :], spread(qx[:, b, :], 2, 1), MUL))

        @block.tensor
        def _(pe):
            def mm(o, l, r, start=True, stop=True):
                return pe.matmul(o, l, r, start=start, stop=stop, skip_group_check=True)

            def tr(o, i):
                n = i.shape[0]
                return pe.transpose(o, i, ident[0:n, 0:n])

            pe.wait_ge(id_in, 16)
            pe.wait_ge(x_in, 16 * 5)
            for j in range(14):
                if j >= 4:
                    pe.wait_ge(pro_dve.sem, j - 3)
                o = sd[:, j % 4, :]
                if j == 0:
                    for k in range(KD):
                        last = tr(o[:, k * NB:(k + 1) * NB], xrow[0:NB, QT, k * P:(k + 1) * P])
                elif j <= KD:
                    for t in range(QT):
                        last = tr(o[:, t * P:(t + 1) * P], xrow[:, t, (j - 1) * P:j * P])
                else:
                    if j == 9:
                        pe.wait_ge(par_in, 16 * 18)
                    for b in range(4 * (j - 9), min(4 * (j - 9) + 4, N_BLK)):
                        last = tr(o[:, (b % 4) * P:(b % 4 + 1) * P], pv[:, b, :])
                pro_pe.by(last)

            def norm_sum(i, k):
                if i > 0 and k == 0:
                    pe.wait_ge(act_s.sem, upto(act_works, side_n[0]))
                    pe.wait_ge(dve_s.sem, upto(dve_works, side_n[0]))
                    pe.wait_ge(n_rt.sem, i)
                pe.wait_ge(n_sq.sem, KD * i + k + 1)
                for h in range(1 if i == 1 else 2):
                    w = MEM if i == 1 else TH
                    o = pb[:, 0, h, 0:w] if i == 0 else s0[:, 0:w] if i == 1 else sd[:, 2 + h, 0:w]
                    last = mm(o, ones, (pairB if i == 1 else sqb)[:, k % 2, h * w:(h + 1) * w], k == 0, k == KD - 1)
                n_pe.by(last)
                sums[0] = i + 1

            side_n, sums = [0], [0]
            ready = {}

            def rhs_ready(kind):
                if kind == "brA":
                    pe.wait_ge(ev_all.sem, count(dve_tile, mt_of("ab")))
                elif kind == "fo":
                    pe.wait_ge(ev_all.sem, count(dve_tile, mt_of("fu")))

            norm_of = {"fq": 0, "kv": 1, "cq": 2, "fg": 3}
            split_of = {"brC": 0, "brD": 4, "brB": 8, "wo": 12, "co": 12 + KD}

            def piece(p, h):
                u, half, kt, kind, idx, first, last_ = PIECES[p]
                m = PIECE_MT[p]
                if h == 0:
                    pe.wait_ge(hi.sem, p + 1)
                    pe.wait_ge(lo.sem, p + 1)
                    if kind not in ready:
                        ready[kind] = p
                        rhs_ready(kind)
                    if first and m >= 2:
                        if MT_ACT[m - 2]:
                            pe.wait_ge(mt_act.sem, mt_a[m - 2])
                        else:
                            pe.wait_ge(mt_dve.sem, mt_d[m - 2])
                    if p == 0:
                        pe.wait_ge(n_rt.sem, 1)
                if kind == "kv" and h == 1:
                    return
                w = MEM if kind == "kv" else TH
                c = slice(0, MEM) if kind == "kv" else slice(h * TH, (h + 1) * TH)
                k0 = UNITS[u][1] // P if kind == "fo" else 0
                for k in range(kt):
                    if h == 0 and kind in norm_of and ready[kind] == p:
                        pe.wait_ge(n_lo.sem, KD * norm_of[kind] + k + 1)
                    if h == 0 and kind in split_of and ready[kind] == p:
                        pe.wait_ge(sp_lo.sem, split_of[kind] + k + 1)
                    if kind == "kv":
                        xa, xb = memh[:, k, :], meml[:, k, :]
                    elif kind.startswith("br") or kind == "co":
                        xa, xb = oh[:, k, c], ol[:, k, c]
                    elif kind == "fo":
                        xa, xb = hh[:, k0 + k, c], hl[:, k0 + k, c]
                    else:
                        xa, xb = xh[:, k, c], xl[:, k, c]
                    o = pb[:, m % 2, h, 0:w]
                    mm(o, wh[:, p % 2, k, :], xa, first and k == 0, False)
                    mm(o, wh[:, p % 2, k, :], xb, False, False)
                    last = mm(o, wl[:, p % 2, k, :], xa, False, last_ and k == kt - 1)
                if h == 1 or kind == "kv":
                    piece_done.by(last)

            def logits(n):
                q, h = n // 2, 2 * (n % 2)
                for j in range(2):
                    last = mm(sd[:, 3 * (n % 2), j * MEM:(j + 1) * MEM], qc[:, h + j, q * P:(q + 1) * P], mkT[:, h + j, :])
                return last

            def side(K, s):
                kind, n = s[0], s[1]
                side_n[0] = K + 1
                if not pe_works(s):
                    return
                if sums[0] > 1 and kind != "ef":
                    pe.wait_ge(n_rt.sem, sums[0])
                if kind == "x" and 0 < n < XU:
                    pe.wait_ge(act_s.sem, upto(act_works, K))
                    pe.wait_ge(dve_s.sem, upto(dve_works, K))
                    last = logits(n)
                if kind == "y" and n == 0:
                    pe.wait_ge(n_tmp.sem, 5 * KD)
                done = K if kind == "y" else K + 1
                if upto(act_works, done):
                    pe.wait_ge(act_s.sem, upto(act_works, done))
                if upto(dve_works, done):
                    pe.wait_ge(dve_s.sem, upto(dve_works, done))
                if kind == "sm" and n == 0:
                    pe.wait_ge(wsm_lo.sem, 1)
                    for h in range(2):
                        c = slice(h * TH, (h + 1) * TH)
                        for k in range(KD):
                            o = sd[0:16, 2 + h, 0:TH]
                            mm(o, wsh[:, k, :], xh[:, k, c], k == 0, False)
                            mm(o, wsh[:, k, :], xl[:, k, c], False, False)
                            last = mm(o, wsl[:, k, :], xh[:, k, c], False, k == KD - 1)
                elif kind == "sm" and n == 1:
                    for t in range(5):
                        w = P if t < QT else NB
                        last = tr(s1[0:w, t * 16:t * 16 + 16], zrow[0:16, t * P:t * P + w])
                elif kind == "sm" and n == 2:
                    for t in range(QT):
                        tr(s0[0:FH, t * P:(t + 1) * P], fltok[:, t, :])
                    mm(s3[:, 0:P], ones[0:NB, :], exs[0:NB, :])
                    mm(s2[:, 0:16], cs(I_UP), gtok[:, :, :].rearrange("p a b -> p (a b)"))
                    last = mm(s2[:, 16:32], ones, gtok[:, :, :].rearrange("p a b -> p (a b)"))
                elif kind == "fst" and n < 3:
                    if n == 0:
                        pe.wait_ge(mt_act.sem, mt_a[mt_of("fv")])
                    for c in range(4):
                        last = tr(s0[0:NB, c * P:(c + 1) * P], fs[:, 4 * n + c, :])
                elif kind in ("fvt", "fkt") and n < QT:
                    src = fv if kind == "fvt" else fk
                    for c in range(4):
                        last = tr(s0[:, c * P:(c + 1) * P], src[:, c, n * P:(n + 1) * P])
                elif kind == "fox":
                    if n < FOX:
                        h, q = divmod(n, QT)
                        r = slice(FD * (h % 2), FD * (h % 2) + FD)
                        w = (q + 1) * P
                        mm(s0[:, 0:w], fq[r, h // 2, q * P:(q + 1) * P], fk[r, h // 2, 0:w], True, False)
                        mm(s0[:, 0:w], sel(h), cnh[0:FH, 0:w], False, False)
                        mm(s0[:, 0:w], sel(h), cnl[0:FH, 0:w], False, False)
                        last = mm(s0[:, q * P:w], mask_r[:, 0, :], mask_r[:, 1, :], False, True)
                    if 1 <= n <= FOX:
                        for b in range((n - 1) % QT + 1):
                            last = tr(s1[:, b * P:(b + 1) * P], fP[:, b * P:(b + 1) * P])
                    if 2 <= n <= FOX + 1:
                        h, q = divmod(n - 2, QT)
                        for b in range(q + 1):
                            last = mm(s2[FD * (h % 2):FD * (h % 2) + FD, 0:P], vt[:, b, h * FD:(h + 1) * FD], fPT[:, b, :], b == 0, b == q)
                elif kind == "l2":
                    for j in range(2):
                        for h in range(2):
                            last = mm(sd[:, 2 * j + h, 0:TH], ones, lsq2[:, j, h * TH:(h + 1) * TH])
                elif kind == "gp":
                    if n < 4:
                        for h in range(2):
                            last = mm(sd[:, h, 0:TH], ones, lsq[:, h * TH:(h + 1) * TH])
                elif kind == "gdn":
                    c = s[2]
                    cc = slice(c * P, (c + 1) * P)
                    if n == -1 and c == 0:
                        pe.wait_ge(ev_all.sem, count(dve_tile, mt_of("gx")))
                    for h in range(GH):
                        o = slice(h * P, (h + 1) * P)
                        q_, k_, v_ = (gx_tile(4 * j + h)[:, cc] for j in range(3))
                        if n == -1:
                            tr(s0[:, o], k_)
                            tr(s1[:, o], v_)
                            last = mm(s2[:, o], gtok[:, c, h:h + 1].to_broadcast([P, P]), cs(I_UP))
                        elif n == 0:
                            last = mm(s0[:, o], k_, k_)
                        elif n == 1:
                            mm(s0[:, o], k_, q_)
                            last = tr(s1[:, o], gM[:, h, :])
                        elif 2 <= n <= 12 and n % 2 == 0:
                            last = mm(s0[:, o], gM[:, h, :], gXT[:, h, :])
                        elif 3 <= n <= 13:
                            last = mm(s1[:, o], gX[:, h, :], gQ[:, h, :])
                            if n < 13:
                                last = mm(s2[:, o], gQ[:, h, :], gX[:, h, :])
                        elif n == 14:
                            mm(s0[:, o], gXT[:, h, :], gvb[:, h, :], h == 0, False)
                            last = mm(s1[:, o], gR[:, h, :], gXT[:, h, :])
                        elif n == 15:
                            last = mm(s0[:, o], gW[:, h, :], gS[:, h, :], False, h == GH - 1)
                        elif n == 16:
                            mm(s2[:, o], gS[:, h, :], gqd[:, h, :], True, False)
                            mm(s2[:, o], gM[:, h, :], gQK[:, h, :], False, True)
                            last = mm(s1[:, o], gkd[:, h, :], gM[:, h, :])
                elif kind == "cln":
                    for c in (range(KB) if n == 0 else [n - 1] if n < 5 else []):
                        src = oC[:, c, :] if n == 0 else lsq
                        for h in range(2):
                            last = mm(sd[:, (0 if n == 0 else 2) + h, 0:TH], ones, src[:, h * TH:(h + 1) * TH], c == 0, c == KB - 1)
                elif kind == "gs":
                    if n == 1:
                        pe.wait_ge(ss_in, 16)
                        for u in range(32):
                            mm(s0[:, 2 * u:2 * u + 2], ssam[:, u, :], qkp[:, u, :])
                        last = mm(s1[:, 0:32], ones, kqs)
                    elif n == 2:
                        tr(s2[0:32, 0:P], dl)
                        last = tr(s2[0:32, P:2 * P], kc)
                    elif 3 <= n <= 10:
                        last = mm(s0[:, :], krow[0:32, :], blk[0:32, :, :].rearrange("p a b -> p (a b)"))
                elif kind == "dc" and n == 0:
                    mm(s0[:, 0:FH], cs(I_PAGE), tot)
                    last = mm(s1[:, 0:64], ones, totm[:, :, :].rearrange("p a b -> p (a b)"))
                elif kind == "dc" and n == 1:
                    for h in range(FH):
                        last = tr(sd[:, 2 + h // 4, (h % 4) * P:(h % 4 + 1) * P], cpg[:, h, :])
                elif kind == "ds" and n == 0:
                    tr(s0[0:64, 0:P], mx64[:, :, :].rearrange("p a b -> p (a b)"))
                    f = qk32[:, :, :].rearrange("p a b -> p (a b)")
                    mm(s1[:, 0:32], cs(I_LO), f)
                    last = mm(s1[:, 32:64], cs(I_HI), f)
                elif kind == "ds" and n == 1:
                    last = mm(s2[:, 0:64], ones[0:64, :], dg64[0:64, :])
                elif kind == "ds" and n == 2:
                    last = mm(s3[:, 0:64], ones, rs64[:, :, :].rearrange("p a b -> p (a b)"))
                elif kind == "df" and n == 0:
                    pe.wait_ge(v64_in, 32)
                    last = tr(s3[:, 0:64], v64[0:NB * FH, :, :].rearrange("p a b -> p (a b)"))
                elif kind in ("ex", "ef") and pe_works(s):
                    src, c0, nc_, w = exports[kind][n][:4]
                    for c in range(nc_):
                        last = tr(s0[0:w, c * P:(c + 1) * P], src[:, c0 + c, :])
                elif kind == "ml" and n == 1:
                    pe.wait_ge(mem_in, 16)
                    for k in range(KD):
                        for t in range(2):
                            last = tr(sd[:, k // 2, ((k % 2) * 2 + t) * P:((k % 2) * 2 + t + 1) * P], mrow[:, t, k * P:(k + 1) * P])
                elif kind == "xm" and n == 0:
                    pe.wait_ge(mt_act.sem, mt_a[mt_of("cq")])
                    for t in range(2):
                        for h in range(XH):
                            tr(sd[:, t, h * P:(h + 1) * P], mvT[:, h, t * P:(t + 1) * P])
                            last = tr(sd[:, 2 + t, h * P:(h + 1) * P], mkT[:, h, t * P:(t + 1) * P])
                elif kind == "xm" and n == 1:
                    for h in range(XH):
                        last = tr(s0[0:NB, h * P:(h + 1) * P], qc[:, h, SEQ:T])
                elif kind == "x":
                    if n == 0:
                        last = logits(0)
                    if 1 <= n <= XU:
                        for j in range(2):
                            for t in range(2):
                                last = tr(s1[:, (2 * j + t) * P:(2 * j + t + 1) * P], xP[:, j, t * P:(t + 1) * P])
                    if 2 <= n <= XU + 1:
                        h = 2 * (n % 2)
                        for j in range(2):
                            for t in range(2):
                                last = mm(s2[:, j * P:(j + 1) * P], mv[:, t, (h + j) * P:(h + j + 1) * P], xPT[:, 2 * j + t, :],
                                          t == 0, t == 1)
                elif kind == "xd" and n == 0:
                    last = tr(s0[0:32, 0:P], xmx[:, :, :].rearrange("p a b -> p (a b)"))
                elif kind == "xd" and n == 1:
                    last = mm(s1[:, 0:32], ones[0:32, :], xdg[0:32, :])
                elif kind == "xd" and n == 2:
                    mm(s2[:, 0:32], ones, xrs[:, :, :].rearrange("p a b -> p (a b)"))
                    for b in range(NB):
                        if b < 2:
                            pe.wait_ge(mv_in[b], 16 * NB // 2)
                        for h in range(XH):
                            for t in range(2):
                                last = mm(s3[:, b * 8 + 2 * h:b * 8 + 2 * h + 2], kvc[:, b, t, h * P:(h + 1) * P],
                                          xsc[:, b, t, 2 * (h // 2):2 * (h // 2) + 2], t == 0, t == 1)
                elif kind == "y":
                    w = P if n < QT else NB
                    for k in range(KD):
                        last = tr(sd[0:w, 2 * (n % 2) + k // 4, (k % 4) * P:(k % 4 + 1) * P], xT[:, k, n * P:n * P + w])
                pe_s.by(last)

            def page(i):
                if i == 0:
                    pe.wait_ge(dve_s.sem, upto(dve_works, ITEMS.index(("ds", 3)) + 1))
                elif i % PAGES == 0:
                    pe.wait_ge(v_rows.sem, i // PAGES)
                pe.wait_ge(page_in[i % 4], 16 * (N_PAGE // 4 + i // 4 + 1))
                v_used.by(mm(s3[0:FH, :], sc[:, i, :], kring[:, i % 4, :], i % PAGES == 0, i % PAGES == PAGES - 1))

            for e in TIMELINE:
                if e[0] == "nsq":
                    norm_sum(e[1], e[2])
                elif e[0] == "piece":
                    piece(e[1], e[2])
                elif e[0] == "side":
                    side(e[1], e[2])
                elif e[0] == "v":
                    page(e[1])

        @block.scalar
        def _(act):
            def own(ins, st=act_c):
                st.by(ins)
                act.wait_ge(st.sem, st.n)

            def fn(o, i, f, st=act_c, **kw):
                own(act.activation(o, i, f, **kw), st)

            def split(p):
                u, half, kt = PIECES[p][:3]
                if half == 0:
                    act.wait_ge(raw_in[u % 2], 16 * (u // 2 + 1))
                if p >= 2:
                    act.wait_ge(piece_done.sem, p - 1)
                    act.wait_ge(lo.sem, p - 1)
                fn(wh[:, p % 2, 0:kt, :], raw[:, u % 2, 0:kt, half * P:(half + 1) * P], ACT.Copy, hi)

            def evac(m, second):
                p = MT_LAST[m]
                kind, idx = PIECES[p][3:5]
                s = idx % 2
                if second and not second_tile[m]:
                    return
                if second and kind in ("gx", "fg"):
                    y = gx_tile(idx) if kind == "gx" else pairA[:, s, :]
                    act.wait_ge(ev_y.sem, count(conv_tile, m))
                    fn(pairB[:, s, :], y, ACT.Tanh, ev_t)
                    return
                if second:
                    act.wait_ge(mt_dve.sem, mt_d[m])
                    fn(oh[:, idx, :] if kind == "ab" else hh[:, idx, :], tmp, ACT.Copy, ev_t)
                    return
                if not MT_ACT[m]:
                    return
                if m >= 2:
                    act.wait_ge(ev_all.sem, count(dve_tile, m - 2))
                act.wait_ge(piece_done.sem, p + 1)
                x = bulk(m)
                if kind in ("fq", "fk", "fv"):
                    j = 4 * ("fq", "fk", "fv").index(kind) + idx
                    c = FD ** -0.5 if kind == "fq" else 1.0
                    act_c.by(act.activation(both(qkv[:, j, :]), x, ACT.Copy, scale=c))
                    fn(fs[:, j, :], pb[:, m % 2, 1, TH - NB:TH], ACT.Copy, mt_act, scale=c)
                elif kind == "cv":
                    fn(both(pairA[:, s, :]), x, ACT.Copy, mt_act, scale=0.5)
                elif kind == "cg" or kind.startswith("gate"):
                    fn(both(pairB[:, s, :]), x, ACT.Tanh, mt_act, scale=0.5)
                elif kind in ("gx", "fg"):
                    n_ = 11 if kind == "gx" else 10
                    act_c.by(act.activation((tail_gx if kind == "gx" else tail_ff)[:, idx, :],
                                            pb[:, m % 2, 1, TH - n_:TH], ACT.Copy))
                    fn(both(cb[:, s, 3:3 + T]), x, ACT.Copy, mt_act)
                elif kind == "ac":
                    fn(both(pairA[:, s, :]), x, ACT.Copy, mt_act)
                elif kind == "gz":
                    fn(both(pairA[:, s, :]), x, ACT.Copy, scale=0.5)
                    fn(both(pairB[:, s, :]), x, ACT.Tanh, mt_act, scale=0.5)
                elif kind == "kv":
                    o = mkT[:, idx, :] if idx < XH else mvT[:, idx - XH, :]
                    fn(o, pb[:, m % 2, 0, 0:MEM], ACT.Copy, mt_act)
                elif kind == "cq":
                    fn(both(qc[:, idx, :]), x, ACT.Copy, mt_act, scale=P ** -0.5)

            def norm_square(i, k):
                if k >= 2:
                    act.wait_ge(n_pe.sem, KD * i + k - 1)
                if i == 0:
                    act.wait_ge(pro_dve.sem, k + 2)
                elif i == 1:
                    act.wait_ge(dve_s.sem, upto(dve_works, ITEMS.index(("ml", 2)) + 1))
                    act.wait_ge(ev_all.sem, count(dve_tile, mt_of("brB")))
                else:
                    act.wait_ge(ev_all.sem, count(dve_tile, mt_of({2: "wo", 3: "co", 4: "fo"}[i], k)))
                    act.wait_ge(n_lo.sem, KD * (1 if i == 2 else i))
                if i == 1:
                    own(act.activation(pairB[:, k % 2, 0:MEM], memT[:, k, :], ACT.Square), n_sq)
                else:
                    own(act.activation(sqb[:, k % 2, 0:T], xT[:, k, :], ACT.Square), n_sq)

            def norm_root(i):
                act.wait_ge(n_pe.sem, KD * (i + 1))
                x = pb[:, 0, :, 0:TH] if i == 0 else s0[:, 0:MEM] if i == 1 else sd[:, 2:4, 0:TH]
                r = lrs[:, 0:MEM] if i == 1 else lrs
                fn(r if i == 1 else both(r), x, ACT.Ln, scale=1.0 / D, bias=eps6[:, 0:1])
                fn(r, r, ACT.Exp, n_rt, scale=-0.5)

            def norm_apply(i, k, width):
                if i == 4 or k == KD:
                    return
                if i == 1 and k == 0:
                    act.wait_ge(piece_done.sem, last_piece("brB") + 1)
                act.wait_ge(n_tmp.sem, KD * i + k + 1)
                if i == 1:
                    fn(memh[:, k, :], pairB[:, k % 2, 0:MEM], ACT.Copy, n_hi)
                else:
                    fn(xh[:, k, :], sqb[:, k % 2, :], ACT.Copy, n_hi)

            def store(dst, src, st=out_sem):
                act.dma_start(dst, src).then_inc(st, 16)

            used = [0, 0]

            def sent(n, dst, src):
                used[n % 2] += 1
                store(dst, src, stg_out[n % 2])

            def side(K, s):
                kind, n = s[0], s[1]
                works = act_works(s) or s in (("gs", 12), ("ml", 0)) or (kind == "x" and n > 0)
                if not works:
                    return
                if upto(pe_works, K):
                    act.wait_ge(pe_s.sem, upto(pe_works, K))
                if upto(dve_works, K):
                    act.wait_ge(dve_s.sem, upto(dve_works, K))
                fins = None
                va, av = upto(to_act, K), upto(to_dve, K)
                if kind == "sm" and n == 1:
                    fins = act.activation(both(zrow[0:16, :]), sd[0:16, 2:4, 0:TH], ACT.Copy)
                elif kind == "sm" and n == 2:
                    act.wait_ge(v2a.sem, va + 1)
                    for x_, y_ in ((slice(0, P), slice(0, 64)), (slice(0, NB), slice(64, 80))):
                        fn(zl[x_, y_], az[x_, y_], ACT.Exp, scale=-1.0)
                        fn(zb[x_, y_], zt[x_, y_], ACT.Tanh, scale=0.5)
                    fn(bias[:, 16:20], bias[:, 16:20], ACT.Exp)
                    fn(zl[:, 0:64], zl[:, 0:64], ACT.Ln, bias=1.0)
                    fn(zl[0:NB, 64:80], zl[0:NB, 64:80], ACT.Ln, a2v, bias=1.0)
                    fins = act.activation(rsum[:, 0:1], eps6[:, 0:1], ACT.Copy)
                elif kind == "sm" and n == 3:
                    act.wait_ge(v2a.sem, va + 1)
                    fn(bsc[:, :, 0:4], bsc[:, :, 0:4], ACT.Exp)
                    fn(edc, dcol, ACT.Exp)
                    fn(kdf, kdf, ACT.Exp)
                    fn(edl, edl, ACT.Exp, a2v)
                    act.wait_ge(xs_out, 16)
                    fn(mask_r[:, 0, :], ident, ACT.Copy)
                    fn(mask_r[:, 1, :], cs(I_CAUSAL), ACT.Copy)
                    act.wait_ge(v2a.sem, va + 2)
                    fn(cnh[0:FH, :], cneg[0:FH, :], ACT.Copy, a2v)
                    with nc.allow_non_contiguous_dma(reason="8 values of a token"):
                        store(out["fl_p"][0, :, 0, :].rearrange("(t p) h -> p t h", p=P), fltok[:, :, :])
                        store(out["fl_s"][:, 0, 0, :], zsam[0:NB, 8:16])
                    fins = act.activation(rsum[:, 0:1], eps6[:, 0:1], ACT.Copy)
                elif kind == "fst":
                    if n == 3:
                        act.wait_ge(qs_out, 16)
                    fn(srow[0:NB, n % 2, :], s0[0:NB, :], ACT.Copy)
                    if n == 1:
                        store(qscr, srow[0:NB, 1, :], qs_out)
                    else:
                        dst = out["fk_s" if n == 2 else "fv_s"]
                        store(dst.rearrange("b t l h d -> b (t l h d)"), srow[0:NB, n % 2, :], ss_st)
                    fins = act.activation(rsum[:, 0:1], eps6[:, 0:1], ACT.Copy)
                elif kind == "fvt":
                    fn(vt[:, n - 1, :], s0, ACT.Copy)
                    store(out["fv_p"][0, (n - 1) * P:n * P].rearrange("t l h d -> t (l h d)"), vt[:, n - 1, :], vt_out)
                    fins = act.activation(rsum[:, 0:1], eps6[:, 0:1], ACT.Copy)
                elif kind == "fkt":
                    if n >= 3:
                        act.wait_ge(stg_out[(n - 1) % 2], 16)
                    fn(stg[:, (n - 1) % 2, :], s0, ACT.Copy)
                    sent(n - 1, out["fk_p"][0, (n - 1) * P:n * P].rearrange("t l h d -> t (l h d)"), stg[:, (n - 1) % 2, :])
                    fins = act.activation(rsum[:, 0:1], eps6[:, 0:1], ACT.Copy)
                elif kind == "fox":
                    if n <= FOX:
                        w = ((n - 1) % QT + 1) * P
                        act.wait_ge(v2a.sem, va + 1)
                        fn(fP[:, 0:w], s0[:, 0:w], ACT.Exp, a2v, bias=nmx[:, 0:1], accum_out=rsum[:, 0:1])
                    w = ((n - 2) % QT + 1) if 2 <= n <= FOX + 1 else 1
                    if 2 <= n <= FOX + 1:
                        fins = act.activation(fPT[:, 0:w, :], s1[:, 0:w * P].rearrange("p (a b) -> p a b", a=w), ACT.Copy)
                    else:
                        fins = act.activation(rsum[:, 1:2], eps6[:, 0:1], ACT.Copy)
                elif kind == "l2":
                    if n == 0:
                        fox_stored(act)
                        act.dma_start(ssam[:, :, :], a["state_gdn"].rearrange("b l h k v -> k (b l h) v")).then_inc(ss_in, 16)
                    if n:
                        fn(lrs2[:, :, :].rearrange("p j (h c) -> p (j h) c", h=2), sd[:, :, 0:TH], ACT.Ln, bias=eps6[:, 0:1])
                        fn(lrs2[:, :, :], lrs2[:, :, :], ACT.Exp, a2v, scale=-0.5)
                    if n < 4:
                        act.wait_ge(ev_all.sem, count(dve_tile, mt_of("gx", 2 * n + 1)))
                        fins = act.activation(lsq2[:, :, :], qkv[:, (8 + 2 * n) % 12:(8 + 2 * n) % 12 + 2, :], ACT.Square)
                    else:
                        fins = act.activation(rsum[:, 0:1], eps6[:, 0:1], ACT.Copy)
                elif kind == "gp":
                    if n == 0:
                        store(out["S_p"].rearrange("b l h k v -> k (b l h) v"), gS[:, :, :], gs_out)
                    if n:
                        fn(both(lrs), sd[:, 0:2, 0:TH], ACT.Ln, scale=1.0 / P, bias=eps6[:, 0:1])
                        fn(lrs, lrs, ACT.Exp, a2v, scale=-0.5)
                    if n < 4:
                        fins = act.activation(lsq, oB[:, n, :], ACT.Square)
                    else:
                        fins = act.activation(rsum[:, 0:1], eps6[:, 0:1], ACT.Copy)
                elif kind == "gdn":
                    c = s[2]
                    s4 = [x.rearrange("p (a b) -> p a b", a=GH) for x in (s0, s1, s2)]
                    if n == 0:
                        if c == 0:
                            act.wait_ge(ss_out, 16)
                        for h in range(GH):
                            o = slice(h * P, (h + 1) * P)
                            act_c.by(act.activation(gR[:, h, :], s0[:, o], ACT.Copy, scale=bed[:, 4 * c + h:4 * c + h + 1]))
                            act_c.by(act.activation(gkd[:, h, :], s0[:, o], ACT.Copy, scale=kdf[:, 4 * c + h:4 * c + h + 1]))
                        act.wait_ge(v2a.sem, va + 1)
                        fn(gQ[:, :, :], gQ[:, :, :], ACT.Exp, a2v, scale=-1.0)
                        act.wait_ge(v2a.sem, va + 2)
                        fn(gqd[:, :, :], s4[2], ACT.Exp, a2v)
                        fins = act.activation(gXT[:, :, :], gM[:, :, :], ACT.Exp)
                    elif n <= 13:
                        fins = act.activation(gQ[:, :, :], s4[0], ACT.Copy)
                    elif n == 15:
                        fins = act.activation(gW[:, :, :], s4[1], ACT.Copy, scale=-1.0)
                    elif n == 16:
                        fins = act.activation(gM[:, :, :], s4[0], ACT.Copy)
                    else:
                        fins = act.activation(oB[:, :, c * P:(c + 1) * P], s4[2], ACT.Copy)
                elif kind == "cln":
                    if n < 5:
                        if n == 1:
                            act.wait_ge(v2a.sem, va + 1)
                        fins = act.activation(lsq, oC[:, n - 1, :], ACT.Square)
                    elif n == 5:
                        fn(both(lrs), sd[:, 2:4, 0:TH], ACT.Ln, scale=1.0 / BD, bias=eps5[:, 0:1])
                        fn(lrs, lrs, ACT.Exp, a2v, scale=-0.5)
                        fins = act.activation(rsum[:, 0:1], eps6[:, 0:1], ACT.Copy)
                    else:
                        for c in range(KB):
                            if c >= 2:
                                act.wait_ge(v2a.sem, va + c - 1)
                            fn(lsq if c % 2 == 0 else lrs, oC[:, c, :], ACT.Tanh, a2v)
                        fins = act.activation(rsum[:, 0:1], eps6[:, 0:1], ACT.Copy)
                elif kind == "gs" and n == 12:
                    store(out["S_s"].rearrange("b l h k v -> k (b l h) v"), ssam[:, :, :], ss_out)
                elif kind == "ds":
                    if n == 2:
                        act.wait_ge(v2a.sem, va + 1)
                        fn(pn[:, :, :], pn[:, :, :], ACT.Exp)
                        fn(sc[:, :, :], sc[:, :, :], ACT.Exp, a2v)
                        fins = act.activation(rsum[:, 0:1], eps6[:, 0:1], ACT.Copy)
                elif kind in ("ex", "ef"):
                    src, c0, nc_, w, wp, dp, ds_ = exports[kind][n - 1]
                    st_ = stg if kind == "ex" else mstg
                    j = (n - 1) % 2
                    if used[j]:
                        act.wait_ge(stg_out[j], 16 * used[j])
                    fn(st_[0:w, j, 0:nc_ * P], s0[0:w, 0:nc_ * P], ACT.Copy)
                    sent(j, dp, st_[0:wp, j, 0:nc_ * P])
                    sent(j, ds_, st_[wp:w, j, 0:nc_ * P])
                    fins = act.activation(rsum[:, 0:1], eps6[:, 0:1], ACT.Copy)
                elif kind == "ml" and n == 0:
                    act.wait_ge(gs_out, 16)
                    for j in range(2):
                        act.wait_ge(stg_out[j], 16 * used[j])
                    act.dma_start(mrow[:, :, :], a["mem_prompt"][0].rearrange("(t p) d -> p t d", p=P)).then_inc(mem_in, 16)
                    act.dma_start(kvc[:, :, :, :].rearrange("p b t n -> p (b t) n"),
                                  a["cache_mem_k"].rearrange("b l (t p) h d -> p (b l t) (h d)", p=P)).then_inc(mk_in, 16)
                elif kind == "xm":
                    if n == 1:
                        fn(mv[:, :, :], sd[:, 0:2, :], ACT.Copy)
                        fn(xstg[:, :, :], sd[:, 2:4, :], ACT.Copy)
                        store(out["mv_p"][0, 0].rearrange("(t p) h d -> p t (h d)", p=P), mv[:, :, :])
                        store(out["mk_p"][0, 0].rearrange("(t p) h d -> p t (h d)", p=P), xstg[:, :, :])
                        fins = act.activation(rsum[:, 0:1], eps6[:, 0:1], ACT.Copy)
                    else:
                        own(act.activation(qrow[0:NB, :], s0[0:NB, :], ACT.Copy), act_s)
                        store(qscr, qrow[0:NB, :], qs_out)
                        return
                elif kind == "x":
                    if 3 <= n <= NB + 2:
                        b = n - 3
                        act.wait_ge(kred.sem, b + 1)
                        act.dma_start(kvc[:, b, :, :], a["cache_mem_v"][b, 0].rearrange("(t p) h d -> p t (h d)", p=P))\
                            .then_inc(mv_in[b % 2], 16)
                    if n <= XU:
                        act.wait_ge(v2a.sem, va + 1)
                        for j in range(2):
                            (a2v if j else act_c).by(act.activation(
                                xP[:, j, :], sd[:, 3 * ((n - 1) % 2), j * MEM:(j + 1) * MEM], ACT.Exp, bias=xnm[:, j:j + 1], accum_out=xsum[:, j:j + 1]))
                    if 2 <= n <= XU + 1:
                        fins = act.activation(xPT[:, :, :], s1.rearrange("p (a b) -> p a b", a=4), ACT.Copy)
                    elif n == 1:
                        fins = act.activation(rsum[:, 1:2], eps6[:, 0:1], ACT.Copy)
                elif kind == "xd":
                    if n == 2:
                        act.wait_ge(v2a.sem, va + 1)
                        fn(xsc[:, :, :, :], xsc[:, :, :, :], ACT.Exp, a2v)
                        fins = act.activation(rsum[:, 0:1], eps6[:, 0:1], ACT.Copy)
                elif kind == "y":
                    t = n - 1
                    w = P if t < QT else NB
                    if t == 0:
                        act.wait_ge(piece_done.sem, NP_)
                    own(act.activation(ystg[0:w, t, :, :], sd[0:w, 2 * (t % 2):2 * (t % 2) + 2, :], ACT.Copy), act_s)
                    dst = out["y_p"][0, t * P:(t + 1) * P, :] if t < QT else out["y_s"][:, 0, :]
                    store(dst, ystg[0:w, t, :, :].rearrange("p a b -> p (a b)"))
                    return
                if act_works(s):
                    own(fins, act_s)

            with nc.allow_non_contiguous_dma(reason="16 columns of w_in"):
                act.dma_start(wsm[:, :, 0:8], W["w_in"][:, C_GA:C_GA + 8].rearrange("(k p) n -> p k n", p=P)).then_inc(small_in, 16)
                act.dma_start(wsm[:, :, 8:16], W["w_in"][:, C_FF:C_FF + 8].rearrange("(k p) n -> p k n", p=P)).then_inc(small_in, 16)
            act.wait_ge(small_in, 16 * 5)
            fn(wsh[:, :, :], wsm[:, :, :], ACT.Copy, wsm_hi)
            split(0)
            done = [0]
            spl = [0]
            for e in TIMELINE:
                if e[0] == "nsq":
                    if e[1:] == (0, 0):
                        act.wait_ge(pool_made.sem, 6)
                    norm_square(e[1], e[2])
                elif e[0] == "nroot":
                    norm_root(e[1])
                    if e[1] == 0:
                        store(xscr, xT[:, :, :].rearrange("p a b -> p (a b)"), xs_out)
                elif e[0] == "napply":
                    norm_apply(e[1], e[2], MEM if e[1] == 1 else T)
                elif e[0] == "piece":
                    cur = e[1]
                    if e[2] == 0 and cur + 1 < NP_:
                        split(cur + 1)
                elif e[0] in ("evac", "evac2"):
                    evac(e[1], e[0] == "evac2")
                    if e[0] == "evac2":
                        done[0] = e[1] + 1
                elif e[0] == "split":
                    src, n = {"brC": (oC, 4), "brB": (oB, 4), "brD": (oD, 4), "brX": (oX, 4), "merged": (xT, 8)}[e[1]]
                    act.wait_ge(piece_done.sem, cur if e[1] not in ("merged", "brX") else cur + 1)
                    act.wait_ge(ev_all.sem, count(dve_tile, done[0] - 1))
                    if upto(dve_works, side_at[0]):
                        act.wait_ge(dve_s.sem, upto(dve_works, side_at[0]))
                    for k in range(n):
                        fn((xh if n == 8 else oh)[:, k, :], src[:, k, :], ACT.Copy, sp_hi)
                    spl[0] += n
                    if e[1] == "merged":
                        act.wait_ge(sp_lo.sem, spl[0])
                        act.wait_ge(xs_out, 16)
                        act.dma_start(xT[:, :, :].rearrange("p a b -> p (a b)"), xscr).then_inc(xs_in, 16)
                elif e[0] == "side":
                    side(e[1], e[2])
                    side_at[0] = e[1] + 1
                elif e[0] == "v" and e[1] % PAGES == PAGES - 1:
                    b = e[1] // PAGES
                    act.wait_ge(v_used.sem, e[1] + 1)
                    if b >= 2:
                        act.wait_ge(vs_out[b % 2], 16 * (b // 2))
                    fn(vrow[0:FH, b % 2, :], s3[0:FH, :], ACT.Copy, v_rows)
                    at = b * FH * (512 + FD)
                    store(vscr[at:at + FH * 512].rearrange("(h n) -> h n", h=FH), vrow[0:FH, b % 2, :], vs_out[b % 2])
                    if b == NB - 1:
                        for j in range(2):
                            act.wait_ge(vs_out[j], 16 * NB // 2)
                        for j in range(2):
                            act.dma_start(v64[0:NB * FH, j, :], vscr.rearrange("(r n) -> r n", n=512 + FD)[:, 0:FD]).then_inc(v64_in, 16)
            for st_, k in ((out_sem, out_total[0]),):
                act.wait_ge(st_, k)
            for j in range(2):
                act.wait_ge(stg_out[j], 16 * used[j])
            act.wait_ge(ss_out, 16)
            act.wait_ge(gs_out, 16)
            act.wait_ge(ss_st, 32)
            act.wait_ge(vt_out, 64)

        @block.vector
        def _(dve):
            def own(ins, st=dve_c):
                st.by(ins)
                dve.wait_ge(st.sem, st.n)

            def tt(o, x, y, op, st=dve_c):
                own(dve.tensor_tensor(o, x, y, op), st)

            def ts(o, x, s1_, s2_=None, op0=MUL, op1=None, st=dve_c):
                own(dve.tensor_scalar(o, x, s1_, s2_, op0, op1) if op1 else dve.tensor_scalar(o, x, s1_, None, op0), st)

            def stt(o, x, s_, y, op0, op1, st=dve_c):
                own(dve.scalar_tensor_tensor(out=o, in0=x, scalar=s_, in1=y, op0=op0, op1=op1), st)

            def cp(o, x, st=dve_c):
                own(dve.tensor_copy(o, x), st)

            def red(o, x, op, st=dve_c):
                own(dve.tensor_reduce(o, x, AX, op), st)

            def conv(x, y, width, wcol, hist, w_last, st):
                ts(y, x[:, 3:3 + T], w_last)
                for j in range(width - 1):
                    if j:
                        dve.wait_ge(dve_c.sem, dve_c.n - 1)
                    dve_c.by(dve.scalar_tensor_tensor(out=y[:, 0:SEQ], in0=x[:, 4 - width + j:4 - width + j + SEQ],
                                                      scalar=wcol(j), in1=y[:, 0:SEQ], op0=MUL, op1=ADD))
                    past = hist(j)
                    ys = y[:, SEQ:T] if len(past.shape) == 2 else y[:, SEQ:T].rearrange("p (n b) -> p n b", b=2)
                    if j:
                        dve.wait_ge(dve_c.sem, dve_c.n - 1)
                    (st if j == width - 2 else dve_c).by(dve.scalar_tensor_tensor(
                        out=ys, in0=past, scalar=wcol(j), in1=ys, op0=MUL, op1=ADD))

            def evac(m, second):
                p = MT_LAST[m]
                kind, idx = PIECES[p][3:5]
                s = idx % 2
                if second and not second_tile[m]:
                    return
                if second:
                    dve.wait_ge(ev_t.sem, count(second_tile, m))
                    if kind == "gx":
                        stt(gx_tile(idx), pairB[:, s, :], 1.0, gx_tile(idx), ADD, MUL, ev_all)
                    elif kind == "fg":
                        stt(pairA[:, s, :], pairB[:, s, :], 1.0, pairA[:, s, :], ADD, MUL, ev_all)
                    else:
                        h_, l_ = (oh, ol) if kind == "ab" else (hh, hl)
                        tt(l_[:, idx, :], tmp, h_[:, idx, :].bitcast(F32), SUB, ev_all)
                    return
                if MT_ACT[m]:
                    dve.wait_ge(mt_act.sem, mt_a[m])
                else:
                    dve.wait_ge(piece_done.sem, p + 1)
                x = bulk(m)
                if kind == "cg":
                    if idx == 0:
                        dve.wait_ge(xs_out, 16)
                        own(dve.memset(glu[:, :, 0:CFW - 1], 0.0))
                    stt(glu[:, idx, CFW - 1:CFW - 1 + T], pairB[:, s, :], 1.0, pairA[:, s, :], ADD, MUL)
                    cp(tail_cf[:, idx, :], glu[:, idx, SEQ:SEQ + 38], ev_all)
                elif kind == "gx":
                    if idx == 0:
                        dve.wait_ge(pe_s.sem, upto(pe_works, ITEMS.index(("fvt", 4))))
                    if idx >= 4:
                        at = ITEMS.index(("fox", 8 * (idx % 4) + 9 if idx == 4 else FOX - 1))
                        dve.wait_ge(pe_s.sem, upto(pe_works, at + 1))

                    gh = cols[:, B_GS:B_GS + 4, 0:72].rearrange("p n (b r) -> p n b r", b=2)

                    def hist(j):
                        return gh[:, :, :, j * 12 + idx]

                    conv(cb[:, s, :], gx_tile(idx), GCW, lambda j: col(V_GW + 12 * j + idx), hist, col(V_GW + 36 + idx), ev_y)
                elif kind == "ah":
                    tt(both(cb[:, s, 3:3 + T]), both(pairA[:, s, :]), x, MUL, mt_dve)
                    cp(tail_sc[:, idx, :], cb[:, s, SEQ + 1:SEQ + 11])
                    conv(cb[:, s, :], pairB[:, s, :], SCW, lambda j: col(V_SW + 4 * j + idx),
                         lambda j: cols[:, B_SS, 0:64].rearrange("p (b r) -> p b r", b=NB)[:, :, 4 * j + idx], col(V_SW + 8 + idx), ev_all)
                elif kind == "ab":
                    tt(both(tmp), both(pairB[:, s, :]), x, MUL, mt_dve)
                elif kind.startswith("br"):
                    if kind == "brA":
                        stt(both(xT[:, idx, :]), both(pairB[:, s, :]), 1.0, x, ADD, MUL, mt_dve)
                        cp(fl8[:, 0:1], fl8[:, 1:2], ev_all)
                    else:
                        stt(both(tmp), both(pairB[:, s, :]), 1.0, x, ADD, MUL, mt_dve)
                        tt(xT[:, idx, :], xT[:, idx, :], tmp, ADD, ev_all)
                elif kind == "gz":
                    stt(pairA[:, s, :], pairB[:, s, :], 1.0, pairA[:, s, :], ADD, MUL)
                    tt(oB[:, idx, :], oB[:, idx, :], pairA[:, s, :], MUL, ev_all)
                elif kind in ("wo", "co", "fo"):
                    if kind == "wo" and idx == 0:
                        dve.wait_ge(xs_in, 16)
                    stt(both(xT[:, idx, :]), x, 0.5 if kind == "wo" else 1.0, both(xT[:, idx, :]), MUL, ADD, mt_dve)
                    cp(fl8[:, 0:1], fl8[:, 1:2], ev_all)
                elif kind == "fg":
                    fh = cols[:, B_FS:B_FS + 4, 0:88].rearrange("p n (b r) -> p n b r", b=2)

                    def hist(j):
                        return fh[:, :, :, j * KF + idx]
                    conv(cb[:, s, :], pairA[:, s, :], FCW, lambda j: cols[:, B_FW, KF * j + idx:KF * j + idx + 1], hist,
                         cols[:, B_FW, 2 * KF + idx:2 * KF + idx + 1], ev_y)
                elif kind == "fu":
                    tt(both(tmp), both(pairA[:, s, :]), x, MUL, mt_dve)

            def norm_apply(i, k, src, width, gain):
                q, hb, lb = (pairB, memh, meml) if i == 1 else (sqb, xh, xl)
                if k < KD:
                    stt(xT[:, k, :] if i == 4 else q[:, k % 2, 0:width], src[:, k, :], col(gain + k), lrs[:, 0:width],
                        MUL, MUL, n_tmp)
                if k and i < 4:
                    dve.wait_ge(n_hi.sem, KD * i + k)
                    tt(lb[:, k - 1, :], q[:, (k - 1) % 2, 0:width], hb[:, k - 1, :].bitcast(F32), SUB, n_lo)

            tap_at = {}

            def split(p):
                if PIECES[p][3] not in LOW_BY_DVE:
                    return
                if p and PIECES[p - 1][3] not in LOW_BY_DVE:
                    dve.wait_ge(lo.sem, p)
                u, half, kt = PIECES[p][:3]
                dve.wait_ge(hi.sem, p + 1)
                dve.tensor_tensor(wl[:, p % 2, 0:kt, :], raw[:, u % 2, 0:kt, half * P:(half + 1) * P],
                                  wh[:, p % 2, 0:kt, :].bitcast(F32), SUB).then_inc(lo.sem, 1)

            def tap(n):
                j, c = divmod(n, KB)
                w = cols[:, B_CW, 0:124].rearrange("p (j c) -> p j c", c=KB)[:, :, c]
                g = glu[:, c, :]
                if j == 0:
                    own(dve.tensor_scalar(oC[:, c, :], g[:, 30:30 + T], w[:, 30:31], col(V_CB + c), MUL, ADD))
                    hs = cols[:, B_CS:B_CS + NB, 0:120].rearrange("p b (j c) -> p b j c", c=KB)[:, :, :, c]
                    tt(htmp, hs, w[:, None, 0:30].to_broadcast([P, NB, 30]), MUL)
                    red(fl8, htmp, ADD)
                    tt(oC[:, c, SEQ:T], oC[:, c, SEQ:T], fl8, ADD)
                    return
                if c in tap_at:
                    dve.wait_ge(dve_c.sem, tap_at[c])
                dve_c.by(dve.scalar_tensor_tensor(out=oC[:, c, 0:SEQ], in0=g[:, j - 1:j - 1 + SEQ], scalar=w[:, j - 1:j],
                                                  in1=oC[:, c, 0:SEQ], op0=MUL, op1=ADD))
                tap_at[c] = dve_c.n

            def reduce_page(i):
                dve.wait_ge(prod_done.sem, i + 1)
                page_free.by(dve.tensor_reduce(sc[:, i, :], kring[:, i % 4, :].rearrange("p (h d) -> p h d", h=FH), AX, ADD))

            def side(K, s):
                kind, n = s[0], s[1]
                if not dve_works(s):
                    return
                if upto(pe_works, K):
                    dve.wait_ge(pe_s.sem, upto(pe_works, K))
                if upto(act_works, K):
                    dve.wait_ge(act_s.sem, upto(act_works, K))
                av = upto(to_dve, K)

                def fin():
                    cp(fl8[:, 0:1], fl8[:, 1:2], dve_s)

                if kind == "sm" and n == 2:
                    zps = s1[:, 0:80]
                    z4 = zt[:, 0:64].rearrange("p (t c) -> p t c", t=QT)
                    tt(z4, zps[:, 0:64].rearrange("p (t c) -> p t c", t=QT), spread(bias[:, 0:16], QT, 1), ADD)
                    tt(zt[0:NB, 64:80], zps[0:NB, 64:80], bias[0:NB, 0:16], ADD)
                    stt(az[:, 0:64], zt[:, 0:64], -1.0, zt[:, 0:64], MUL, MAX)
                    stt(az[0:NB, 64:80], zt[0:NB, 64:80], -1.0, zt[0:NB, 64:80], MUL, MAX, v2a)
                    dve.wait_ge(a2v.sem, av + 1)
                    for r, at, g_, b_, f_ in ((P, 0, gtok[:, :, :], btok[:, :, :], fltok[:, :, :]),
                                              (NB, 64, zsam[0:NB, 0:4], zsam[0:NB, 4:8], zsam[0:NB, 8:16])):
                        def view(x, c0, c1):
                            if r == P:
                                return x[:, 0:64].rearrange("p (t c) -> p t c", t=QT)[:, :, c0:c1]
                            return x[0:r, at + c0:at + c1]
                        ea = bias[0:r, 16:20]
                        stt(g_, view(zt, 0, 4), 0.0, view(zl, 0, 4), MAX, ADD)
                        stt(g_, g_, -1.0, spread(ea, QT, 1) if r == P else ea, MUL, MUL)
                        ts(b_, view(zb, 4, 8), 0.5, 0.5, MUL, ADD)
                        stt(f_, view(zt, 8, 16), 0.0, view(zl, 8, 16), MIN, SUB)
                    tt(exs[0:NB, :, :], spread(zsam[0:NB, :], NB, 1), spread(ident[0:NB, 0:NB], 16, 2), MUL, dve_s)
                elif kind == "sm" and n == 3:
                    cp(bsc[:, :, :], s3[:, 0:P].rearrange("p (b c) -> p b c", b=NB))
                    cp(dcol, s2[:, 0:16])
                    cp(edl, s2[:, 16:32])
                    tt(kdf, edl, dcol, SUB, v2a)
                    cp(cneg[0:FH, :], s0[0:FH, :])
                    own(dve.tensor_tensor_scan(cneg[0:FH, :], ones[0:FH, 0:1].to_broadcast([FH, SEQ]), cneg[0:FH, :], 0.0, MUL, ADD))
                    ts(cneg[0:FH, :], cneg[0:FH, :], -1.0, st=v2a)
                    dve.wait_ge(a2v.sem, av + 2)
                    tt(cnl[0:FH, :], cneg[0:FH, :], cnh[0:FH, :].bitcast(F32), SUB)
                    tt(bed, edc, btok[:, :, :].rearrange("p a b -> p (a b)"), MUL, dve_s)
                elif kind == "fox":
                    if n <= FOX:
                        w = ((n - 1) % QT + 1) * P
                        v2a.by(dve.tensor_reduce(nmx[:, 0:1], s0[:, 0:w], AX, MAX, negate=True))
                    if n >= 3:
                        h, q = divmod(n - 3, QT)
                        r = slice(FD * (h % 2), FD * (h % 2) + FD)
                        (dve_c if n <= FOX else dve_s).by(dve.tensor_copy(oD[r, h // 2, q * P:(q + 1) * P], s2[r, 0:P]))
                    if n <= FOX:
                        dve.wait_ge(a2v.sem, av + 1)
                        own(dve.reciprocal(nmx[:, 1:2], rsum[:, 0:1]))
                        ts(fP[:, 0:w], fP[:, 0:w], nmx[:, 1:2], st=dve_s)
                elif kind == "l2":
                    dve.wait_ge(a2v.sem, av + 1)
                    for j in range(2):
                        t = gx_tile(2 * n - 2 + j)
                        (dve_s if j else dve_c).by(dve.scalar_tensor_tensor(
                            out=t, in0=t, scalar=P ** -0.5 if n <= 2 else 1.0, in1=lrs2[:, j, :], op0=MUL, op1=MUL))
                elif kind == "gp":
                    dve.wait_ge(a2v.sem, av + 1)
                    stt(oB[:, n - 1, :], oB[:, n - 1, :], col(V_GN), lrs, MUL, MUL, dve_s)
                elif kind == "gdn":
                    c = s[2]
                    cc = slice(c * P, (c + 1) * P)
                    lv = lambda j: spread(cs(I_LVL + j), GH, 1)
                    b4 = lambda x: x.rearrange("p (a b) -> p a b", a=GH)
                    if n == 0:
                        if c == 0:
                            dve.wait_ge(ss_out, 16)
                            own(dve.memset(gS[:, :, :], 0.0))
                        for dst, op, in ((gQ, MAX), (gM, MIN)):
                            for h in range(GH):
                                (v2a if h == GH - 1 else dve_c).by(dve.tensor_scalar(
                                    dst[:, h, :], s2[:, h * P:(h + 1) * P], dcol[:, 4 * c + h:4 * c + h + 1], 0.0, SUB, op))
                        dve_s.by(dve.tensor_tensor(gvb[:, :, :], b4(s1), spread(btok[:, c, :], P, 2), MUL))
                        dve.wait_ge(a2v.sem, av + 2)
                        dve_c.by(dve.tensor_tensor(gqd[:, :, :], gqd[:, :, :], qkv[:, 8:12, cc], MUL))
                    elif n == 1:
                        for h in range(GH):
                            dve_c.by(dve.scalar_tensor_tensor(out=gN[:, h, :], in0=s0[:, h * P:(h + 1) * P], scalar=btok[:, c, h:h + 1],
                                                              in1=gQ[:, h, :], op0=MUL, op1=MUL))
                        dve.wait_ge(dve_c.sem, dve_c.n)
                        tt(gN[:, :, :], gN[:, :, :], spread(cs(I_NEGLOW), GH, 1), MUL)
                        tt(gM[:, :, :], gN[:, :, :], lv(0), MUL, dve_s)
                    elif n == 2:
                        dve_c.by(dve.tensor_tensor(gQK[:, :, :], b4(s0), gXT[:, :, :], MUL))
                        dve_c.by(dve.tensor_tensor(gX[:, :, :], gM[:, :, :], spread(ident, GH, 1), ADD))
                        dve.wait_ge(dve_c.sem, dve_c.n - 1)
                        dve_c.by(dve.tensor_tensor(gXT[:, :, :], b4(s1), spread(ident, GH, 1), ADD))
                        dve.wait_ge(dve_c.sem, dve_c.n - 1)
                        dve_s.by(dve.tensor_tensor(gM[:, :, :], gN[:, :, :], lv(1), MUL))
                        dve_c.by(dve.tensor_tensor(gQK[:, :, :], gQK[:, :, :], spread(cs(I_UP), GH, 1), MUL))
                    elif n <= 14:
                        l = n // 2 - 1
                        if l < LEVELS - 1:
                            dve_c.by(dve.tensor_tensor(gX[:, :, :], gX[:, :, :], b4(s2), ADD))
                            dve_c.by(dve.tensor_tensor(gM[:, :, :], gN[:, :, :], lv(l + 1), MUL))
                        tt(gXT[:, :, :], gXT[:, :, :], b4(s1), ADD, dve_s)
                    elif n == 17:
                        for h in range(GH):
                            (dve_s if h == GH - 1 else dve_c).by(dve.scalar_tensor_tensor(
                                out=gS[:, h, :], in0=gS[:, h, :], scalar=edl[:, 4 * c + h:4 * c + h + 1],
                                in1=s1[:, h * P:(h + 1) * P], op0=MUL, op1=ADD))
                elif kind == "cln":
                    if n == 0:
                        fin()
                    elif n == 1:
                        for c in range(KB):
                            stt(both(oC[:, c, :]), sd[:, 0:2, 0:TH], -1.0 / BD, both(oC[:, c, :]), MUL, ADD,
                                v2a if c == KB - 1 else dve_c)
                        fin()
                    elif n == 5:
                        dve.wait_ge(a2v.sem, av + 1)
                        for c in range(KB):
                            dve_c.by(dve.tensor_tensor(oC[:, c, :], oC[:, c, :], lrs, MUL))
                        for c in range(KB):
                            dve.wait_ge(dve_c.sem, dve_c.n - KB + 1 + c)
                            (dve_s if c == KB - 1 else dve_v).by(dve.tensor_scalar(
                                oC[:, c, :], oC[:, c, :], col(V_LG + c), col(V_LB + c), MUL, ADD))
                    else:
                        for c in range(KB):
                            dve.wait_ge(a2v.sem, av + 1 + c)
                            (v2a if c < 2 else dve_s if c == KB - 1 else dve_c).by(dve.scalar_tensor_tensor(
                                out=oC[:, c, :], in0=lsq if c % 2 == 0 else lrs, scalar=1.0, in1=oC[:, c, :], op0=ADD, op1=MUL))
                elif kind == "gs":
                    def bh(x):
                        return x.rearrange("p (b h) -> p h b", h=GH)
                    if n == 0:
                        fox_stored(dve)
                        cp(bh(kc), qkv[:, 0:4, SEQ:T])
                        cp(qkp[:, :, 0].rearrange("p (b h) -> p h b", h=GH), qkv[:, 8:12, SEQ:T])
                        cp(qkp[:, :, 1], kc)
                        cp(bh(vc), qkv[:, 4:8, SEQ:T])
                        tt(kqs, kc, qkp[:, :, 0], MUL, dve_s)
                    elif n == 2:
                        aa, bb = bsc[:, :, 0:4], bsc[:, :, 4:8]
                        b3 = lambda x: x.rearrange("p (b h) -> p b h", h=GH)
                        pr_ = s0[:, 0:64].rearrange("p (b h t) -> p b h t", h=GH, t=2)
                        tt(b3(dl), pr_[:, :, :, 1], aa, MUL)
                        tt(dl, vc, dl, SUB)
                        tt(b3(dl), b3(dl), bb, MUL)
                        tt(b3(oo), pr_[:, :, :, 0], aa, MUL)
                        tt(kqs, dl, s1[:, 0:32], MUL)
                        tt(oo, oo, kqs, ADD)
                        cp(oB[:, :, SEQ:T], bh(oo), dve_s)
                    else:
                        g = n - 3
                        if n == 3:
                            dve.wait_ge(ss_in, 16)
                            cp(drow_[0:32, :], s2[0:32, 0:P])
                            cp(krow[0:32, :], s2[0:32, P:2 * P])
                        else:
                            for h in range(GH):
                                u = 4 * (g - 1) + h
                                dve_c.by(dve.scalar_tensor_tensor(out=ssam[:, u, :], in0=ssam[:, u, :], scalar=bsc[:, g - 1, h:h + 1],
                                                                  in1=s0[:, h * P:(h + 1) * P], op0=MUL, op1=ADD))
                        if g < NB:
                            tt(blk[0:32, :, :], spread(drow_[0:32, :], 4, 1), spread(ident[0:32, 4 * g:4 * g + 4], P, 2), MUL, dve_s)
                        else:
                            fin()
                elif kind == "dc":
                    if n == 0:
                        dve.wait_ge(lf_in, 16)
                        red(tot, lf[:, :, :].rearrange("p t h -> p h t"), ADD)
                        tt(totm[:, :, :], spread(tot, NB, 1), spread(cst[:, N_CST * P:N_CST * P + NB], FH, 2), MUL, dve_s)
                    elif n == 1:
                        cp(offs, s0[:, 0:FH])
                        for h in range(FH):
                            own(dve.tensor_tensor_scan(cpg[:, h, :], ones, lf[:, :, h], offs[:, h:h + 1], MUL, ADD))
                        tt(cq[:, :, :], s1[:, 0:64].rearrange("p (b h) -> p b h", b=NB), bsc[:, :, 8:16], ADD, dve_s)
                    else:
                        for j in range(2):
                            o = sc[:, :, 4 * j:4 * j + 4].rearrange("p i h -> p h i")
                            tt(o, o, sd[:, 2 + j, :].rearrange("p (h i) -> p h i", h=4), SUB)
                        o = sc[:, :, :].rearrange("p (b j) h -> p b j h", b=NB)
                        tt(o, o, cq[:, :, None, :].to_broadcast([P, NB, PAGES, FH]), ADD, dve_s)
                elif kind == "ds":
                    s4 = sc[:, :, :].rearrange("p (b j) h -> p b j h", b=NB)
                    if n == 0:
                        red(mx64[:, :, :], s4.rearrange("p b j h -> p b h j"), MAX)
                        tt(qk32[:, :, :], fs[:, 0:4, :], fs[:, 4:8, :], MUL, dve_s)
                    elif n == 1:
                        red(m1[0:64, :], s0[0:64, 0:P], MAX)
                        ts(dg64[0:64, :], ident[0:64, 0:64], m1[0:64, 0:1], st=dve_c)
                        for j in range(2):
                            cp(pn[:, :, :].rearrange("p b (c t) -> p b c t", t=2)[:, :, :, j],
                               s1[:, 32 * j:32 * j + 32].rearrange("p (c b) -> p b c", c=4), dve_s if j else dve_c)
                    elif n == 2:
                        tt(mb[:, :, :], s2[:, 0:64].rearrange("p (b h) -> p b h", b=NB), pn[:, :, :], MAX)
                        tt(pn[:, :, :], pn[:, :, :], mb[:, :, :], SUB)
                        tt(s4, s4, mb[:, :, None, :].to_broadcast([P, NB, PAGES, FH]), SUB, v2a)
                        dve.wait_ge(a2v.sem, av + 1)
                        red(rs64[:, :, :], s4.rearrange("p b j h -> p b h j"), ADD, dve_s)
                    else:
                        tt(rd64[:, :, :], s3[:, 0:64].rearrange("p (b h) -> p b h", b=NB), pn[:, :, :], ADD)
                        own(dve.reciprocal(rd64[:, :, :], rd64[:, :, :]), dve_s)
                elif kind == "df":
                    for j in range(2):
                        r = slice(FD * j, FD * j + FD)
                        o = oD[r, :, SEQ:T]
                        p4 = lambda x: x[r, :, :].rearrange("p b (c t) -> p c b t", t=2)[:, :, :, j]
                        tt(o, fs[r, 8:12, :], p4(pn), MUL)
                        tt(o, o, s3[r, 0:64].rearrange("p (b c t) -> p c b t", b=NB, t=2)[:, :, :, j], ADD)
                        tt(o, o, p4(rd64), MUL)
                    fin()
                elif kind == "ml":
                    for j in range(4):
                        cp(memT[:, 2 * j:2 * j + 2, :], sd[:, j, :].rearrange("p (k m) -> p k m", k=2), dve_s if j == 3 else dve_c)
                elif kind == "x":
                    if n <= XU:
                        own(dve.tensor_reduce(xnm[:, 0:2], sd[:, 3 * ((n - 1) % 2), :].rearrange("p (a b) -> p a b", a=2), AX, MAX, negate=True), v2a)
                        if n >= 3:
                            q, h = (n - 3) // 2, 2 * ((n - 3) % 2)
                            cp(oX[:, h:h + 2, q * P:(q + 1) * P], s2[:, 0:2 * P].rearrange("p (a b) -> p a b", a=2))
                        dve.wait_ge(a2v.sem, av + 1)
                        own(dve.reciprocal(xnm[:, 2:4], xsum[:, 0:2]))
                        tt(xP[:, :, :], xP[:, :, :], spread(xnm[:, 2:4], MEM, 2), MUL, dve_s)
                    else:
                        q, h = (n - 3) // 2, 2 * ((n - 3) % 2)
                        cp(oX[:, h:h + 2, q * P:(q + 1) * P], s2[:, 0:2 * P].rearrange("p (a b) -> p a b", a=2), dve_s)
                    if 2 <= n <= NB + 1:
                        b = n - 2
                        dve.wait_ge(kprod.sem, b + 1)
                        red(xsc[:, b, :, :], kvc[:, b, :, :].rearrange("p t (h d) -> p t h d", h=XH), ADD, kred)
                elif kind == "xd":
                    x4_ = xsc[:, :, :, :]
                    if n == 0:
                        dve.wait_ge(kred.sem, NB)
                    if n == 0:
                        red(xmx[:, :, :], x4_.rearrange("p b t h -> p b h t"), MAX, dve_s)
                    elif n == 1:
                        red(xm1[0:32, :], s0[0:32, 0:P], MAX)
                        ts(xdg[0:32, :], ident[0:32, 0:32], xm1[0:32, 0:1], st=dve_s)
                    elif n == 2:
                        tt(x4_, x4_, s1[:, 0:32].rearrange("p (b h) -> p b h", b=NB)[:, :, None, :].to_broadcast([P, NB, 2, XH]), SUB, v2a)
                        dve.wait_ge(a2v.sem, av + 1)
                        red(xrs[:, :, :], x4_.rearrange("p b t h -> p b h t"), ADD, dve_s)
                    else:
                        own(dve.reciprocal(xrd[:, :, :].rearrange("p b h -> p (b h)"), s2[:, 0:32]))
                        for j in range(2):
                            tt(oX[:, :, SEQ:T].rearrange("p (c j) b -> p c j b", j=2)[:, :, j],
                               s3[:, 0:64].rearrange("p (b c j i) -> p c j i b", b=NB, j=2, i=2)[:, :, j, j],
                               xrd[:, :, :].rearrange("p b (c j) -> p c j b", j=2)[:, :, j], MUL, dve_s if j else dve_c)

            dve.wait_ge(pool_made.sem, 6)
            for j in range(14):
                dve.wait_ge(pro_pe.sem, j + 1)
                o = sd[:, j % 4, :]
                if j == 0:
                    src, dst = o[:, 0:KD * NB].rearrange("p (k b) -> p k b", k=KD), xT[:, :, SEQ:T]
                elif j <= KD:
                    src, dst = o, xT[:, j - 1, 0:SEQ]
                else:
                    b = 4 * (j - 9)
                    n = min(4, N_BLK - b)
                    src, dst = o[:, 0:n * P].rearrange("p (n m) -> p n m", n=n), cols[:, b:b + n, :]
                pro_dve.by(dve.tensor_copy(dst, src))
            dve.wait_ge(pro_dve.sem, 14)
            ts(cols[:, B_VEC, V_GW:V_GW + 48], cols[:, B_VEC, V_GW:V_GW + 48], 0.5)
            ts(cols[:, B_VEC, V_LG:V_LG + 8], cols[:, B_VEC, V_LG:V_LG + 8], 0.5)
            ts(cols[:, B_FW, 0:66], cols[:, B_FW, 0:66], 0.5)
            dve.wait_ge(wsm_hi.sem, 1)
            tt(wsl[:, :, :], wsm[:, :, :], wsh[:, :, :].bitcast(F32), SUB, wsm_lo)
            spl = [0]
            for e in TIMELINE:
                if e[0] == "nroot":
                    dve.wait_ge(n_rt.sem, e[1] + 1)
                elif e[0] == "napply":
                    i = e[1]
                    norm_apply(i, e[2], memT if i == 1 else xT, MEM if i == 1 else T, [V_MIX, V_MEM, V_CROSS, V_FFN, V_FIN][i])
                elif e[0] in ("evac", "evac2") and dve_tile[e[1]]:
                    evac(e[1], e[0] == "evac2")
                elif e[0] == "split":
                    src, n = {"brC": (oC, 4), "brB": (oB, 4), "brD": (oD, 4), "brX": (oX, 4), "merged": (xT, 8)}[e[1]]
                    for k in range(n):
                        dve.wait_ge(sp_hi.sem, spl[0] + 1)
                        tt((xl if n == 8 else ol)[:, k, :], src[:, k, :], (xh if n == 8 else oh)[:, k, :].bitcast(F32), SUB, sp_lo)
                        spl[0] += 1
                elif e[0] == "side":
                    side(e[1], e[2])
                elif e[0] == "tap":
                    tap(e[1])
                elif e[0] == "piece" and e[2] == 0 and e[1] + 1 < NP_:
                    split(e[1] + 1)
                elif e[0] == "k" and e[1] > 0:
                    reduce_page(e[1] - 1)
                elif e[0] == "kend":
                    reduce_page(N_PAGE - 1)


_INS = ["x_prompt", "x_sample", "cache_fox_k", "cache_fox_v", "cache_fox_logf", "cache_mem_k", "cache_mem_v",
        "state_sconv", "state_gdn_conv", "state_gdn", "state_conf_conv", "state_ffn_conv", "page_table", "mem_prompt",
        "norm_mix", "w_in", "w_branch", "w_out", "sconv_w", "gdn_conv_w", "gdn_a_log", "gdn_dt_bias", "gdn_norm",
        "conf_dw_w", "conf_dw_b", "conf_ln_g", "conf_ln_b", "fox_fbias", "norm_cross", "norm_mem", "w_cq", "w_ckv", "w_co",
        "norm_ffn", "w_ffn_in", "ffn_conv_w", "w_ffn_out", "norm_final"]
_OUTS = [("y_p", (1, SEQ, D)), ("y_s", (NB, 1, D)),
         ("fk_p", (1, SEQ, 1, FH, FD)), ("fv_p", (1, SEQ, 1, FH, FD)), ("fl_p", (1, SEQ, 1, FH)),
         ("mk_p", (1, 1, MEM, XH, P)), ("mv_p", (1, 1, MEM, XH, P)),
         ("sc_p", (1, 1, SCW - 1, BD)), ("gc_p", (1, 1, GCW - 1, 3 * BD)), ("S_p", (1, 1, GH, P, P)),
         ("cf_p", (1, 1, CFW - 1, BD)), ("ff_p", (1, 1, FCW - 1, FF)),
         ("fk_s", (NB, 1, 1, FH, FD)), ("fv_s", (NB, 1, 1, FH, FD)), ("fl_s", (NB, 1, 1, FH)),
         ("sc_s", (NB, 1, SCW - 1, BD)), ("gc_s", (NB, 1, GCW - 1, 3 * BD)), ("S_s", (NB, 1, GH, P, P)),
         ("cf_s", (NB, 1, CFW - 1, BD)), ("ff_s", (NB, 1, FCW - 1, FF))]


def kernel(**inputs):
    import concourse.bacc as bacc
    from concourse.bass_utils import run_bass_kernel_spmd

    nc = bacc.Bacc("TRN2", target_bir_lowering=False, num_devices=1, dynamic_dma_scratch_size=1024)
    arrays, a, out = {}, {}, {}
    for name in _INS:
        x = np.ascontiguousarray(inputs[name])
        arrays[f"in_{name}"] = x
        a[name] = nc.dram_tensor(f"in_{name}", x.shape, mybir.dt.from_np(x.dtype), kind="ExternalInput").ap()
    r = np.arange(P)[:, None]
    arrays["in_cst"] = np.concatenate([constants(), (r // PAGES == np.arange(NB)[None]).astype(np.float32)], axis=1)
    a["cst"] = nc.dram_tensor("in_cst", arrays["in_cst"].shape, F32, kind="ExternalInput").ap()
    for name, shape in _OUTS:
        out[name] = nc.dram_tensor(f"out_{name}", shape, F32, kind="ExternalOutput").ap()
    build(nc, a, out)
    res = run_bass_kernel_spmd(nc, [arrays], core_ids=[0])
    return tuple(res.results[0][f"out_{name}"] for name, _ in _OUTS)
```
